# Optimizing a Trainium2 kernel written in Bass

```python
import math
import jax
import jax.numpy as jnp
from jax import lax
import numpy as np

D_MODEL = 1024
BATCH = 1
SEQ = 256
DEPTH = 2

GRID_W = 64
CTX_LEN = 256
N_MOD = 9
SC_WIDTH = 512
SC_KSIZE = 3
ML_HEADS = 4
ML_DQK = 128
ML_DV = 256
ML_CHUNK = 64
ML_QK_W = ML_HEADS * ML_DQK
ML_V_W = ML_HEADS * ML_DV
DA_HEADS = 4
DA_HALF = 64
DA_DV = 2 * DA_HALF
DA_QK_W = DA_HEADS * 2 * DA_HALF
DA_V_W = DA_HEADS * DA_DV
Q_BLOCK = 128
ROPE_BASE = 10000.0
FFN_HIDDEN = 2816
ALPHA = (2 * DEPTH) ** 0.25
BETA = (8 * DEPTH) ** -0.25
LN_EPS = 1e-5

kernel_name = 'hybrid_conv_mlstm_diffattn_prefix_block'

def mixer_split_sizes():
    return (SC_WIDTH, SC_WIDTH, SC_WIDTH,
            ML_QK_W, ML_QK_W, ML_V_W, ML_V_W, 4 * ML_HEADS,
            DA_QK_W, DA_QK_W, DA_V_W,
            D_MODEL, D_MODEL, D_MODEL)

def split_cols(z):
    idx = np.cumsum(mixer_split_sizes())[:-1].tolist()
    return jnp.split(z, idx, axis=-1)

def layer_norm(x, g, b):
    xf = x.astype(jnp.float32)
    mu = jnp.mean(xf, axis=-1, keepdims=True)
    var = jnp.mean(jnp.square(xf - mu), axis=-1, keepdims=True)
    return ((xf - mu) * lax.rsqrt(var + LN_EPS) * g + b).astype(x.dtype)

def rms_norm(x, g):
    xf = x.astype(jnp.float32)
    return (xf * lax.rsqrt(jnp.mean(jnp.square(xf), axis=-1, keepdims=True) + LN_EPS) * g).astype(x.dtype)

def post_norm(h, delta, g, b):
    return layer_norm(ALPHA * h + delta, g, b)

def modulate(h, shift, scale):
    return h * (1.0 + scale) + shift

def swiglu(u, w_up, w_down):
    a, v = jnp.split(u @ w_up, 2, axis=-1)
    return (jax.nn.silu(a) * v) @ w_down

def centred_depthwise_conv(z, w):
    k, ch = w.shape
    return lax.conv_general_dilated(z, w[:, None, :].astype(z.dtype), window_strides=(1,),
                                    padding=[(k // 2, k // 2)],
                                    dimension_numbers=('NWC', 'WIO', 'NWC'),
                                    feature_group_count=ch)

def axial_rope_tables(row_ids, col_ids, rot_dim):
    n_freq = rot_dim // 4
    inv = ROPE_BASE ** (-jnp.arange(n_freq, dtype=jnp.float32) / n_freq)
    ang = jnp.concatenate([row_ids[:, None] * inv, col_ids[:, None] * inv], axis=-1)
    return jnp.cos(ang), jnp.sin(ang)

def apply_rope(x, cos, sin):
    x1, x2 = jnp.split(x.astype(jnp.float32), 2, axis=-1)
    return jnp.concatenate([x1 * cos - x2 * sin, x1 * sin + x2 * cos], axis=-1).astype(x.dtype)

def to_heads(a, n_heads):
    b, t, _ = a.shape
    return a.reshape(b, t, n_heads, -1).transpose(0, 2, 1, 3)

def from_heads(a):
    b, h, t, d = a.shape
    return a.transpose(0, 2, 1, 3).reshape(b, t, h * d)

def flip_t(a):
    return jnp.flip(a, axis=2)

def mlstm_chunk_scan(q, k, v, log_i, log_f, state):
    b, h, t, _ = q.shape
    dv = v.shape[-1]
    n_chunks = t // ML_CHUNK

    def chunks(a):
        return jnp.moveaxis(a.reshape(b, h, n_chunks, ML_CHUNK, *a.shape[3:]), 2, 0)

    lower = jnp.tril(jnp.ones((ML_CHUNK, ML_CHUNK), dtype=bool))

    def step(carry, xs):
        C, n, m = carry
        qc, kc, vc, ic, fc = xs
        bcum = jnp.cumsum(fc, axis=-1)
        d_log = jnp.where(lower, bcum[..., :, None] - bcum[..., None, :] + ic[..., None, :], -jnp.inf)
        m_inter = bcum + m[..., None]
        m_t = jnp.maximum(m_inter, jnp.max(d_log, axis=-1))
        w_inter = jnp.exp(m_inter - m_t)
        s = jnp.einsum('bhtd,bhsd->bhts', qc, kc).astype(jnp.float32) * jnp.exp(d_log - m_t[..., None])
        num = w_inter[..., None] * jnp.einsum('bhtd,bhde->bhte', qc, C) + jnp.einsum('bhts,bhse->bhte', s, vc)
        den = w_inter * jnp.einsum('bhtd,bhd->bht', qc, n) + jnp.sum(s, axis=-1)
        h_out = num / jnp.maximum(jnp.abs(den), jnp.exp(-m_t))[..., None]
        b_end = bcum[..., -1]
        g_log = b_end[..., None] - bcum + ic
        m_new = jnp.maximum(b_end + m, jnp.max(g_log, axis=-1))
        a_prev = jnp.exp(b_end + m - m_new)
        kw = kc * jnp.exp(g_log - m_new[..., None])[..., None]
        C_new = a_prev[..., None, None] * C + jnp.einsum('bhsd,bhse->bhde', kw, vc)
        n_new = a_prev[..., None] * n + jnp.sum(kw, axis=2)
        return (C_new, n_new, m_new), h_out

    state, hs = lax.scan(step, state, (chunks(q), chunks(k), chunks(v), chunks(log_i), chunks(log_f)))
    return jnp.moveaxis(hs, 0, 2).reshape(b, h, t, dv), state

def mlstm_inputs(mq, mk, mv, mg):
    b, t, _ = mg.shape
    g = mg.astype(jnp.float32).reshape(b, t, 4, ML_HEADS).transpose(2, 0, 3, 1)
    gates = (g[0], g[1], jax.nn.log_sigmoid(g[2]), jax.nn.log_sigmoid(g[3]))
    return (to_heads(mq, ML_HEADS), to_heads(mk, ML_HEADS) * (ML_DQK ** -0.5), to_heads(mv, ML_HEADS), gates)

def bidir_mlstm(q, k, v, gates, state_fwd, state_bwd):
    i_f, i_b, lf_f, lf_b = gates
    h_f, st_f = mlstm_chunk_scan(q, k, v, i_f, lf_f, state_fwd)
    h_b, st_b = mlstm_chunk_scan(flip_t(q), flip_t(k), flip_t(v), flip_t(i_b), flip_t(lf_b), state_bwd)
    return h_f + flip_t(h_b), st_f, st_b

def da_heads(a):
    b, t, _ = a.shape
    return a.reshape(b, t, DA_HEADS, 2, DA_HALF).transpose(0, 2, 3, 1, 4)

def diff_attend(q, k, v, lam):
    s = jnp.einsum('bhjqd,bhjkd->bhjqk', q, k).astype(jnp.float32) * (DA_HALF ** -0.5)
    p = jax.nn.softmax(s, axis=-1)
    w = p[:, :, 0] - lam * p[:, :, 1]
    return jnp.einsum('bhqk,bhkd->bhqd', w.astype(v.dtype), v)

def diff_head_out(o, g, lam_init):
    return from_heads(rms_norm(o, g) * (1.0 - lam_init))

def token_mixer(u, uc, cos, sin, w_in, b_in, conv_w, w_sc, w_ml, w_da, w_o, lam, lam_init, da_g, need_ctx):
    (sb, scg, sx, mq, mk, mv, mo, mg, dq, dk, dv, gs, gm, gd) = split_cols(u @ w_in + b_in)
    (sbc, scc, sxc, mqc, mkc, mvc, moc, mgc, dqc, dkc, dvc, gsc, gmc, gdc) = split_cols(uc @ w_in + b_in)

    y_sc = sb * centred_depthwise_conv(scg * sx, conv_w)

    ql, kl, vl, gl = mlstm_inputs(mq, mk, mv, mg)
    qcm, kcm, vcm, gcm = mlstm_inputs(mqc, mkc, mvc, mgc)
    bsz = ql.shape[0]
    zero = (jnp.zeros((bsz, ML_HEADS, ML_DQK, ML_DV), jnp.float32),
            jnp.zeros((bsz, ML_HEADS, ML_DQK), jnp.float32),
            jnp.zeros((bsz, ML_HEADS), jnp.float32))
    hc_ml, st_f, st_b = bidir_mlstm(qcm, kcm, vcm, gcm, zero, zero)
    hl_ml, _, _ = bidir_mlstm(ql, kl, vl, gl, st_f, st_b)
    y_ml = jax.nn.sigmoid(mo) * from_heads(hl_ml).astype(mo.dtype)

    q_l = apply_rope(da_heads(dq), cos, sin)
    k_l = apply_rope(da_heads(dk), cos, sin)
    v_l = to_heads(dv, DA_HEADS)
    k_c = da_heads(dkc)
    v_c = to_heads(dvc, DA_HEADS)
    k_all = jnp.concatenate([k_l, k_c], axis=3)
    v_all = jnp.concatenate([v_l, v_c], axis=2)
    _, nh, _, t, dh = q_l.shape
    nb = t // Q_BLOCK
    q_blocks = q_l.reshape(bsz, nh, 2, nb, Q_BLOCK, dh).transpose(3, 0, 1, 2, 4, 5)
    o_blocks = lax.map(lambda qb: diff_attend(qb, k_all, v_all, lam), q_blocks)
    o_l = o_blocks.transpose(1, 2, 0, 3, 4).reshape(bsz, nh, t, DA_DV)
    y_da = diff_head_out(o_l, da_g, lam_init)

    y = (jax.nn.sigmoid(gs) * (y_sc @ w_sc) + jax.nn.sigmoid(gm) * (y_ml @ w_ml)
         + jax.nn.sigmoid(gd) * (y_da @ w_da)) @ w_o
    if not need_ctx:
        return y, None

    yc_sc = sbc * centred_depthwise_conv(scc * sxc, conv_w)
    yc_ml = jax.nn.sigmoid(moc) * from_heads(hc_ml).astype(moc.dtype)
    yc_da = diff_head_out(diff_attend(da_heads(dqc), k_c, v_c, lam), da_g, lam_init)
    yc = (jax.nn.sigmoid(gsc) * (yc_sc @ w_sc) + jax.nn.sigmoid(gmc) * (yc_ml @ w_ml)
          + jax.nn.sigmoid(gdc) * (yc_da @ w_da)) @ w_o
    return y, yc

def setup_inputs(seed: int = 0) -> dict:
    key = jax.random.key(seed)
    ks = iter(jax.random.split(key, 32))

    def nrm(shape, s):
        return jax.random.normal(next(ks), shape, jnp.float32) * s

    n_in = sum(mixer_split_sizes())
    f_off = 3 * SC_WIDTH + 2 * ML_QK_W + 2 * ML_V_W + 2 * ML_HEADS
    forget_bias = jnp.tile(jnp.linspace(3.0, 6.0, ML_HEADS, dtype=jnp.float32), 2)
    return {
        'x': nrm((BATCH, SEQ, D_MODEL), 1.0),
        'c': nrm((BATCH, D_MODEL), 1.0),
        'ctx': nrm((BATCH, CTX_LEN, D_MODEL), 1.0),
        'c_ctx': nrm((D_MODEL,), 1.0),
        'w_ada': nrm((DEPTH, D_MODEL, N_MOD * D_MODEL), 0.5 * D_MODEL ** -0.5),
        'b_ada': nrm((DEPTH, N_MOD * D_MODEL), 0.02),
        'ln_g': 1.0 + nrm((DEPTH, 3, D_MODEL), 0.02),
        'ln_b': nrm((DEPTH, 3, D_MODEL), 0.02),
        'ffn1_up': nrm((DEPTH, D_MODEL, 2 * FFN_HIDDEN), D_MODEL ** -0.5),
        'ffn1_down': nrm((DEPTH, FFN_HIDDEN, D_MODEL), BETA * FFN_HIDDEN ** -0.5),
        'ffn2_up': nrm((DEPTH, D_MODEL, 2 * FFN_HIDDEN), D_MODEL ** -0.5),
        'ffn2_down': nrm((DEPTH, FFN_HIDDEN, D_MODEL), BETA * FFN_HIDDEN ** -0.5),
        'w_in': nrm((DEPTH, D_MODEL, n_in), D_MODEL ** -0.5),
        'b_in': nrm((DEPTH, n_in), 0.02).at[:, f_off:f_off + 2 * ML_HEADS].add(forget_bias),
        'conv_w': nrm((DEPTH, SC_KSIZE, SC_WIDTH), SC_KSIZE ** -0.5),
        'w_sc': nrm((DEPTH, SC_WIDTH, D_MODEL), BETA * SC_WIDTH ** -0.5),
        'w_ml': nrm((DEPTH, ML_V_W, D_MODEL), BETA * ML_V_W ** -0.5),
        'w_da': nrm((DEPTH, DA_V_W, D_MODEL), BETA * DA_V_W ** -0.5),
        'w_o': nrm((DEPTH, D_MODEL, D_MODEL), BETA * D_MODEL ** -0.5),
        'lam_q1': nrm((DEPTH, DA_HALF), 0.1),
        'lam_k1': nrm((DEPTH, DA_HALF), 0.1),
        'lam_q2': nrm((DEPTH, DA_HALF), 0.1),
        'lam_k2': nrm((DEPTH, DA_HALF), 0.1),
        'da_norm_g': 1.0 + nrm((DEPTH, DA_DV), 0.02),
    }

def reference(x, c, ctx, c_ctx, w_ada, b_ada, ln_g, ln_b, ffn1_up, ffn1_down, ffn2_up, ffn2_down,
              w_in, b_in, conv_w, w_sc, w_ml, w_da, w_o, lam_q1, lam_k1, lam_q2, lam_k2, da_norm_g):
    n_tok = x.shape[1]
    ROWS = n_tok // GRID_W
    row_ids = jnp.repeat(jnp.arange(ROWS, dtype=jnp.float32), GRID_W)
    col_ids = jnp.tile(jnp.arange(GRID_W, dtype=jnp.float32), ROWS)
    cos, sin = axial_rope_tables(row_ids, col_ids, DA_HALF)

    h, hc = x, ctx
    for l in range(DEPTH):
        last = l == DEPTH - 1
        mods = jnp.split((jax.nn.silu(c) @ w_ada[l] + b_ada[l])[:, None, :], N_MOD, axis=-1)
        mods_c = jnp.split(jax.nn.silu(c_ctx) @ w_ada[l] + b_ada[l], N_MOD, axis=-1)

        h = post_norm(h, 0.5 * mods[2] * swiglu(modulate(h, mods[0], mods[1]), ffn1_up[l], ffn1_down[l]),
                      ln_g[l, 0], ln_b[l, 0])
        hc = post_norm(hc, 0.5 * mods_c[2] * swiglu(modulate(hc, mods_c[0], mods_c[1]), ffn1_up[l], ffn1_down[l]),
                       ln_g[l, 0], ln_b[l, 0])

        lam_init = 0.8 - 0.6 * math.exp(-0.3 * l)
        lam = (jnp.exp(jnp.sum(lam_q1[l].astype(jnp.float32) * lam_k1[l].astype(jnp.float32)))
               - jnp.exp(jnp.sum(lam_q2[l].astype(jnp.float32) * lam_k2[l].astype(jnp.float32))) + lam_init)
        y, yc = token_mixer(modulate(h, mods[3], mods[4]), modulate(hc, mods_c[3], mods_c[4]), cos, sin,
                            w_in[l], b_in[l], conv_w[l], w_sc[l], w_ml[l], w_da[l], w_o[l],
                            lam, lam_init, da_norm_g[l], not last)
        h = post_norm(h, mods[5] * y, ln_g[l, 1], ln_b[l, 1])

        h = post_norm(h, 0.5 * mods[8] * swiglu(modulate(h, mods[6], mods[7]), ffn2_up[l], ffn2_down[l]),
                      ln_g[l, 2], ln_b[l, 2])
        if not last:
            hc = post_norm(hc, mods_c[5] * yc, ln_g[l, 1], ln_b[l, 1])
            hc = post_norm(hc, 0.5 * mods_c[8] * swiglu(modulate(hc, mods_c[6], mods_c[7]), ffn2_up[l], ffn2_down[l]),
                           ln_g[l, 2], ln_b[l, 2])
    return h


_drawn_inputs = setup_inputs


def setup_inputs(seed=0):
    import zlib

    import numpy as np

    out = dict(_drawn_inputs(seed))
    spreads = {}
    factors = {'lam_q1': 3.371, 'lam_k1': 8.0, 'lam_q2': 8.0, 'lam_k2': 8.0, 'da_norm_g': 45.346}
    for name, (base, spread) in spreads.items():
        noise = np.random.default_rng([zlib.crc32(name.encode()), seed]).standard_normal(out[name].shape)
        drawn = base * np.exp(spread * noise) if base else spread * noise
        out[name] = jnp.asarray(drawn.astype(out[name].dtype))
    for name, factor in factors.items():
        out[name] = (out[name] * factor).astype(out[name].dtype)
    return out
```

```python
import math

import numpy as np

import concourse.bass as bass
from concourse import mybir

F32 = mybir.dt.float32
F32R = mybir.dt.float32r
ACT = mybir.ActivationFunctionType
ALU = mybir.AluOpType
AXX = mybir.AxisListType.X

P = 128
D = 1024
KD = D // P
SEG = 256
TOK = 2 * SEG
TT = TOK // P
DEPTH = 2
FH = 2816
KF = FH // P
N_IN = 9232
MG_COL = 4608
GRID_W = 64
HEADS = 4
DQK = 128
DA_HALF = 64
ALPHA = (2 * DEPTH) ** 0.25
EPS = 1e-5
N_MOD = 9
MODT = N_MOD * KD
DOWN_K = [range(0, 6), range(6, 12), range(12, 17), range(17, 22)]
RAW = 4
SPLIT = 2
CH_UP, CH_DOWN, CH_PROJ, CH_GATE, CH_WO = 2 * KF, 4 * KD, 48, 6 * KD, KD
CH_MIX = CH_PROJ + CH_GATE + CH_WO
CH_LAYER = 2 * (CH_UP + CH_DOWN) + CH_MIX
ADA_UP, ADA_DOWN, ADA_LN = 4, 2, 20

SEC = {"sb": 0, "cg": 4, "sx": 8, "mq": 12, "mk": 16, "mv": 20, "mo": 28,
       "dq": 36, "dk": 40, "dv": 44, "gs": 48, "gm": 56, "gd": 64}


def in_col(tile):
    return tile * P + (16 if tile >= 36 else 0)


def bias_at(layer, tile):
    if layer == 0:
        return 2, tile
    return (2, 72 + tile) if tile < 36 else (3, tile - 36)


def proj_order():
    order = [("gates", 0)]
    order += [("mq", i) for i in range(4)] + [("mk", i) for i in range(4)]
    for i in range(8):
        order.append(("mv", i))
        if i:
            order.append(("turn_v", i - 1))
    for i in range(4):
        order += [("cg", i)]
        if i == 0:
            order.append(("turn_v", 7))
        order += [("sx", i), ("sb", i)]
    order += [("mlstm", h) for h in range(HEADS)]
    order += [("mo", i) for i in range(8)]
    for i in range(4):
        order.append(("dv", i))
        if i:
            order.append(("turn_v", 8 + i - 1))
    order.append(("dq", 0))
    order.append(("turn_v", 11))
    order += [("dq", 1), ("rope", 0), ("dq", 2), ("rope", 1), ("dq", 3), ("rope", 2)]
    order += [("dk", 0), ("rope", 3), ("dk", 1), ("rope", 4), ("dk", 2), ("rope", 5), ("dk", 3), ("rope", 6), ("rope", 7)]
    order += [("attend", 0)]
    return order


ORDER = proj_order()
EVAC_ENGINE = {"mq": "act", "mk": "dve", "mv": "act", "cg": "act", "sx": "dve", "sb": "dve",
               "mo": "act", "dv": "act", "dq": "act", "dk": "act"}
X_ONLY = {"cg", "sx", "sb", "mq", "mo", "dq"}


def proj_plan():
    plan, n, a, d, y = {}, 0, 0, 0, 0
    for step in ORDER:
        if step[0] in EVAC_ENGINE:
            plan[step] = (n, a, d, y)
            n += 1
            a += EVAC_ENGINE[step[0]] == "act"
            d += EVAC_ENGINE[step[0]] == "dve"
            y += step[0] in ("sb", "mo")
    assert n == CH_PROJ
    return plan, a, d


PLAN, PROJ_A, PROJ_D = proj_plan()
BY_CHUNK = {v[0]: k for k, v in PLAN.items()}


def bases():
    out, r, a, d = {}, 0, 4, 4
    for layer in range(DEPTH):
        for name in ("up0", "down0", "proj", "gate", "wo", "up1", "down1"):
            out[layer, name] = (r, a, d)
            kind = name.rstrip("01")
            r += {"up": CH_UP, "down": CH_DOWN, "proj": CH_PROJ, "gate": CH_GATE, "wo": CH_WO}[kind]
            a += {"up": KF, "down": 0, "proj": PROJ_A, "gate": 3 * KD, "wo": 0}[kind]
            d += {"up": KF, "down": KD, "proj": PROJ_D, "gate": 3 * KD, "wo": KD}[kind]
    return out


BASES = bases()
CHUNKS = DEPTH * CH_LAYER


def head_ranges(s, t0):
    forward = (max(s * P, t0), TOK)
    backward = (t0, TOK) if s in (0, 1) else (SEG, (s + 1) * P)
    if s == 0 and t0 == 0:
        backward = (0, TOK)
    diag = s if s * P >= t0 else None
    return (forward, backward), diag


KEYS = {("f", 0): [0], ("f", 1): [0, 1], ("f", 2): [0, 1, 2], ("f", 3): [0, 1, 2, 3],
        ("b", 0): [0, 1], ("b", 1): [1], ("b", 2): [0, 1, 2, 3], ("b", 3): [0, 1, 3]}


def build(nc, x, c, ctx, c_ctx, w_ada, b_ada, ln_g, ln_b, ffn1_up, ffn1_down, ffn2_up, ffn2_down,
          w_in, b_in, conv_w, w_sc, w_ml, w_da, w_o, lam_q1, lam_k1, lam_q2, lam_k2, da_norm_g,
          consts, out):
    spot = [16512]

    def at(name, shape, dtype, offset=None):
        size = int(np.prod(shape[1:])) * 4
        if offset is None:
            offset = spot[0]
            spot[0] += (size + 31) // 32 * 32
        return nc.alloc_sbuf_tensor_at(name, shape, dtype, offset=offset)

    h = at("h", [P, KD, TOK], F32)
    u_hi = at("u_hi", [P, KD, TOK], F32R)
    u_lo = at("u_lo", [P, KD, TOK], F32R)
    raw = at("raw", [P, RAW, D], F32)
    w_hi = at("w_hi", [P, SPLIT, D], F32R)
    w_lo = at("w_lo", [P, SPLIT, D], F32R)
    ada_w = at("ada_w", [P, 2, D], F32)
    con = at("con", [P, 1152], F32)
    ident, mask_f, mask_b = con[:, 0:128], con[:, 128:256], con[:, 256:384]
    rot_w, mean_w = con[:, 384:512], con[:, 512:640]
    rope_cos, rope_sin = con[:, 640:896], con[:, 896:1152]
    cols = at("cols", [P, 4, P], F32)
    mods = at("mods", [P, DEPTH * MODT, 2], F32)
    cs = at("cs", [P, KD, 2], F32)
    one_zero = at("one_zero", [P, 2, KD], F32)
    mod_a = at("mod_a", [P, KD, 2], F32)
    mod_b = at("mod_b", [P, KD, 2], F32)
    res_g = at("res_g", [P, KD], F32)
    res_b = at("res_b", [P, KD], F32)
    gate = at("gate", [P, KD, 2], F32)
    neg_lam = at("neg_lam", [P, DEPTH], F32)
    lam_e = at("lam_e", [P, DEPTH, 2], F32)
    gate_bias = at("gate_bias", [P, DEPTH], F32)
    small = at("small", [P, 16], F32)
    region = spot[0]
    spot[0] += 96 * 1024
    scr = [at(f"scr{i}", [P, TOK], F32) for i in range(6)]
    assert spot[0] <= 229368, spot[0]
    KB = 1024
    g_hi = at("g_hi", [P, KF, TOK], F32R, region)
    g_lo = at("g_lo", [P, KF, TOK], F32R, region + KF * TOK * 4)
    x_in = at("x_in", [P, TT, D], F32, region)
    rows = at("rows", [P, 4, P], F32, region + 16 * KB)
    lam_in = at("lam_in", [P, DEPTH, 4, DA_HALF], F32, region + 20 * KB)
    lam_p = at("lam_p", [P, DEPTH, 2, DA_HALF], F32, region + 22 * KB)
    y_out = at("y_out", [P, 2, D], F32, region)
    ysc_hi = at("ysc_hi", [P, 4, TOK], F32R, region)
    ysc_lo = at("ysc_lo", [P, 4, TOK], F32R, region + 8 * KB)
    yml_hi = at("yml_hi", [P, 8, TOK], F32R, region + 16 * KB)
    yml_lo = at("yml_lo", [P, 8, TOK], F32R, region + 32 * KB)
    vaug = at("vaug", [P, TT, HEADS, 257], F32, region + 16 * KB)
    neg_g = at("neg_g", [64, TOK], F32, region + 33 * KB)
    am = at("am", [P, TT, P], F32, region + 35 * KB)
    em = at("em", [P, TT, 64], F32, region + 37 * KB)
    xt = at("xt", [P, 2, TOK], F32, region + 38 * KB)
    hs = at("hs", [P, 2, SEG], F32, region + 42 * KB)
    hf = at("hf", [P, SEG], F32, region + 44 * KB)
    pw = at("pw", [P, 2, TT, TOK], F32, region + 48 * KB)
    cgt = at("cgt", [P, TOK], F32, region + 48 * KB)
    zpad = at("zpad", [P, 2, SEG + 2], F32, region + 50 * KB)
    cv = at("cv", [P, TOK], F32, region + 53 * KB)
    dav = at("dav", [P, TT, HEADS, P], F32, region + 48 * KB)
    yda_hi = at("yda_hi", [P, 4, TOK], F32R, region + 48 * KB)
    yda_lo = at("yda_lo", [P, 4, TOK], F32R, region + 56 * KB)
    gt = [at(f"gt{i}", [P, TOK], F32, region + (64 + 2 * i) * KB) for i in range(8)]
    ht = at("ht", [P, 8, TOK], F32, region + 64 * KB)
    oda = at("oda", [P, TT, HEADS, P], F32, region + 64 * KB)
    ssq = at("ssq", [P, TT, HEADS], F32, region + 72 * KB)
    z_hi = at("z_hi", [P, KD, TOK], F32R, region + 64 * KB)
    z_lo = at("z_lo", [P, KD, TOK], F32R, region + 80 * KB)
    qt = at("qt", [P, HEADS, TOK], F32, region + 80 * KB)
    kt = at("kt", [P, HEADS, TOK], F32, region + 88 * KB)
    dqk = at("dqk", [P, 8, TOK], F32, region + 80 * KB)
    wg_in = at("wg_in", [P, KD, 16], F32, region + 54 * KB + 512)
    wg = at("wg", [P, KD, P], F32, region + 56 * KB)

    ps = [nc.alloc_psum_tensor(f"ps{i}", [P, 512], F32) for i in range(8)]

    def sem(name):
        return nc.alloc_semaphore(name)

    const_in, x_landed, rows_in, lam_landed, gate_in, wg_landed = (
        sem(n) for n in ("const_in", "x_landed", "rows_in", "lam_landed", "gate_in", "wg_landed"))
    raw_in = [sem(f"raw_in{i}") for i in range(RAW)]
    ada_in = [sem(f"ada_in{i}") for i in range(2)]
    zeroed = sem("zeroed")
    rows_turned, cols_ready, cs_ready, lam_dot, lam_exp = (
        sem(n) for n in ("rows_turned", "cols_ready", "cs_ready", "lam_dot", "lam_exp"))
    x_turned, hi_done, lo_done, chunk_used, evac_act, evac_dve = (
        sem(n) for n in ("x_turned", "hi_done", "lo_done", "chunk_used", "evac_act", "evac_dve"))
    ada_done, ada_ev, g_hi_done, g_ready = (sem(n) for n in ("ada_done", "ada_ev", "g_hi_done", "g_ready"))
    gate_cols = sem("gate_cols")
    ln_mean, ln_cent, ln_sq, ln_sq_used, ln_std, ln_xn = (
        sem(n) for n in ("ln_mean", "ln_cent", "ln_sq", "ln_sq_used", "ln_std", "ln_xn"))
    cols_mod, u_hi_done, u_ready, h_ready = (sem(n) for n in ("cols_mod", "u_hi_done", "u_ready", "h_ready"))
    yf_ready, y_hi_done, y_ready = (sem(n) for n in ("yf_ready", "y_hi_done", "y_ready"))
    v_turned, v_placed, rot_done, rope_done = (sem(n) for n in ("v_turned", "v_placed", "rot_done", "rope_done"))
    wg_ready, mg_done, gate_act, gate_dve, gate_turn = (
        sem(n) for n in ("wg_ready", "mg_done", "gate_act", "gate_dve", "gate_turn"))
    ng_ready, s_ready, x_ready, e_ready, pw_ready = (
        sem(n) for n in ("ng_ready", "s_ready", "x_ready", "e_ready", "pw_ready"))
    num_ready, hsum_ready, h_turned, ht_ready = (sem(n) for n in ("num_ready", "hsum_ready", "h_turned", "ht_ready"))
    sc_ready, smax_ready, p_ready, wgt_ready, wgt_turned, wt_ready, o_ready, o_copied, o_sq = (
        sem(n) for n in ("sc_ready", "smax_ready", "p_ready", "wgt_ready", "wgt_turned", "wt_ready",
                         "o_ready", "o_copied", "o_sq"))
    o_std, o_scaled, o_turned, yda_f, yda_h, yda_ready = (
        sem(n) for n in ("o_std", "o_scaled", "o_turned", "yda_f", "yda_h", "yda_ready"))
    z_part, z_sum, z_hi_done, z_ready = (sem(n) for n in ("z_part", "z_sum", "z_hi_done", "z_ready"))
    gate_abs = sem("gate_abs")
    out_turned, out_ready, out_done = (sem(n) for n in ("out_turned", "out_ready", "out_done"))
    dve_chain = sem("dve_chain")
    act_chain = sem("act_chain")

    def wait(eng, s, value):
        if isinstance(value, int) and value <= 0:
            return
        eng.wait_ge(s, value)

    def halves(t0):
        return [(0, slice(0, SEG)), (1, slice(SEG, TOK))] if t0 == 0 else [(1, slice(SEG, TOK))]

    def t0_of(layer, x_only=True):
        return SEG if layer == DEPTH - 1 and x_only else 0

    ups = (ffn1_up, ffn2_up)
    downs = (ffn1_down, ffn2_down)

    def norm_cols(n):
        if n == 0:
            return one_zero[:, 0, :], one_zero[:, 1, :]
        layer, i = (n - 1) // 3, (n - 1) % 3
        o = 72 + (layer * 3 + i) * KD
        return cols[:, 0, o:o + KD], cols[:, 1, o:o + KD]

    def next_mods(n):
        return (n // 3) * MODT + (n % 3) * 3 * KD

    def gate_mods(layer, i):
        return layer * MODT + (3 * i + 2) * KD

    def norm_t0(n):
        return SEG if n >= 5 else 0

    def norm_d(n):
        layer, i = (n - 1) // 3, (n - 1) % 3
        return BASES[layer, ("down0", "wo", "down1")[i]][2] + KD

    def run(eng, count, body, peel_first=False, peel_last=False):
        n = count - 1 if peel_last else count
        if peel_first:
            body(0)
        with eng.Fori(int(peel_first), n) as i:
            body(i)
        if peel_last:
            body(n)

    block = nc.Block()
    block.__enter__()

    @block.sync
    def _(sp):
        sp.dma_start(con[:, :], consts).then_inc(const_in, 16)

        def turn(a, rows_of, tile, r0, n):
            sp.dma_start(rows[r0:r0 + n, tile, :], a).then_inc(rows_in, 16)

        def as_rows(a):
            return a.rearrange("(r p) -> r p", p=P)
        for layer in range(DEPTH):
            turn(as_rows(b_ada[layer]), 0, layer, 0, 72)
            turn(as_rows(b_in[layer, 0:MG_COL]), 0, 2, 72 * layer, 36)
            turn(as_rows(b_in[layer, MG_COL + 16:N_IN]), 0, *((2, 36) if layer == 0 else (3, 0)), 36)
        turn(ln_g.rearrange("l i (r p) -> (l i r) p", p=P), 0, 0, 72, 48)
        turn(ln_b.rearrange("l i (r p) -> (l i r) p", p=P), 0, 1, 72, 48)
        turn(conv_w.rearrange("l t (r p) -> (l t r) p", p=P), 0, 3, 36, 24)
        turn(as_rows(c_ctx), 0, 3, 60, 8)
        turn(c.rearrange("a (r p) -> (a r) p", p=P), 0, 3, 68, 8)
        turn(da_norm_g, 0, 3, 76, 2)
        for n, a in enumerate((lam_q1, lam_k1, lam_q2, lam_k2)):
            sp.dma_start(lam_in[:, :, n, :], a.rearrange("l d -> (l d)").partition_broadcast(P)
                         .rearrange("p (l d) -> p l d", l=DEPTH)).then_inc(lam_landed, 16)
        for s, a in enumerate((ctx, x)):
            sp.dma_start(x_in[:, 2 * s:2 * s + 2, :], a[0].rearrange("(t p) d -> p t d", p=P)).then_inc(x_landed, 16)
        sp.wait_ge(zeroed, 1)
        for layer in range(DEPTH):
            for q in range(4):
                sp.dma_start(gate_bias[32 * q:32 * q + 4, layer:layer + 1],
                             b_in[layer, MG_COL + 4 * q:MG_COL + 4 * q + 4].rearrange("(p a) -> p a", a=1)
                             ).then_inc(gate_in, 16)

        def load(r, src, slot, kt_n, width, free=True):
            if free:
                wait(sp, lo_done, r - RAW + 1)
            dst = raw[:, slot, 0:kt_n * width].rearrange("p (k n) -> p k n", k=kt_n)
            sp.dma_start(dst, src).then_inc(raw_in[slot], 16)

        def up(layer, f):
            base = BASES[layer, f"up{f}"][0]
            src = ups[f][layer].rearrange("(k p) n -> p k n", p=P)

            def body(i):
                for q in range(4):
                    column = (2 * i + q // 2) * P + (q % 2) * FH
                    column = column if isinstance(column, int) else sp.snap(column)
                    load(base + 4 * i + q, src[:, :, bass.ds(column, P)], (base + q) % RAW, KD, P)
            run(sp, CH_UP // 4, body, peel_first=(layer, f) == (0, 0))

        def down(layer, f):
            base = BASES[layer, f"down{f}"][0]
            src = downs[f][layer].rearrange("(k p) n -> p k n", p=P)

            def body(i):
                for e in range(2):
                    column = sp.snap((2 * i + e) * P)
                    for q, ks in enumerate(DOWN_K):
                        load(base + 8 * i + 4 * e + q, src[:, ks[0]:ks[-1] + 1, bass.ds(column, P)],
                             (base + 4 * e + q) % RAW, len(ks), P)
            run(sp, KD // 2, body)

        def mixer(layer):
            base = BASES[layer, "proj"][0]
            src = w_in[layer].rearrange("(k p) n -> p k n", p=P)
            sp.wait_ge(chunk_used, base)
            sp.dma_start(wg_in[:, :, :], src[:, :, MG_COL:MG_COL + 16]).then_inc(wg_landed, 16)
            for n in range(CH_PROJ):
                kind, i = BY_CHUNK[n]
                col = in_col(SEC[kind] + i)
                load(base + n, src[:, :, col:col + P], (base + n) % RAW, KD, P)
            base = BASES[layer, "gate"][0]

            def body(i):
                for e in range(2):
                    for q, (g, w, kn) in enumerate((("gs", w_sc, 4), ("gm", w_ml, 8), ("gd", w_da, 4))):
                        at_ = 12 * i + 6 * e + 2 * q
                        column = sp.snap((2 * i + e) * P + in_col(SEC[g]))
                        sp.wait_ge(lo_done, base + at_ + 2 - RAW)
                        load(base + at_, src[:, :, bass.ds(column, P)],
                             (base + 6 * e + 2 * q) % RAW, KD, P, free=False)
                        column = sp.snap((2 * i + e) * P)
                        load(base + at_ + 1, w[layer].rearrange("(k p) n -> p k n", p=P)[
                            :, :, bass.ds(column, P)], (base + 6 * e + 2 * q + 1) % RAW, kn, P, free=False)
            run(sp, KD // 2, body)
            base = BASES[layer, "wo"][0]
            srco = w_o[layer].rearrange("(k p) n -> p k n", p=P)

            def body_o(i):
                for e in range(4):
                    column = sp.snap((4 * i + e) * P)
                    load(base + 4 * i + e, srco[:, :, bass.ds(column, P)], (base + e) % RAW, KD, P)
            run(sp, KD // 4, body_o)

        for layer in range(DEPTH):
            up(layer, 0)
            down(layer, 0)
            mixer(layer)
            up(layer, 1)
            down(layer, 1)
        for s in range(2):
            sp.wait_ge(out_ready, 4 * (s + 1))
            sp.dma_start(out[0, s * P:(s + 1) * P, :], y_out[:, s, :]).then_inc(out_done, 16)
        sp.wait_ge(out_done, 32)

    @block.gpsimd
    def _(pool):
        ada_v = w_ada.rearrange("l (k p) n -> l p k n", p=P)

        def load(t, layer, column, slot):
            wait(pool, ada_done, t - 1)
            pool.dma_start(ada_w[:, slot, :].rearrange("p (k n) -> p k n", k=KD),
                           ada_v[layer, :, :, bass.ds(column, P)]).then_inc(ada_in[slot], 16)

        def body(layer):
            def pair(i):
                for e in range(2):
                    column = pool.snap((2 * i + e) * P)
                    load(MODT * layer + 2 * i + e, layer, column, e)
            return pair
        load(0, 0, 0, 0)
        load(1, 0, P, 1)
        with pool.Fori(1, MODT // 2) as i:
            body(0)(i)
        with pool.Fori(0, MODT // 2) as i:
            body(1)(i)

    @block.tensor
    def _(pe):
        pe.wait_ge(const_in, 16)
        pe.wait_ge(rows_in, 16 * 12)
        for n, r in enumerate((120, 120, 108, 78)):
            pe.transpose(ps[4 + n][:, 0:r], rows[0:r, n, :], ident[0:r, 0:r]).then_inc(rows_turned, 1)
        pe.wait_ge(x_landed, 32)
        for d in range(KD):
            if d >= 4:
                pe.wait_ge(evac_act if d % 2 == 0 else evac_dve, (d - 4) // 2 + 1)
            for t in range(TT):
                m = pe.transpose(ps[d % 4][:, t * P:(t + 1) * P], x_in[:, t, d * P:(d + 1) * P], ident)
            m.then_inc(x_turned, 1)

        def ada(t, slot, use):
            pe.wait_ge(ada_in[slot], use)
            wait(pe, ada_ev, t - 1)
            for k in range(KD):
                m = pe.matmul(ps[4 + slot][:, 0:2], ada_w[:, slot, k * P:(k + 1) * P], cs[:, k, :],
                              start=(k == 0), stop=(k == KD - 1))
            m.then_inc(ada_done, 1)

        def ada_tile(t, i=0, step=0, c0=0):
            slot = (t + c0) % 2
            ada(t + c0 + step * i, slot, 16 * ((t + c0) // 2 + 1) + (16 * step // 2) * i)

        pe.wait_ge(cs_ready, 1)
        pe.wait_ge(cols_ready, 4)
        for m in range(2 * KD):
            ada_tile(m)

        def chunk(r, slot, bank, parts, t0, done=True, first=True, last=True):
            pe.wait_ge(lo_done, r + 1)
            for n, (a_hi, a_lo) in enumerate(parts):
                wh, wl = w_hi[:, slot, n * P:(n + 1) * P], w_lo[:, slot, n * P:(n + 1) * P]
                a, b = first and n == 0, last and n == len(parts) - 1
                pe.matmul(ps[bank][:, t0:TOK], wh, a_hi, start=a, stop=False)
                pe.matmul(ps[bank][:, t0:TOK], wh, a_lo, start=False, stop=False)
                m = pe.matmul(ps[bank][:, t0:TOK], wl, a_hi, start=False, stop=b)
            m.then_inc(chunk_used, 1)

        def of(hi, lo, ks, t0):
            return [(hi[:, k, t0:TOK], lo[:, k, t0:TOK]) for k in ks]

        def up(layer, f, ada_t, n):
            base, a0, d0 = BASES[layer, f"up{f}"]
            t0 = t0_of(layer) if f else 0
            pe.wait_ge(u_ready, KD * (n + 1))
            pe.wait_ge(evac_act, a0)
            pe.wait_ge(evac_dve, d0)

            def body(i):
                for q in range(4):
                    r = base + 4 * i + q
                    pe.wait_ge(evac_act if q % 2 == 0 else evac_dve, (a0 if q % 2 == 0 else d0) - 1 + 2 * i + q // 2)
                    chunk(r, (base + q) % SPLIT, q, of(u_hi, u_lo, range(KD), t0), t0)
                    if ada_t is not None:
                        ada_tile(ada_t, i, 4, q)
            run(pe, CH_UP // 4, body)

        def down(layer, f, ada_t):
            base, a0, d0 = BASES[layer, f"down{f}"]
            t0 = t0_of(layer) if f else 0
            pe.wait_ge(g_ready, KF * (2 * layer + f + 1))
            pe.wait_ge(evac_act, a0)
            pe.wait_ge(evac_dve, d0)

            def body(i):
                for e in range(2):
                    pe.wait_ge(evac_dve, d0 - 1 + 2 * i + e)
                    for q, ks in enumerate(DOWN_K):
                        chunk(base + 8 * i + 4 * e + q, (base + 4 * e + q) % SPLIT, e,
                              of(g_hi, g_lo, ks, t0), t0, first=(q == 0), last=(q == 3))
                    if ada_t is not None:
                        ada_tile(ada_t, i, 2, e)
            run(pe, KD // 2, body)

        def norm(n):
            t0 = norm_t0(n)
            k0 = KD * (n - 1)
            pe.wait_ge(evac_dve, norm_d(n))
            for k in range(KD):
                m = pe.matmul(ps[6][:, t0:TOK], mean_w, h[:, k, t0:TOK], start=(k == 0), stop=(k == KD - 1))
            m.then_inc(ln_mean, 1)
            for k in range(KD):
                pe.wait_ge(ln_sq, k0 + k + 1)
                pe.matmul(ps[7][:, t0:TOK], mean_w, scr[k % 2][:, t0:TOK], start=(k == 0),
                          stop=(k == KD - 1)).then_inc(ln_sq_used, 1)

        def proj(layer, step):
            n = PLAN[step][0]
            base, a0, d0 = BASES[layer, "proj"]
            t0 = t0_of(layer, step[0] in X_ONLY)
            if n >= 4:
                before = BY_CHUNK[n - 4]
                by = EVAC_ENGINE[before[0]]
                _, a, d, _ = PLAN[before]
                pe.wait_ge(evac_act if by == "act" else evac_dve, (a0 + a if by == "act" else d0 + d) + 1)
            chunk(base + n, (base + n) % SPLIT, n % 4, of(u_hi, u_lo, range(KD), t0), t0)

        def turn_v(layer, v):
            kind, i = ("mv", v) if v < 8 else ("dv", v - 8)
            pe.wait_ge(evac_act, BASES[layer, "proj"][1] + PLAN[kind, i][1] + 1)
            g = 12 * layer + v
            wait(pe, v_placed, g - 1)
            for t in range(TT):
                m = pe.transpose(ps[4 + v % 2][:, t * P:(t + 1) * P], scr[4 + v % 2][:, t * P:(t + 1) * P], ident)
            m.then_inc(v_turned, 1)

        def rope(layer, i):
            kind = ("dq", i) if i < 4 else ("dk", i - 4)
            pe.wait_ge(evac_act, BASES[layer, "proj"][1] + PLAN[kind][1] + 1)
            wait(pe, rope_done, 8 * layer + i - 1)
            pe.matmul(ps[6 + i % 2][:, 0:SEG], rot_w, dqk[:, i, SEG:TOK], start=True, stop=True
                      ).then_inc(rot_done, 1)

        def gates(layer):
            pe.wait_ge(wg_ready, layer + 1)
            for n, a in enumerate((u_hi, u_lo)):
                for k in range(KD):
                    m = pe.matmul(ps[6][:, :], wg[:, k, :], a[:, k, :].bitcast(F32),
                                  start=(n == 0 and k == 0), stop=(n == 1 and k == KD - 1))
            m.then_inc(mg_done, 1)

        def gates_turn(layer):
            pe.wait_ge(gate_dve, layer + 1)
            for t in range(TT):
                m = pe.transpose(ps[7][:, t * P:(t + 1) * P], gt[0][:, t * P:(t + 1) * P], ident)
            m.then_inc(gate_turn, 1)

        def mlstm(layer, head):
            t0 = t0_of(layer)
            tiles = range(t0 // P, TT)
            u = HEADS * layer + head
            nt = 4 * HEADS * layer + (len(tiles) * head if layer else 4 * head)
            if head == 0:
                gates_turn(layer)
                pe.wait_ge(v_placed, 12 * layer + 8)
                pe.wait_ge(gate_act, 4 * layer + 4)
            wait(pe, ht_ready, u)
            for n in range(2):
                row = 32 * n + head
                m = pe.matmul(ps[4 + n][:, t0:TOK], ident[0:64, row:row + 1].to_broadcast([64, P]),
                              neg_g[0:64, t0:TOK], start=True, stop=True)
            m.then_inc(ng_ready, 1)
            base, a0, d0 = BASES[layer, "proj"]
            pe.wait_ge(evac_act, a0 + PLAN["mq", head][1] + 1)
            pe.wait_ge(evac_dve, d0 + PLAN["mk", head][2] + 1)
            wait(pe, hsum_ready, nt)
            for s in range(TT):
                if s >= 2:
                    pe.wait_ge(pw_ready, 8 * u + 2 * (s - 1))
                ts = max(t0, SEG if s >= 2 else 0)
                pe.matmul(ps[6 + s % 2][:, ts:TOK], kt[:, head, s * P:(s + 1) * P], qt[:, head, ts:TOK],
                          start=True, stop=True).then_inc(s_ready, 1)
            pe.wait_ge(pw_ready, 8 * (u + 1))

            def turn_h(j, t):
                pe.wait_ge(hsum_ready, nt + j + 1)
                for e in range(2):
                    m = pe.transpose(ps[4 + e][:, t * P:(t + 1) * P], hs[:, j % 2, e * P:(e + 1) * P], ident)
                m.then_inc(h_turned, 1)
            for j, t in enumerate(tiles):
                if j:
                    pe.wait_ge(hsum_ready, nt + j)
                for n, w in enumerate("fb"):
                    keys = KEYS[w, t]
                    for s in keys:
                        m = pe.matmul(ps[6 + n][:, 0:257], pw[:, n, s, t * P:(t + 1) * P], vaug[:, s, head, :],
                                      start=(s == keys[0]), stop=(s == keys[-1]))
                m.then_inc(num_ready, 1)
                if j:
                    turn_h(j - 1, tiles[j - 1])
            turn_h(len(tiles) - 1, tiles[-1])

        def attend(layer):
            tiles = range(t0_of(layer) // P, TT)
            pe.wait_ge(v_placed, 12 * (layer + 1))
            pe.wait_ge(rope_done, 8 * (layer + 1))
            u = 16 * layer
            for t in tiles:
                keys = range(2 if t < 2 else 4)
                for head in range(HEADS):
                    wait(pe, p_ready, 2 * u)
                    for j in range(2):
                        rows_ = slice(j * DA_HALF, (j + 1) * DA_HALF)
                        pe.matmul(ps[4 + j][:, 0:len(keys) * P], dqk[rows_, head, t * P:(t + 1) * P],
                                  dqk[rows_, 4 + head, 0:len(keys) * P], start=True, stop=True
                                  ).then_inc(sc_ready, 1)
                    pe.wait_ge(wgt_ready, u + 1)
                    wait(pe, wt_ready, u)
                    for k in keys:
                        m = pe.transpose(ps[6][:, k * P:(k + 1) * P], scr[4][:, k * P:(k + 1) * P], ident)
                    m.then_inc(wgt_turned, 1)
                    pe.wait_ge(wt_ready, u + 1)
                    wait(pe, o_copied, u)
                    for k in keys:
                        m = pe.matmul(ps[7][:, 0:P], scr[5][:, k * P:(k + 1) * P], dav[:, k, head, :],
                                      start=(k == keys[0]), stop=(k == keys[-1]))
                    m.then_inc(o_ready, 1)
                    u += 1
            pe.wait_ge(o_scaled, layer + 1)
            for head in range(HEADS):
                wait(pe, yda_f, 4 * layer + head - 1)
                for t in tiles:
                    m = pe.transpose(ps[4 + head % 2][:, t * P:(t + 1) * P], oda[:, t, head, :], ident)
                m.then_inc(o_turned, 1)

        def mixer(layer):
            t0 = t0_of(layer)
            pe.wait_ge(u_ready, KD * (3 * layer + 2))
            pe.wait_ge(evac_dve, BASES[layer, "proj"][2])
            for step in ORDER:
                if step[0] in EVAC_ENGINE:
                    proj(layer, step)
                elif step[0] == "attend":
                    attend(layer)
                elif step[0] == "gates":
                    gates(layer)
                else:
                    {"turn_v": turn_v, "rope": rope, "mlstm": mlstm}[step[0]](layer, step[1])
            base, a0, d0 = BASES[layer, "gate"]
            pe.wait_ge(evac_act, a0)
            pe.wait_ge(evac_dve, d0)
            pe.wait_ge(y_ready, 12 * (layer + 1))
            pe.wait_ge(yda_ready, 4 * (layer + 1))

            def body(i):
                for q in range(12):
                    pe.wait_ge(evac_act if q % 2 == 0 else evac_dve, (a0 if q % 2 == 0 else d0) - 1 + 6 * i + q // 2)
                    if q % 2 == 0:
                        parts = of(u_hi, u_lo, range(KD), t0)
                    else:
                        hi, lo, kn = ((ysc_hi, ysc_lo, 4), (yml_hi, yml_lo, 8), (yda_hi, yda_lo, 4))[(q // 2) % 3]
                        parts = of(hi, lo, range(kn), t0)
                    chunk(base + 12 * i + q, (base + q) % SPLIT, q % 4, parts, t0)
            run(pe, KD // 2, body)
            base, a0, d0 = BASES[layer, "wo"]
            pe.wait_ge(z_ready, KD * (layer + 1))
            pe.wait_ge(evac_act, a0)
            pe.wait_ge(evac_dve, d0)

            def body_o(i):
                for e in range(4):
                    pe.wait_ge(evac_dve, d0 - 3 + 4 * i + e)
                    chunk(base + 4 * i + e, (base + e) % SPLIT, e, of(z_hi, z_lo, range(KD), t0), t0)
            run(pe, KD // 4, body_o)

        t = 2 * KD
        up(0, 0, t, 0)
        down(0, 0, t + 44)
        for m in range(4):
            ada_tile(t + 52 + m)
        norm(1)
        mixer(0)
        norm(2)
        up(0, 1, MODT, 2)
        down(0, 1, MODT + 44)
        norm(3)
        for m in range(ADA_LN):
            ada_tile(MODT + 52 + m)
        up(1, 0, None, 3)
        down(1, 0, None)
        norm(4)
        mixer(1)
        norm(5)
        up(1, 1, None, 5)
        down(1, 1, None)
        norm(6)
        pe.wait_ge(h_ready, KD * 7)
        for s in range(2):
            for q in range(2):
                n = 2 * s + q
                for k in range(4):
                    m = pe.transpose(ps[n][:, k * P:(k + 1) * P], h[:, 4 * q + k, SEG + s * P:SEG + (s + 1) * P], ident)
                m.then_inc(out_turned, 1)

    @block.scalar
    def _(act):
        chain = [0]

        def link(ins):
            chain[0] += 1
            ins.then_inc(act_chain, 1)
            act.wait_ge(act_chain, chain[0])

        def split(r, slot, raw_slot, use):
            wait(act, chunk_used, r - SPLIT + 1)
            act.wait_ge(raw_in[raw_slot], use)
            act.activation(w_hi[:, slot, :], raw[:, raw_slot, :], ACT.Copy).then_inc(hi_done, 1)

        def ahead(base, c, i=0, step=0):
            r = base + c + SPLIT
            if isinstance(i, int) and r + step * i >= CHUNKS:
                return
            split(r + step * i, r % SPLIT, r % RAW, 16 * (r // RAW + 1) + 16 * step // RAW * i)

        act.wait_ge(zeroed, 2)
        act.wait_ge(cols_ready, 4)
        act.activation(cs[:, :, 0], cols[:, 3, 60:68], ACT.Silu)
        act.activation(cs[:, :, 1], cols[:, 3, 68:76], ACT.Silu).then_inc(cs_ready, 1)
        act.wait_ge(lam_dot, 1)
        act.activation(lam_e[:, :, :], lam_e[:, :, :], ACT.Exp).then_inc(lam_exp, 1)
        for d in range(0, KD, 2):
            act.wait_ge(x_turned, d + 1)
            act.activation(h[:, d, :], ps[d % 4][:, :], ACT.Copy).then_inc(evac_act, 1)
        split(0, 0, 0, 16)
        split(1, 1, 1, 16)

        def modulate(n):
            t0 = norm_t0(n)
            act.wait_ge(cols_mod, n + 1)
            if n == 0:
                act.wait_ge(evac_act, 4)
                act.wait_ge(evac_dve, 4)
            last = None
            for k in range(KD + 1):
                if k < KD and n < 6:
                    if n:
                        act.wait_ge(ln_xn, KD * (n - 1) + k + 1)
                    for s, seg in halves(t0):
                        m = act.activation(u_hi[:, k, seg], h[:, k, seg], ACT.Identity,
                                           scale=mod_a[:, k, s:s + 1], bias=mod_b[:, k, s:s + 1])
                    m.then_inc(u_hi_done, 1)
                j = k - 1 if n < 6 else k
                if 0 <= j < KD:
                    if n < 6:
                        act.wait_ge(u_ready, KD * n + j + 1)
                    else:
                        act.wait_ge(ln_xn, KD * (n - 1) + j + 1)
                    act.activation(h[:, j, t0:TOK], h[:, j, t0:TOK], ACT.Identity, scale=res_g[:, j:j + 1],
                                   bias=res_b[:, j:j + 1]).then_inc(h_ready, 1)

        def norm(n):
            t0 = norm_t0(n)
            k0 = KD * (n - 1)
            for k in range(KD):
                act.wait_ge(ln_cent, k0 + k + 1)
                wait(act, ln_sq_used, k0 + k - 1)
                act.activation(scr[k % 2][:, t0:TOK], h[:, k, t0:TOK], ACT.Square).then_inc(ln_sq, 1)
            act.wait_ge(ln_sq_used, k0 + KD)
            act.activation(scr[2][:, t0:TOK], ps[7][:, t0:TOK], ACT.Sqrt, bias=small[:, 0:1]).then_inc(ln_std, 1)
            modulate(n)

        def up(layer, f):
            base, a0, d0 = BASES[layer, f"up{f}"]
            g0 = KF * (2 * layer + f)
            t0 = t0_of(layer) if f else 0

            def body(i):
                for q in range(4):
                    ahead(base, q, i, 4)
                    act.wait_ge(chunk_used, base + q + 1 + 4 * i)
                    if q % 2 == 0:
                        act.wait_ge(evac_dve, d0 - 1 + 2 * i + q // 2)
                        act.activation(scr[q // 2][:, t0:TOK], ps[q][:, t0:TOK], ACT.Silu).then_inc(evac_act, 1)
                    else:
                        act.wait_ge(evac_dve, d0 + 1 + 2 * i + q // 2)
                        act.activation(g_hi[:, 2 * i + q // 2, t0:TOK], scr[2 + q // 2][:, t0:TOK], ACT.Copy
                                       ).then_inc(g_hi_done, 1)
            run(act, CH_UP // 4, body)

        def down(layer, f):
            base = BASES[layer, f"down{f}"][0]

            def body(i):
                for q in range(8):
                    ahead(base, q, i, 8)
            run(act, KD // 2, body, peel_last=(layer, f) == (DEPTH - 1, 1))

        def split_y(y, hi, k, t0):
            act.wait_ge(yf_ready, y + 1)
            act.activation(hi[:, k, t0:TOK], scr[2 + y % 2][:, t0:TOK], ACT.Copy).then_inc(y_hi_done, 1)

        def proj(layer, step):
            kind, i = step
            base, a0, d0 = BASES[layer, "proj"]
            n, a, d, y = PLAN[step]
            t0 = t0_of(layer, kind in X_ONLY)
            ahead(base, n)
            if kind in ("sx", "mk"):
                return
            y += 12 * layer
            if kind == "sb":
                split_y(y, ysc_hi, i, t0)
                return
            act.wait_ge(chunk_used, base + n + 1)
            ct, cc = bias_at(layer, SEC[kind] + i)
            bias = cols[:, ct, cc:cc + 1]
            if kind == "cg":
                dst, func = cgt[:, t0:TOK], ACT.Identity
                if i:
                    act.wait_ge(evac_dve, d0 + PLAN["sx", i - 1][2] + 1)
            elif kind == "mq":
                dst, func = qt[:, i, t0:TOK], ACT.Identity
            elif kind in ("mv", "dv"):
                v = i if kind == "mv" else 8 + i
                wait(act, v_turned, 12 * layer + v - 1)
                dst, func = scr[4 + v % 2][:, t0:TOK], ACT.Identity
            elif kind == "mo":
                dst, func = scr[i % 2][:, t0:TOK], ACT.Sigmoid
                if i >= 2:
                    act.wait_ge(yf_ready, y - 1)
            else:
                if kind == "dq" and i == 0:
                    act.wait_ge(ht_ready, HEADS * (layer + 1))
                dst, func = dqk[:, i if kind == "dq" else 4 + i, t0:TOK], ACT.Identity
            act.activation(dst, ps[n % 4][:, t0:TOK], func, bias=bias).then_inc(evac_act, 1)
            if kind == "mo":
                split_y(y, yml_hi, i, t0)

        def gates(layer):
            act.wait_ge(mg_done, layer + 1)
            act.wait_ge(gate_in, 16 * 4 * DEPTH)
            act.activation(gt[1][:, :], ps[6][:, :], ACT.Identity, bias=gate_bias[:, layer:layer + 1]
                           ).then_inc(gate_act, 1)
            act.wait_ge(gate_abs, layer + 1)
            link(act.activation(gt[3][64:128, :], gt[3][64:128, :], ACT.Exp, scale=-1.0))
            act.activation(gt[3][64:128, :], gt[3][64:128, :], ACT.Ln, bias=1.0).then_inc(gate_act, 1)

        def mlstm(layer, head):
            t0 = t0_of(layer)
            tiles = range(t0 // P, TT)
            u = HEADS * layer + head
            if head == 0:
                act.wait_ge(gate_turn, layer + 1)
                act.activation(am[:, :, :], ps[7][:, :].rearrange("p (t n) -> p t n", t=TT), ACT.Copy
                               ).then_inc(gate_act, 1)
                act.activation(em[:, :, :], ps[7][:, :].rearrange("p (t n) -> p t n", t=TT)[:, :, 64:128],
                               ACT.Exp, scale=-1.0).then_inc(gate_act, 1)
            for s in range(TT):
                ranges, _ = head_ranges(s, t0)
                for n, (b, e) in enumerate(ranges):
                    v = 2 * s + n
                    act.wait_ge(x_ready, 8 * u + v + 1)
                    act.activation(xt[:, v % 2, b:e], xt[:, v % 2, b:e], ACT.Exp).then_inc(e_ready, 1)
            turned = (4 * HEADS if layer else 0) + len(tiles) * (head + 1)
            act.wait_ge(h_turned, turned)
            for e in range(2):
                m = act.activation(ht[:, 2 * head + e, t0:TOK], ps[4 + e][:, t0:TOK], ACT.Copy)
            m.then_inc(ht_ready, 1)

        def attend(layer):
            tiles = range(t0_of(layer) // P, TT)
            u = 16 * layer
            for t in tiles:
                nk = (2 if t < 2 else 4) * P
                for head in range(HEADS):
                    for j in range(2):
                        act.wait_ge(smax_ready, 2 * u + j + 1)
                        if j == 0:
                            wait(act, wgt_ready, u)
                        act.activation(scr[2 + j][:, 0:nk], ps[4 + j][:, 0:nk], ACT.Exp, scale=DA_HALF ** -0.5,
                                       bias=small[:, 2 + j:3 + j], accum_out=small[:, 4 + j:5 + j]
                                       ).then_inc(p_ready, 1)
                    act.wait_ge(wgt_turned, u + 1)
                    wait(act, o_ready, u)
                    act.activation(scr[5][:, 0:nk], ps[6][:, 0:nk], ACT.Copy).then_inc(wt_ready, 1)
                    act.wait_ge(o_copied, u + 1)
                    act.activation(scr[0][:, 0:P], oda[:, t, head, :], ACT.Square, accum_out=ssq[:, t, head:head + 1]
                                   ).then_inc(o_sq, 1)
                    u += 1
            act.wait_ge(o_sq, u)
            act.activation(ssq[:, tiles[0]:TT, :], ssq[:, tiles[0]:TT, :], ACT.Sqrt, scale=1.0 / P, bias=small[:, 0:1]
                           ).then_inc(o_std, 1)
            for head in range(HEADS):
                act.wait_ge(yda_f, 4 * layer + head + 1)
                act.activation(yda_hi[:, head, tiles[0] * P:TOK], scr[2 + head % 2][:, tiles[0] * P:TOK], ACT.Copy
                               ).then_inc(yda_h, 1)

        def mixer(layer):
            t0 = t0_of(layer)
            for step in ORDER:
                if step[0] in EVAC_ENGINE:
                    proj(layer, step)
                elif step[0] == "gates":
                    gates(layer)
                elif step[0] == "mlstm":
                    mlstm(layer, step[1])
                elif step[0] == "attend":
                    attend(layer)
            base, a0, d0 = BASES[layer, "gate"]

            def body(i):
                for q in range(12):
                    ahead(base, q, i, 12)
                    if q % 2 == 0:
                        act.wait_ge(chunk_used, base + q + 1 + 12 * i)
                        act.wait_ge(evac_dve, d0 - 1 + 6 * i + q // 2)
                        tile = SEC[("gs", "gm", "gd")[(q // 2) % 3]] + q // 6
                        ct, cc = bias_at(layer, tile)
                        act.activation(scr[(q // 2) % 2][:, t0:TOK], ps[q % 4][:, t0:TOK], ACT.Sigmoid,
                                       bias=cols[:, ct, bass.ds(cc + 2 * i, 1)]).then_inc(evac_act, 1)
                    elif q % 6 == 5:
                        act.wait_ge(z_sum, 2 * i + (KD * layer + q // 6 + 1))
                        act.activation(z_hi[:, 2 * i + q // 6, t0:TOK], scr[2 + q // 6][:, t0:TOK], ACT.Copy
                                       ).then_inc(z_hi_done, 1)
            run(act, KD // 2, body)
            base = BASES[layer, "wo"][0]

            def body_o(i):
                for e in range(4):
                    ahead(base, e, i, 4)
            run(act, KD // 4, body_o)

        modulate(0)
        for layer in range(DEPTH):
            up(layer, 0)
            down(layer, 0)
            norm(3 * layer + 1)
            mixer(layer)
            norm(3 * layer + 2)
            up(layer, 1)
            down(layer, 1)
            norm(3 * layer + 3)
        for s in range(2):
            act.wait_ge(out_turned, 2 * s + 2)
            for q in range(2):
                act.activation(y_out[:, s, q * 512:(q + 1) * 512], ps[2 * s + q][:, :], ACT.Copy
                               ).then_inc(out_ready, 2)

    @block.vector
    def _(dve):
        chain = [0]

        def link(ins):
            chain[0] += 1
            ins.then_inc(dve_chain, 1)
            dve.wait_ge(dve_chain, chain[0])

        def split(r, slot, raw_slot):
            dve.wait_ge(hi_done, r + 1)
            dve.tensor_tensor(w_lo[:, slot, :], raw[:, raw_slot, :], w_hi[:, slot, :].bitcast(F32), ALU.subtract
                              ).then_inc(lo_done, 1)

        def ahead(base, c, i=0, step=0):
            r = base + c + SPLIT
            if isinstance(i, int) and r + step * i >= CHUNKS:
                return
            split(r + step * i, r % SPLIT, r % RAW)

        dve.memset(gate_bias[:, :], 0.0).then_inc(zeroed, 1)
        dve.memset(one_zero[:, 0, :], 1.0)
        dve.memset(one_zero[:, 1, :], 0.0)
        link(dve.memset(small[:, 0:1], EPS))
        dve.memset(small[:, 1:2], 0.0).then_inc(zeroed, 1)
        for n, r in enumerate((120, 120, 108, 78)):
            dve.wait_ge(rows_turned, n + 1)
            dve.tensor_copy(cols[:, n, 0:r], ps[4 + n][:, 0:r]).then_inc(cols_ready, 1)
        dve.wait_ge(lam_landed, 64)
        for layer in range(DEPTH):
            link(dve.tensor_tensor(lam_p[:, layer], lam_in[:, layer, 0:4:2, :], lam_in[:, layer, 1:4:2, :], ALU.mult))
        dve.tensor_reduce(lam_e[:, :, :], lam_p[:, :, :, :], AXX, ALU.add).then_inc(lam_dot, 1)
        dve.wait_ge(lam_exp, 1)
        for layer in range(DEPTH):
            lam_init = 0.8 - 0.6 * math.exp(-0.3 * layer)
            link(dve.tensor_tensor(neg_lam[:, layer:layer + 1], lam_e[:, layer, 1:2], lam_e[:, layer, 0:1], ALU.subtract))
            link(dve.tensor_scalar(neg_lam[:, layer:layer + 1], neg_lam[:, layer:layer + 1], -lam_init, None, ALU.add))
        for d in range(1, KD, 2):
            dve.wait_ge(x_turned, d + 1)
            dve.tensor_copy(h[:, d, :], ps[d % 4][:, :]).then_inc(evac_dve, 1)

        def ada(t, slot, m):
            dve.wait_ge(ada_done, t + 1)
            layer = 0 if isinstance(m, int) and m < MODT else 1
            dve.tensor_scalar(mods[:, m, :], ps[4 + slot][:, 0:2], cols[:, layer, bass.ds(m - layer * MODT, 1)]
                              if not isinstance(m, int) else cols[:, layer, m - layer * MODT:m - layer * MODT + 1],
                              None, ALU.add).then_inc(ada_ev, 1)

        def ada_loop(layer, t, i, step, c0):
            dve.wait_ge(ada_done, t + c0 + 1 + step * i)
            dve.tensor_scalar(mods[:, t + c0 + step * i, :], ps[4 + (t + c0) % 2][:, 0:2],
                              cols[:, layer, bass.ds(t + c0 - layer * MODT + step * i, 1)], None, ALU.add
                              ).then_inc(ada_ev, 1)

        for m in range(2 * KD):
            ada(m, m % 2, m)
        split(0, 0, 0)
        split(1, 1, 1)

        def columns(n):
            g, b = norm_cols(n)
            if n == 6:
                dve.tensor_copy(res_g[:, :], g)
                link(dve.tensor_copy(res_b[:, :], b))
            else:
                m0 = next_mods(n)
                shift, scale = mods[:, m0:m0 + KD, :], mods[:, m0 + KD:m0 + 2 * KD, :]
                for s in range(2):
                    link(dve.scalar_tensor_tensor(mod_a[:, :, s], scale[:, :, s], 1.0, g, ALU.add, ALU.mult))
                    link(dve.scalar_tensor_tensor(mod_b[:, :, s], scale[:, :, s], 1.0, b, ALU.add, ALU.mult))
                    link(dve.tensor_tensor(mod_b[:, :, s], mod_b[:, :, s], shift[:, :, s], ALU.add))
                dve.tensor_scalar(res_g[:, :], g, ALPHA, None, ALU.mult)
                link(dve.tensor_scalar(res_b[:, :], b, ALPHA, None, ALU.mult))
            dve.engine_nop().then_inc(cols_mod, 1)

        def modulate(n):
            t0 = norm_t0(n)

            def normed(k):
                dve.tensor_tensor(h[:, k, t0:TOK], h[:, k, t0:TOK], scr[3][:, t0:TOK], ALU.mult).then_inc(ln_xn, 1)
            if n:
                normed(0)
            for k in range(KD):
                if n and k + 1 < KD:
                    normed(k + 1)
                if n == 6:
                    continue
                if n:
                    dve.wait_ge(ln_xn, KD * (n - 1) + k + 1)
                for s, seg in halves(t0):
                    m = dve.tensor_scalar(scr[4 + k % 2][:, seg], h[:, k, seg], mod_a[:, k, s:s + 1],
                                          mod_b[:, k, s:s + 1], ALU.mult, ALU.add)
                link(m)
                dve.wait_ge(u_hi_done, KD * n + k + 1)
                dve.tensor_tensor(u_lo[:, k, t0:TOK], scr[4 + k % 2][:, t0:TOK], u_hi[:, k, t0:TOK].bitcast(F32),
                                  ALU.subtract).then_inc(u_ready, 1)

        def norm(n):
            t0 = norm_t0(n)
            k0 = KD * (n - 1)
            columns(n)
            dve.wait_ge(ln_mean, n)
            for k in range(KD):
                dve.tensor_tensor(h[:, k, t0:TOK], h[:, k, t0:TOK], ps[6][:, t0:TOK], ALU.subtract
                                  ).then_inc(ln_cent, 1)
            dve.wait_ge(ln_std, n)
            link(dve.reciprocal(scr[3][:, t0:TOK], scr[2][:, t0:TOK]))
            modulate(n)

        def gate_columns(layer, i, factor):
            m0 = gate_mods(layer, i)
            dve.wait_ge(h_ready, KD * (3 * layer + i + 1))
            link(dve.tensor_scalar(gate[:, :, :], mods[:, m0:m0 + KD, :], factor, None, ALU.mult))

        def add_branch(layer, tile, bank, t0):
            for s, seg in halves(t0):
                m = dve.scalar_tensor_tensor(h[:, tile, seg], ps[bank][:, seg], gate[:, tile, s:s + 1],
                                             h[:, tile, seg], ALU.mult, ALU.add)
            m.then_inc(evac_dve, 1)

        def up(layer, f, ada_t):
            base, a0, d0 = BASES[layer, f"up{f}"]
            g0 = KF * (2 * layer + f)
            t0 = t0_of(layer) if f else 0

            def body(i):
                for q in range(4):
                    ahead(base, q, i, 4)
                    if q % 2:
                        e = q // 2
                        dve.wait_ge(chunk_used, base + q + 1 + 4 * i)
                        dve.wait_ge(evac_act, a0 + e + 1 + 2 * i)
                        dve.tensor_tensor(scr[2 + e][:, t0:TOK], scr[e][:, t0:TOK], ps[q][:, t0:TOK], ALU.mult
                                          ).then_inc(evac_dve, 1)
                        dve.wait_ge(g_hi_done, g0 + e + 1 + 2 * i)
                        dve.tensor_tensor(g_lo[:, 2 * i + e, t0:TOK], scr[2 + e][:, t0:TOK],
                                          g_hi[:, 2 * i + e, t0:TOK].bitcast(F32), ALU.subtract).then_inc(g_ready, 1)
                    if ada_t is not None:
                        ada_loop(ada_t // MODT, ada_t, i, 4, q)
            run(dve, CH_UP // 4, body)

        def down(layer, f, ada_t):
            base = BASES[layer, f"down{f}"][0]
            t0 = t0_of(layer) if f else 0
            gate_columns(layer, 2 * f, 0.5)

            def body(i):
                for e in range(2):
                    for q in range(4):
                        ahead(base, 4 * e + q, i, 8)
                    dve.wait_ge(chunk_used, base + 4 * e + 4 + 8 * i)
                    add_branch(layer, 2 * i + e, e, t0)
                    if ada_t is not None:
                        ada_loop(ada_t // MODT, ada_t, i, 2, e)
            run(dve, KD // 2, body, peel_last=(layer, f) == (DEPTH - 1, 1))

        def split_y(y, hi, lo, k, t0):
            dve.wait_ge(y_hi_done, y + 1)
            dve.tensor_tensor(lo[:, k, t0:TOK], scr[2 + y % 2][:, t0:TOK], hi[:, k, t0:TOK].bitcast(F32),
                              ALU.subtract).then_inc(y_ready, 1)

        def proj(layer, step):
            kind, i = step
            base, a0, d0 = BASES[layer, "proj"]
            n, a, d, y = PLAN[step]
            t0 = t0_of(layer, kind in X_ONLY)
            bank = ps[n % 4]
            ahead(base, n)
            y += 12 * layer
            ct, cc = bias_at(layer, SEC[kind] + i)
            bias = cols[:, ct, cc:cc + 1]
            if kind == "mk":
                dve.wait_ge(chunk_used, base + n + 1)
                dve.tensor_scalar(kt[:, i, :], bank[:, :], bias, DQK ** -0.5, ALU.add, ALU.mult).then_inc(evac_dve, 1)
            elif kind == "sx":
                dve.wait_ge(chunk_used, base + n + 1)
                dve.wait_ge(evac_act, a0 + PLAN["cg", i][1] + 1)
                if i == 0:
                    link(dve.memset(zpad[:, :, :], 0.0))
                for s, seg in halves(t0):
                    m = dve.scalar_tensor_tensor(zpad[:, s, 1:SEG + 1], bank[:, seg], bias, cgt[:, seg],
                                                 ALU.add, ALU.mult)
                m.then_inc(evac_dve, 1)
                dve.wait_ge(evac_dve, d0 + d + 1)
                tap = [cols[:, 3, 36 + 12 * layer + 4 * j + i:37 + 12 * layer + 4 * j + i] for j in range(3)]
                s0 = t0 // SEG
                z, o = zpad[:, s0:2, :], cv[:, t0:TOK].rearrange("p (s t) -> p s t", t=SEG)
                link(dve.tensor_scalar(o, z[:, :, 0:SEG], tap[0], None, ALU.mult))
                link(dve.scalar_tensor_tensor(o, z[:, :, 1:SEG + 1], tap[1], o, ALU.mult, ALU.add))
                link(dve.scalar_tensor_tensor(o, z[:, :, 2:SEG + 2], tap[2], o, ALU.mult, ALU.add))
            elif kind == "sb":
                dve.wait_ge(chunk_used, base + n + 1)
                dve.scalar_tensor_tensor(scr[2 + y % 2][:, t0:TOK], bank[:, t0:TOK], bias, cv[:, t0:TOK],
                                         ALU.add, ALU.mult).then_inc(evac_dve, 1)
                dve.wait_ge(evac_dve, d0 + d + 1)
                dve.engine_nop().then_inc(yf_ready, 1)
                split_y(y, ysc_hi, ysc_lo, i, t0)
            elif kind == "mo":
                dve.wait_ge(evac_act, a0 + a + 1)
                dve.wait_ge(ht_ready, HEADS * (layer + 1))
                dve.tensor_tensor(scr[2 + y % 2][:, t0:TOK], scr[i % 2][:, t0:TOK], ht[:, i, t0:TOK], ALU.mult
                                  ).then_inc(yf_ready, 1)
                split_y(y, yml_hi, yml_lo, i, t0)

        def turn_v(layer, v):
            g = 12 * layer + v
            dve.wait_ge(v_turned, g + 1)
            src = ps[4 + v % 2][:, :].rearrange("p (t n) -> p t n", t=TT)
            if v < 8:
                dst = vaug[:, :, v // 2, (v % 2) * P:(v % 2 + 1) * P]
            else:
                dst = dav[:, :, v - 8, :]
            dve.tensor_copy(dst, src).then_inc(v_placed, 1)

        def rope(layer, i):
            xs = dqk[:, i, SEG:TOK]
            dve.wait_ge(rot_done, 8 * layer + i + 1)
            wait(dve, rope_done, 8 * layer + i)
            dve.tensor_tensor(scr[0][:, 0:SEG], ps[6 + i % 2][:, 0:SEG], rope_sin, ALU.mult)
            link(dve.tensor_tensor(xs, xs, rope_cos, ALU.mult))
            dve.tensor_tensor(xs, xs, scr[0][:, 0:SEG], ALU.add).then_inc(rope_done, 1)

        def gate_weights(layer):
            link(dve.memset(wg[:, :, :], 0.0))
            dve.wait_ge(wg_landed, 16 * (layer + 1))
            dve.tensor_copy(wg[:, :, :].rearrange("p k (q n) -> p k q n", q=4)[:, :, :, 0:4],
                            wg_in[:, :, :].rearrange("p k (q n) -> p k q n", q=4)).then_inc(wg_ready, 1)

        def flip(dst, src):
            dve.tensor_copy(dst[:, 0:SEG], rev(src, 0))
            return dve.tensor_copy(dst[:, SEG:TOK], rev(src, 1))

        def rev(src, s):
            return src[:, s * SEG:(s + 1) * SEG][:, ::-1]

        def gates(layer):
            gate_weights(layer)
            dve.memset(vaug[:, :, :, 256:257], 1.0)
            raw_g, lf, ln1, ia, la = gt[1], gt[2], gt[3], gt[4], gt[5]
            dve.wait_ge(gate_act, 4 * layer + 1)
            link(dve.tensor_scalar(ln1[64:128, :], raw_g[64:128, :], -1.0, None, ALU.mult))
            dve.tensor_tensor(ln1[64:128, :], raw_g[64:128, :], ln1[64:128, :], ALU.max).then_inc(gate_abs, 1)
            link(dve.tensor_scalar(lf[64:128, :], raw_g[64:128, :], 0.0, None, ALU.min))
            dve.wait_ge(gate_act, 4 * layer + 2)
            link(dve.tensor_tensor(lf[64:128, :], lf[64:128, :], ln1[64:128, :], ALU.subtract))
            dve.tensor_copy(ia[0:32, :], raw_g[0:32, :])
            flip(ia[32:64, :], raw_g[32:64, :])
            dve.tensor_copy(la[0:32, :], lf[64:96, :])
            link(flip(la[32:64, :], lf[96:128, :]))
            ones, fsum, gmax = gt[6], gt[7], gt[2]
            link(dve.memset(ones[0:64, :], 1.0))
            link(dve.tensor_tensor_scan(fsum[0:64, :], ones[0:64, :], la[0:64, :], 0.0, ALU.mult, ALU.add))
            link(dve.tensor_tensor(ia[0:64, :], ia[0:64, :], fsum[0:64, :], ALU.subtract))
            link(dve.tensor_tensor_scan(gmax[0:64, :], ones[0:64, :], ia[0:64, :], -3.0e38, ALU.mult, ALU.max))
            link(dve.tensor_tensor(fsum[0:64, :], fsum[0:64, :], gmax[0:64, :], ALU.add))
            link(dve.tensor_scalar(gmax[0:64, :], gmax[0:64, :], -1.0, None, ALU.mult))
            top = gt[0]
            dve.tensor_copy(top[0:32, :], ia[0:32, :])
            flip(top[32:64, :], ia[32:64, :])
            dve.tensor_copy(top[64:96, :], fsum[0:32, :])
            flip(top[96:128, :], fsum[32:64, :])
            dve.tensor_copy(neg_g[0:32, :], gmax[0:32, :])
            flip(neg_g[32:64, :], gmax[32:64, :]).then_inc(gate_dve, 1)

        def mlstm(layer, head):
            t0 = t0_of(layer)
            tiles = range(t0 // P, TT)
            u = HEADS * layer + head
            if head == 0:
                dve.wait_ge(gate_act, 4 * layer + 4)
            dve.wait_ge(ng_ready, u + 1)

            def exponent(v):
                s, n = v // 2, v % 2
                b, e = head_ranges(s, t0)[0][n]
                row = 32 * n + head
                if v >= 2:
                    dve.wait_ge(pw_ready, 8 * u + v - 1)
                dve.tensor_scalar(xt[:, v % 2, b:e], ps[4 + n][:, b:e], am[:, s, row:row + 1], 0.0, ALU.add, ALU.min
                                  ).then_inc(x_ready, 1)

            def weigh(v):
                s, n = v // 2, v % 2
                (b, e), diag = head_ranges(s, t0)[0][n], head_ranges(s, t0)[1]
                dve.wait_ge(e_ready, 8 * u + v + 1)
                dve.wait_ge(s_ready, 4 * u + s + 1)
                m = dve.tensor_tensor(pw[:, n, s, b:e], xt[:, v % 2, b:e], ps[6 + s % 2][:, b:e], ALU.mult)
                if diag is not None:
                    link(m)
                    own = pw[:, n, s, s * P:(s + 1) * P]
                    m = dve.tensor_tensor(own, own, (mask_f, mask_b)[n], ALU.mult)
                m.then_inc(pw_ready, 1)
            for v in range(8):
                exponent(v)
                if v:
                    weigh(v - 1)
            weigh(7)
            n0 = (16 if layer else 0) + len(tiles) * head
            for j, t in enumerate(tiles):
                dve.wait_ge(num_ready, n0 + j + 1)
                for n in range(2):
                    m = dve.tensor_scalar(small[:, 12 + n:13 + n], ps[6 + n][:, 256:257], -1.0, None, ALU.mult)
                link(m)
                for n in range(2):
                    row = 32 * n + head
                    m = dve.scalar_tensor_tensor(small[:, 6 + n:7 + n], small[:, 12 + n:13 + n],
                                                 em[:, t, row:row + 1], ps[6 + n][:, 256:257], ALU.max, ALU.max)
                link(m)
                link(dve.reciprocal(small[:, 8:10], small[:, 6:8]))
                if j >= 2:
                    dve.wait_ge(h_turned, n0 + j - 1)
                link(dve.tensor_scalar(hf[:, :], ps[6][:, 0:256], small[:, 8:9], None, ALU.mult))
                dve.scalar_tensor_tensor(hs[:, j % 2, :], ps[7][:, 0:256], small[:, 9:10], hf[:, :],
                                         ALU.mult, ALU.add).then_inc(hsum_ready, 1)

        def attend(layer):
            tiles = range(t0_of(layer) // P, TT)
            scale = DA_HALF ** -0.5
            u = 16 * layer
            for t in tiles:
                nk = (2 if t < 2 else 4) * P
                for head in range(HEADS):
                    for j in range(2):
                        dve.wait_ge(sc_ready, 2 * u + j + 1)
                        link(dve.tensor_reduce(small[:, 10 + j:11 + j], ps[4 + j][:, 0:nk], AXX, ALU.max))
                        dve.tensor_scalar(small[:, 2 + j:3 + j], small[:, 10 + j:11 + j], -scale, None, ALU.mult
                                          ).then_inc(smax_ready, 1)
                    dve.wait_ge(p_ready, 2 * u + 2)
                    link(dve.reciprocal(small[:, 12:14], small[:, 4:6]))
                    link(dve.tensor_tensor(small[:, 14:15], small[:, 13:14], neg_lam[:, layer:layer + 1], ALU.mult))
                    wait(dve, wgt_turned, u)
                    link(dve.tensor_scalar(scr[3][:, 0:nk], scr[3][:, 0:nk], small[:, 14:15], None, ALU.mult))
                    dve.scalar_tensor_tensor(scr[4][:, 0:nk], scr[2][:, 0:nk], small[:, 12:13], scr[3][:, 0:nk],
                                             ALU.mult, ALU.add).then_inc(wgt_ready, 1)
                    dve.wait_ge(o_ready, u + 1)
                    dve.tensor_copy(oda[:, t, head, :], ps[7][:, 0:P]).then_inc(o_copied, 1)
                    u += 1
            dve.wait_ge(o_std, layer + 1)
            link(dve.reciprocal(ssq[:, tiles[0]:TT, :], ssq[:, tiles[0]:TT, :]))
            for t in tiles:
                for head in range(HEADS):
                    m = dve.tensor_scalar(oda[:, t, head, :], oda[:, t, head, :], ssq[:, t, head:head + 1], None, ALU.mult)
            m.then_inc(o_scaled, 1)
            t0 = tiles[0] * P
            for head in range(HEADS):
                dve.wait_ge(o_turned, 4 * layer + head + 1)
                if head >= 2:
                    dve.wait_ge(yda_h, 4 * layer + head - 1)
                lam_init = 0.8 - 0.6 * math.exp(-0.3 * layer)
                f = scr[2 + head % 2][:, t0:TOK]
                dve.tensor_scalar(f, ps[4 + head % 2][:, t0:TOK], cols[:, 3, 76 + layer:77 + layer], 1.0 - lam_init,
                                  ALU.mult, ALU.mult).then_inc(yda_f, 1)
                dve.wait_ge(yda_h, 4 * layer + head + 1)
                dve.tensor_tensor(yda_lo[:, head, t0:TOK], f, yda_hi[:, head, t0:TOK].bitcast(F32), ALU.subtract
                                  ).then_inc(yda_ready, 1)

        def mixer(layer):
            t0 = t0_of(layer)
            for step in ORDER:
                if step[0] in EVAC_ENGINE:
                    proj(layer, step)
                elif step[0] == "gates":
                    gates(layer)
                elif step[0] == "attend":
                    attend(layer)
                else:
                    {"turn_v": turn_v, "rope": rope, "mlstm": mlstm}[step[0]](layer, step[1])
            base, a0, d0 = BASES[layer, "gate"]

            def body(i):
                for q in range(12):
                    ahead(base, q, i, 12)
                    if q % 2 == 0:
                        continue
                    e = q // 6
                    dve.wait_ge(chunk_used, base + q + 1 + 12 * i)
                    dve.wait_ge(evac_act, a0 + q // 2 + 1 + 6 * i)
                    z = scr[2 + e][:, t0:TOK]
                    dst = z if q % 6 == 1 else scr[4][:, t0:TOK]
                    dve.tensor_tensor(dst, scr[(q // 2) % 2][:, t0:TOK], ps[q % 4][:, t0:TOK], ALU.mult
                                      ).then_inc(evac_dve, 1)
                    dve.wait_ge(evac_dve, d0 + q // 2 + 1 + 6 * i)
                    if q % 6 == 3:
                        dve.tensor_tensor(z, z, dst, ALU.add).then_inc(z_part, 1)
                        dve.wait_ge(z_part, KD * layer + e + 1 + 2 * i)
                    if q % 6 == 5:
                        dve.tensor_tensor(z, z, dst, ALU.add).then_inc(z_sum, 1)
                        dve.wait_ge(z_hi_done, KD * layer + e + 1 + 2 * i)
                        dve.tensor_tensor(z_lo[:, 2 * i + e, t0:TOK], z, z_hi[:, 2 * i + e, t0:TOK].bitcast(F32),
                                          ALU.subtract).then_inc(z_ready, 1)
            run(dve, KD // 2, body)
            gate_columns(layer, 1, 1.0)
            base = BASES[layer, "wo"][0]

            def body_o(i):
                for e in range(4):
                    ahead(base, e, i, 4)
                    dve.wait_ge(chunk_used, base + e + 1 + 4 * i)
                    add_branch(layer, 4 * i + e, e, t0)
            run(dve, KD // 4, body_o)

        dve.wait_ge(evac_act, 4)
        dve.wait_ge(evac_dve, 4)
        dve.wait_ge(ada_ev, 2 * KD)
        columns(0)
        modulate(0)
        t = 2 * KD
        up(0, 0, t)
        down(0, 0, t + 44)
        for m in range(4):
            ada(t + 52 + m, (t + m) % 2, t + 52 + m)
        dve.wait_ge(ada_ev, MODT)
        norm(1)
        mixer(0)
        norm(2)
        up(0, 1, MODT)
        down(0, 1, MODT + 44)
        norm(3)
        for m in range(ADA_LN):
            ada(MODT + 52 + m, m % 2, MODT + 52 + m)
        dve.wait_ge(ada_ev, 2 * MODT)
        up(1, 0, None)
        down(1, 0, None)
        norm(4)
        mixer(1)
        norm(5)
        up(1, 1, None)
        down(1, 1, None)
        norm(6)

    block.__exit__(None, None, None)


def constants():
    out = np.zeros((P, 1152), np.float32)
    row, col = np.arange(P)[:, None], np.arange(P)[None, :]
    out[:, 0:128] = row == col
    out[:, 128:256] = col >= row
    out[:, 256:384] = col <= row
    first = (col % 64) < 32
    out[:, 384:512] = np.where(first & (row == col + 32), -1.0, 0.0) + np.where(~first & (row == col - 32), 1.0, 0.0)
    out[:, 512:640] = 1.0 / D
    n_freq = DA_HALF // 4
    inv = np.float32(10000.0) ** (-np.arange(n_freq, dtype=np.float32) / np.float32(n_freq))
    t = np.arange(SEG)
    ang = np.concatenate([(t // GRID_W).astype(np.float32)[None, :] * inv[:, None],
                          (t % GRID_W).astype(np.float32)[None, :] * inv[:, None]], 0)
    out[:, 640:896] = np.tile(np.cos(ang), (4, 1))
    out[:, 896:1152] = np.tile(np.sin(ang), (4, 1))
    return out


_INS = ["x", "c", "ctx", "c_ctx", "w_ada", "b_ada", "ln_g", "ln_b", "ffn1_up", "ffn1_down", "ffn2_up",
        "ffn2_down", "w_in", "b_in", "conv_w", "w_sc", "w_ml", "w_da", "w_o", "lam_q1", "lam_k1", "lam_q2",
        "lam_k2", "da_norm_g"]


def kernel(**inputs):
    import concourse.bacc as _bacc
    from concourse.bass_utils import run_bass_kernel_spmd as _run

    nc = _bacc.Bacc("TRN2", target_bir_lowering=False, num_devices=1)
    arrays, args = {}, []
    for name in _INS + ["consts"]:
        a = constants() if name == "consts" else np.ascontiguousarray(inputs[name])
        arrays[f"in_{name}"] = a
        args.append(nc.dram_tensor(f"in_{name}", a.shape, mybir.dt.from_np(a.dtype), kind="ExternalInput").ap())
    args.append(nc.dram_tensor("out_0", (1, SEG, D), F32, kind="ExternalOutput").ap())
    build(nc, *args)
    r = _run(nc, [arrays], core_ids=[0])
    return r.results[0]["out_0"]
```

```python
import math

import numpy as np

import concourse.bass as bass
from concourse import mybir

F32 = mybir.dt.float32
F32R = mybir.dt.float32r
ACT = mybir.ActivationFunctionType
ALU = mybir.AluOpType
AXX = mybir.AxisListType.X

P = 128
D = 1024
KD = D // P
SEG = 256
TOK = 2 * SEG
TT = TOK // P
DEPTH = 2
FH = 2816
KF = FH // P
N_IN = 9232
MG_COL = 4608
GRID_W = 64
HEADS = 4
DQK = 128
DA_HALF = 64
ALPHA = (2 * DEPTH) ** 0.25
EPS = 1e-5
N_MOD = 9
MODT = N_MOD * KD
DOWN_K = [range(0, 6), range(6, 12), range(12, 17), range(17, 22)]
RAW = 2
RAW_LATE = 4
SPLIT = 4
CH_UP, CH_DOWN, CH_PROJ, CH_GATE, CH_WO = 2 * KF, 4 * KD, 48, 6 * KD, KD
BLOCK = 4 * P
ADA_BLOCKS = N_MOD * D // BLOCK

SEC = {"sb": 0, "cg": 4, "sx": 8, "mq": 12, "mk": 16, "mv": 20, "mo": 28,
       "dq": 36, "dk": 40, "dv": 44, "gs": 48, "gm": 56, "gd": 64}


UP_PLAIN = [("w", q) for q in range(4)]
UP_FIRST = UP_PLAIN + [("a", j) for j in range(4)]
UP_ADA = [x for q in range(4) for x in (("a", q), ("w", q))]
GATE_PLAIN = [("w", q) for q in range(12)]
GATE_ADA = (GATE_PLAIN[0:2] + [("a", 0)] + GATE_PLAIN[2:5] + [("a", 1)] + GATE_PLAIN[5:8] + [("a", 2)]
            + GATE_PLAIN[8:10] + [("a", 3)] + GATE_PLAIN[10:12])
ADA_OF = {(0, "up0"): 4, (0, "proj"): 15, (0, "gate"): 18, (0, "up1"): 22, (1, "proj"): 33}


def in_col(tile):
    return tile * P + (16 if tile >= 36 else 0)


def bias_at(layer, tile):
    if layer == 0:
        return 2, tile
    return (2, 72 + tile) if tile < 36 else (3, tile - 36)


def proj_order():
    order = [("mq", i) for i in range(4)] + [("gates", 0)]
    for i in range(4):
        order += [("mk", i)]
        if i:
            order += [("ada", 0, i - 1)]
    order += [("ada", 0, 3)]
    for i in range(8):
        order.append(("mv", i))
        if i == 0:
            order.append(("adat", 0))
        if i:
            order.append(("turn_v", i - 1))
    side = [("ml_gates", 0)]
    for h in range(HEADS):
        side += [("ml_s", h, s) for s in range(TT)] + [("ml_n", h, t) for t in range(TT)] + [("ml_t", h)]
    main = []
    for i in range(4):
        main += [("cg", i), ("sx", i), ("sb", i)]
    order += [main.pop(0), ("turn_v", 7)]
    per = (len(side) + len(main) - 1) // len(main)
    while main:
        order += side[:per]
        del side[:per]
        order.append(main.pop(0))
    order += side
    order += [("mo", i) for i in range(8)]
    for i in range(4):
        order.append(("dv", i))
        if i:
            order.append(("turn_v", 8 + i - 1))
    order.append(("dq", 0))
    order.append(("turn_v", 11))
    order += [("dq", 1), ("rope", 0), ("dq", 2), ("rope", 1), ("dq", 3), ("rope", 2)]
    order += [("dk", 0), ("rope", 3), ("dk", 1), ("rope", 4), ("dk", 2), ("rope", 5)]
    order += [("ada", 1, j) for j in range(4)] + [("dk", 3), ("adat", 1), ("rope", 6)]
    order += [("ada", 2, j) for j in range(4)] + [("rope", 7), ("adat", 2), ("attend", 0)]
    return order


ORDER = proj_order()
EVAC_ENGINE = {"mq": "act", "mk": "dve", "mv": "act", "cg": "act", "sx": "dve", "sb": "dve",
               "mo": "act", "dv": "act", "dq": "act", "dk": "act"}
X_ONLY = {"cg", "sx", "sb", "mq", "mo", "dq"}


def proj_plan():
    plan, r, n, a, d, y = {}, 0, 0, 0, 0, 0
    for step in ORDER:
        if step[0] == "ada":
            plan[step] = (r,)
            r += 1
        elif step[0] in EVAC_ENGINE:
            plan[step] = (r, n, a, d, y)
            r += 1
            n += 1
            a += EVAC_ENGINE[step[0]] == "act"
            d += EVAC_ENGINE[step[0]] == "dve"
            y += step[0] in ("sb", "mo")
    assert n == CH_PROJ
    return plan, r, a, d


PLAN, PROJ_R, PROJ_A, PROJ_D = proj_plan()
NTH_PROJ = {v[1]: k for k, v in PLAN.items() if len(v) > 1}


def bases():
    out, r, a, d = {}, 0, 4, 4
    for layer in range(DEPTH):
        for name in ("up0", "down0", "proj", "gate", "wo", "up1", "down1"):
            out[layer, name] = (r, a, d)
            kind = name.rstrip("01")
            r += {"up": CH_UP, "down": CH_DOWN, "proj": PROJ_R, "gate": CH_GATE, "wo": CH_WO}[kind]
            if (layer, name) in ADA_OF:
                r += {"up": 4 * (CH_UP // 4), "proj": 0, "gate": 4 * (KD // 2)}[kind]
            a += {"up": KF, "down": 0, "proj": PROJ_A, "gate": 3 * KD, "wo": 0}[kind]
            d += {"up": KF, "down": KD, "proj": PROJ_D, "gate": 3 * KD, "wo": KD}[kind]
    return out, r


BASES, CHUNKS = bases()
LATE = BASES[DEPTH - 1, "gate"][0]
assert LATE % RAW == 0


def raw_place(base, c, i=0, step=0):
    r = base + c
    if r < LATE:
        return r % RAW, 16 * (r // RAW + 1) + 16 * step // RAW * i, r - RAW + 1 + step * i
    slot = (r - LATE) % RAW_LATE
    before = LATE // RAW if slot < RAW else 0
    return (slot, 16 * (before + (r - LATE) // RAW_LATE + 1) + 16 * step // RAW_LATE * i,
            r - RAW_LATE + 1 + step * i)


def up_patterns(layer, f):
    return (UP_FIRST, UP_ADA) if (layer, f"up{f}") in ADA_OF else (UP_PLAIN, UP_PLAIN)


def gate_pattern(layer):
    return GATE_ADA if (layer, "gate") in ADA_OF else GATE_PLAIN


def segments(s, n, t0):
    if n == 0:
        found = [(max(s * P, t0), TOK)]
    elif s >= 2:
        found = [(SEG, (s + 1) * P)]
    else:
        found = [(0, (s + 1) * P), (SEG, TOK)] if t0 == 0 else [(SEG, TOK)]
        if t0 == 0 and s == 1:
            found = [(0, TOK)]
    return found, (s if s * P >= t0 else None)


KEYS = {("f", 0): [0], ("f", 1): [0, 1], ("f", 2): [0, 1, 2], ("f", 3): [0, 1, 2, 3],
        ("b", 0): [0, 1], ("b", 1): [1], ("b", 2): [0, 1, 2, 3], ("b", 3): [0, 1, 3]}


def build(nc, x, c, ctx, c_ctx, w_ada, b_ada, ln_g, ln_b, ffn1_up, ffn1_down, ffn2_up, ffn2_down,
          w_in, b_in, conv_w, w_sc, w_ml, w_da, w_o, lam_q1, lam_k1, lam_q2, lam_k2, da_norm_g,
          consts, out):
    spot = [16512]

    def at(name, shape, dtype, offset=None):
        size = int(np.prod(shape[1:])) * 4
        if offset is None:
            offset = spot[0]
            spot[0] += (size + 31) // 32 * 32
        return nc.alloc_sbuf_tensor_at(name, shape, dtype, offset=offset)

    h = at("h", [P, KD, TOK], F32)
    u_hi = at("u_hi", [P, KD, TOK], F32R)
    u_lo = at("u_lo", [P, KD, TOK], F32R)
    raw = at("raw", [P, RAW, D], F32)
    w_hi = at("w_hi", [P, SPLIT, D], F32R)
    w_lo = at("w_lo", [P, SPLIT, D], F32R)
    con = at("con", [P, 1154], F32)
    ada_sum = con[0:4, 1152:1154]
    ident, mask_f, mask_b = con[:, 0:128], con[:, 128:256], con[:, 256:384]
    rot_w, mean_w = con[:, 384:512], con[:, 512:640]
    rope_cos, rope_sin = con[:, 640:896], con[:, 896:1152]
    cols = at("cols", [P, 4, P], F32)
    mods = at("mods", [P, DEPTH * MODT, 2], F32)
    cs = at("cs", [P, KD, 2], F32)
    cs_parts = at("cs_parts", [P, KD, 4], F32R)
    ada_row = at("ada_row", [4, BLOCK], F32)
    one_zero = at("one_zero", [P, 2, KD], F32)
    mod_a = at("mod_a", [P, KD, 2], F32)
    mod_b = at("mod_b", [P, KD, 2], F32)
    res_g = at("res_g", [P, KD], F32)
    res_b = at("res_b", [P, KD], F32)
    gate = at("gate", [P, KD, 2], F32)
    neg_lam = at("neg_lam", [P, DEPTH], F32)
    lam_e = at("lam_e", [P, DEPTH, 2], F32)
    gate_bias = at("gate_bias", [P, DEPTH], F32)
    small = at("small", [P, 16], F32)
    att = at("att", [P, 2, 10], F32)
    region = spot[0]
    spot[0] += 96 * 1024
    scr = [at(f"scr{i}", [P, TOK], F32) for i in range(6)]
    assert spot[0] <= 229368, spot[0]
    KB = 1024
    g_hi = at("g_hi", [P, KF, TOK], F32R, region)
    g_lo = at("g_lo", [P, KF, TOK], F32R, region + KF * TOK * 4)
    x_in = at("x_in", [P, TT, D], F32, region)
    rows = at("rows", [P, 4, P], F32, region + 16 * KB)
    stage = at("stage", [P, 16, D], F32, region + 24 * KB)
    lam_in = at("lam_in", [P, DEPTH, 4, DA_HALF], F32, region + 20 * KB)
    lam_p = at("lam_p", [P, DEPTH, 2, DA_HALF], F32, region + 22 * KB)
    y_out = at("y_out", [P, 2, D], F32, region)
    ysc_hi = at("ysc_hi", [P, 4, TOK], F32R, region)
    ysc_lo = at("ysc_lo", [P, 4, TOK], F32R, region + 8 * KB)
    yml_hi = at("yml_hi", [P, 8, TOK], F32R, region + 16 * KB)
    yml_lo = at("yml_lo", [P, 8, TOK], F32R, region + 32 * KB)
    vaug = at("vaug", [P, TT, HEADS, 257], F32, region + 16 * KB)
    neg_g = at("neg_g", [64, TOK], F32, region + 33 * KB)
    am = at("am", [P, TT, P], F32, region + 35 * KB)
    em = at("em", [P, TT, 64], F32, region + 37 * KB)
    xt = at("xt", [P, 2, TOK], F32, region + 38 * KB)
    hs = at("hs", [P, 2, SEG], F32, region + 42 * KB)
    hf = at("hf", [P, SEG], F32, region + 44 * KB)
    pw = at("pw", [P, 2, TT, TOK], F32, region + 48 * KB)
    nam = at("nam", [P, TT, 64], F32, region + 45 * KB)
    cgt, cv = scr[0], scr[1]
    zpad = at("zpad", [P, 2, SEG + 2], F32, region + 96 * KB + 4 * 2 * KB)
    dav = at("dav", [P, TT, HEADS, P], F32, region + 48 * KB)
    yda_hi = at("yda_hi", [P, 4, TOK], F32R, region + 48 * KB)
    yda_lo = at("yda_lo", [P, 4, TOK], F32R, region + 56 * KB)
    gt = [at(f"gt{i}", [P, TOK], F32, region + (64 + 2 * i) * KB) for i in range(8)]
    ht = at("ht", [P, 8, TOK], F32, region + 64 * KB)
    oda = at("oda", [P, TT, HEADS, P], F32, region + 64 * KB)
    ssq = at("ssq", [P, TT, HEADS], F32, region + 72 * KB)
    wgt = [scr[4], at("wgt1", [P, TOK], F32, region + 73 * KB)]
    wgt_t = [scr[5], at("wgt_t1", [P, TOK], F32, region + 75 * KB)]
    junk = at("junk", [P, P], F32, region + 77 * KB)
    z_hi = at("z_hi", [P, KD, TOK], F32R, region + 64 * KB)
    z_lo = at("z_lo", [P, KD, TOK], F32R, region + 80 * KB)
    qt = at("qt", [P, HEADS, TOK], F32, region + 80 * KB)
    kt = at("kt", [P, HEADS, TOK], F32, region + 88 * KB)
    dqk = at("dqk", [P, 8, TOK], F32, region + 80 * KB)
    wg_in = at("wg_in", [P, KD, 16], F32, region + 88 * KB)
    wg = at("wg", [P, KD, P], F32, region + 90 * KB)

    def raw_tiles(slot, kt_n=KD):
        if slot < RAW:
            return raw[:, slot, :].rearrange("p (k n) -> p k n", n=P)[:, 0:kt_n, :]
        return h[:, 0:kt_n, (slot - RAW) * P:(slot - RAW + 1) * P]

    def split_tiles(w, slot):
        return w[:, slot, :].rearrange("p (k n) -> p k n", n=P)

    ps = [nc.alloc_psum_tensor(f"ps{i}", [P, 512], F32) for i in range(8)]

    def sem(name):
        return nc.alloc_semaphore(name)

    const_in, x_landed, rows_in, lam_landed, gate_in, wg_landed = (
        sem(n) for n in ("const_in", "x_landed", "rows_in", "lam_landed", "gate_in", "wg_landed"))
    raw_in = [sem(f"raw_in{i}") for i in range(RAW_LATE)]
    stage_in = [sem(f"stage_in{i}") for i in range(4)]
    zeroed = sem("zeroed")
    rows_turned, cols_ready, cs_ready, lam_dot, lam_exp = (
        sem(n) for n in ("rows_turned", "cols_ready", "cs_ready", "lam_dot", "lam_exp"))
    x_turned, hi_done, lo_done, chunk_used, evac_act, evac_dve = (
        sem(n) for n in ("x_turned", "hi_done", "lo_done", "chunk_used", "evac_act", "evac_dve"))
    ada_copied, ada_done, ada_ev, g_hi_done, g_ready, sum_done = (
        sem(n) for n in ("ada_copied", "ada_done", "ada_ev", "g_hi_done", "g_ready", "sum_done"))
    cs_lo_done = sem("cs_lo_done")
    gate_cols = sem("gate_cols")
    ln_mean, ln_cent, ln_sq, ln_sq_used, ln_std, ln_xn = (
        sem(n) for n in ("ln_mean", "ln_cent", "ln_sq", "ln_sq_used", "ln_std", "ln_xn"))
    cols_mod, u_hi_done, u_ready, h_ready = (sem(n) for n in ("cols_mod", "u_hi_done", "u_ready", "h_ready"))
    yf_ready, y_hi_done, y_ready = (sem(n) for n in ("yf_ready", "y_hi_done", "y_ready"))
    v_turned, v_placed, rot_done, rope_done = (sem(n) for n in ("v_turned", "v_placed", "rot_done", "rope_done"))
    wg_ready, mg_done, gate_act, gate_dve, gate_turn = (
        sem(n) for n in ("wg_ready", "mg_done", "gate_act", "gate_dve", "gate_turn"))
    ng_ready, s_ready, x_ready, e_ready, pw_ready = (
        sem(n) for n in ("ng_ready", "s_ready", "x_ready", "e_ready", "pw_ready"))
    num_ready, hsum_ready, h_turned, ht_ready = (sem(n) for n in ("num_ready", "hsum_ready", "h_turned", "ht_ready"))
    sc_ready, smax_ready, p_ready, wgt_ready, wgt_turned, wt_ready, o_ready, o_copied, o_sq = (
        sem(n) for n in ("sc_ready", "smax_ready", "p_ready", "wgt_ready", "wgt_turned", "wt_ready",
                         "o_ready", "o_copied", "o_sq"))
    o_std, o_scaled, o_turned, yda_f, yda_h, yda_ready = (
        sem(n) for n in ("o_std", "o_scaled", "o_turned", "yda_f", "yda_h", "yda_ready"))
    ada_summed = sem("ada_summed")
    z_part, z_sum, z_hi_done, z_ready = (sem(n) for n in ("z_part", "z_sum", "z_hi_done", "z_ready"))
    gate_abs = sem("gate_abs")
    out_turned, out_ready, out_done = (sem(n) for n in ("out_turned", "out_ready", "out_done"))
    dve_chain = sem("dve_chain")
    act_chain = sem("act_chain")

    def wait(eng, s, value):
        if isinstance(value, int) and value <= 0:
            return
        eng.wait_ge(s, value)

    def halves(t0):
        return [(0, slice(0, SEG)), (1, slice(SEG, TOK))] if t0 == 0 else [(1, slice(SEG, TOK))]

    def t0_of(layer, x_only=True):
        return SEG if layer == DEPTH - 1 and x_only else 0

    ups = (ffn1_up, ffn2_up)
    downs = (ffn1_down, ffn2_down)

    def norm_cols(n):
        if n == 0:
            return one_zero[:, 0, :], one_zero[:, 1, :]
        layer, i = (n - 1) // 3, (n - 1) % 3
        o = 72 + (layer * 3 + i) * KD
        return cols[:, 0, o:o + KD], cols[:, 1, o:o + KD]

    def next_mods(n):
        return (n // 3) * MODT + (n % 3) * 3 * KD

    def gate_mods(layer, i):
        return layer * MODT + (3 * i + 2) * KD

    def norm_t0(n):
        return SEG if n >= 5 else 0

    def norm_d(n):
        layer, i = (n - 1) // 3, (n - 1) % 3
        return BASES[layer, ("down0", "wo", "down1")[i]][2] + KD

    def run(eng, count, body, peel_first=False, peel_last=False):
        n = count - 1 if peel_last else count
        if peel_first:
            body(0)
        with eng.Fori(int(peel_first), n) as i:
            body(i)
        if peel_last:
            body(n)

    SCORE_BANK = (4, 0)

    def nth_out(layer, head, t):
        n = TT - t0_of(layer) // P
        return (HEADS * TT if layer else 0) + n * head + max(0, t - (TT - n))

    def attention_units(layer):
        tiles = range(t0_of(layer) // P, TT)
        return [(head, t, range(2 if t < 2 else 4)) for t in tiles for head in range(HEADS)], 16 * layer

    block = nc.Block()
    block.__enter__()

    @block.sync
    def _(sp):
        sp.dma_start(con[:, :], consts).then_inc(const_in, 16)
        for p_, a in enumerate((ctx, x)):
            sp.dma_start(x_in[:, 2 * p_:2 * p_ + 2, :], a[0].rearrange("(t p) d -> p t d", p=P)).then_inc(x_landed, 16)
        ada_v = w_ada.rearrange("l (k p) n -> l p k n", p=P)
        for b in range(4):
            for j in range(4):
                sp.dma_start(stage[:, 4 * b + j, :].rearrange("p (k n) -> p k n", k=2),
                             ada_v[0, :, 2 * j:2 * j + 2, b * BLOCK:(b + 1) * BLOCK]).then_inc(stage_in[b], 16)

        def load(place, src, kt_n):
            slot, _, split_before = place
            wait(sp, lo_done, split_before)
            sp.dma_start(raw_tiles(slot, kt_n), src).then_inc(raw_in[slot], 16)

        def ada_chunk(place, block, j, first_column):
            slot, _, split_before = place
            wait(sp, lo_done, split_before)
            sp.dma_start(raw[:, slot, :].rearrange("p (k n) -> p k n", k=2),
                         ada_v[block // ADA_BLOCKS, :, 2 * j:2 * j + 2, bass.ds(first_column, BLOCK)]
                         ).then_inc(raw_in[slot], 16)

        def columns(a, first, column):
            return a[:, :, first:][:, :, bass.ds(column, P)]

        def up(layer, f):
            base = BASES[layer, f"up{f}"][0]
            src = ups[f][layer].rearrange("(k p) n -> p k n", p=P)
            first, other = up_patterns(layer, f)
            block = ADA_OF.get((layer, f"up{f}"))

            def body_of(pattern):
                def body(i):
                    for c, (kind, q) in enumerate(pattern):
                        place = raw_place(base, c, i, len(pattern))
                        if kind == "a":
                            column = block % ADA_BLOCKS * BLOCK + BLOCK * i
                            column = column if isinstance(column, int) else sp.snap(column)
                            ada_chunk(place, block, q, column)
                        else:
                            load(place, columns(src, q // 2 * P + q % 2 * FH, 2 * i * P), KD)
                return body
            body_of(first)(0)
            with sp.Fori(1, CH_UP // 4) as i:
                body_of(other)(i)

        def down(layer, f):
            base = BASES[layer, f"down{f}"][0]
            src = downs[f][layer].rearrange("(k p) n -> p k n", p=P)

            def body(i):
                for e in range(2):
                    for q, ks in enumerate(DOWN_K):
                        load(raw_place(base, 4 * e + q, i, 8),
                             columns(src[:, ks[0]:ks[-1] + 1, :], e * P, 2 * i * P), len(ks))
            run(sp, KD // 2, body)

        def mixer(layer):
            base = BASES[layer, "proj"][0]
            src = w_in[layer].rearrange("(k p) n -> p k n", p=P)
            for step in ORDER:
                if step[0] == "ada":
                    block = ADA_OF[layer, "proj"] + step[1]
                    r = base + PLAN[step][0]
                    ada_chunk(raw_place(r, 0), block, step[2], block % ADA_BLOCKS * BLOCK)
                elif step[0] in EVAC_ENGINE:
                    r = base + PLAN[step][0]
                    col = in_col(SEC[step[0]] + step[1])
                    load(raw_place(r, 0), src[:, :, col:col + P], KD)
            base = BASES[layer, "gate"][0]
            pattern = gate_pattern(layer)
            block = ADA_OF.get((layer, "gate"))

            def body(i):
                after = sp.snap(i + 1)
                if block is not None:
                    ada_column = sp.snap(block % ADA_BLOCKS * BLOCK + BLOCK * i)
                for c, (kind, q) in enumerate(pattern):
                    place, e = raw_place(base, c, i, len(pattern)), q // 6
                    if kind == "a":
                        ada_chunk(place, block, q, ada_column)
                    elif q % 2 == 0:
                        first = e * P + in_col(SEC[("gs", "gm", "gd")[(q // 2) % 3]])
                        load(place, columns(src, first, 2 * i * P), KD)
                    else:
                        w, kn = ((w_sc, 4), (w_ml, 8), (w_da, 4))[(q // 2) % 3]
                        load(place, columns(w[layer].rearrange("(k p) n -> p k n", p=P), e * P, 2 * P * after - 2 * P), kn)
            if base == LATE:
                sp.wait_ge(lo_done, LATE)
                sp.wait_ge(h_ready, KD * 5)
            run(sp, KD // 2, body)
            base = BASES[layer, "wo"][0]
            srco = w_o[layer].rearrange("(k p) n -> p k n", p=P)

            def body_o(i):
                for e in range(4):
                    load(raw_place(base, e, i, 4), columns(srco, e * P, 4 * i * P), KD)
            run(sp, KD // 4, body_o)

        for layer in range(DEPTH):
            up(layer, 0)
            wait(sp, chunk_used, BASES[layer, "up0"][0])
            sp.dma_start(wg_in[:, :, :], w_in[layer, :, MG_COL:MG_COL + 16].rearrange("(k p) n -> p k n", p=P)
                         ).then_inc(wg_landed, 16)
            down(layer, 0)
            mixer(layer)
            up(layer, 1)
            down(layer, 1)
        for q in range(2):
            for s in range(2):
                sp.wait_ge(out_ready, 2 * q + s + 1)
                sp.dma_start(out[0, s * P:(s + 1) * P, q * 512:(q + 1) * 512], y_out[:, s, q * 512:(q + 1) * 512]
                             ).then_inc(out_done, 16)
        sp.wait_ge(out_done, 64)

    @block.tensor
    def _(pe):
        pe.wait_ge(const_in, 16)
        pe.wait_ge(rows_in, 16 * 12)
        for n, r in enumerate((120, 120, 108, 78)):
            pe.transpose(ps[4 + n][:, 0:r], rows[0:r, n, :], ident[0:r, 0:r]).then_inc(rows_turned, 1)
        pe.wait_ge(x_landed, 32)
        for d in range(KD):
            if d >= 4:
                pe.wait_ge(evac_act if d % 2 == 0 else evac_dve, (d - 4) // 2 + 1)
            for t in range(TT):
                m = pe.transpose(ps[d % 4][:, t * P:(t + 1) * P], x_in[:, t, d * P:(d + 1) * P], ident)
            m.then_inc(x_turned, 1)

        def ada_turn(block, bank, rows_n, pick):
            pe.wait_ge(ada_copied, block + 1)
            for t in range(4):
                m = pe.matmul(ps[bank][:, 2 * t:2 * t + 2], ada_row[0:rows_n, t * P:(t + 1) * P], pick,
                              start=True, stop=True)
            m.then_inc(ada_done, 1)

        pe.wait_ge(cs_ready, 1)
        pe.wait_ge(cols_ready, 4)
        for b in range(4):
            pe.wait_ge(stage_in[b], 64)
            for k in range(KD):
                m = pe.matmul(ps[4 + b][0:2, :], cs[:, k, :], stage[:, 4 * b + k // 2, (k % 2) * BLOCK:(k % 2 + 1) * BLOCK],
                              start=(k == 0), stop=(k == KD - 1))
            m.then_inc(ada_summed, 1)
            if b == 0:
                pe.wait_ge(evac_act, 4)
                pe.wait_ge(evac_dve, 4)
            if b:
                ada_turn(b - 1, b - 1, 2, ident[0:2, 0:2])
        ada_turn(3, 3, 2, ident[0:2, 0:2])

        def ada_chunk(r, slot, block, j):
            pe.wait_ge(lo_done, r + 1)
            if j == 0:
                pe.wait_ge(ada_copied, block)
            for e in range(2):
                stationary = cs_parts[:, 2 * j + e, :]
                for part in (w_hi, w_lo):
                    m = pe.matmul(ps[4][0:4, :], stationary, part[:, slot, e * BLOCK:(e + 1) * BLOCK],
                                  start=(j == 0 and e == 0 and part is w_hi), stop=(j == 3 and e == 1 and part is w_lo))
            m.then_inc(chunk_used, 1)

        def ada_columns(block):
            pe.wait_ge(ada_ev, block)
            ada_turn(block, 5, 4, ada_sum)

        def chunk(r, slot, bank, parts, t0, done=True, first=True, last=True):
            pe.wait_ge(lo_done, r + 1)
            for n, (a_hi, a_lo) in enumerate(parts):
                wh, wl = w_hi[:, slot, n * P:(n + 1) * P], w_lo[:, slot, n * P:(n + 1) * P]
                a, b = first and n == 0, last and n == len(parts) - 1
                pe.matmul(ps[bank][:, t0:TOK], wh, a_hi, start=a, stop=False)
                pe.matmul(ps[bank][:, t0:TOK], wh, a_lo, start=False, stop=False)
                m = pe.matmul(ps[bank][:, t0:TOK], wl, a_hi, start=False, stop=b)
            m.then_inc(chunk_used, 1)

        def of(hi, lo, ks, t0):
            return [(hi[:, k, t0:TOK], lo[:, k, t0:TOK]) for k in ks]

        def interleaved(base, n, t0, before=None):
            pe.wait_ge(lo_done, base + 4)
            for k in range(KD):
                pe.wait_ge(u_ready, KD * n + k + 1)
                for q in range(4):
                    wh, wl = (w[:, (base + q) % SPLIT, k * P:(k + 1) * P] for w in (w_hi, w_lo))
                    pe.matmul(ps[q][:, t0:TOK], wh, u_hi[:, k, t0:TOK], start=(k == 0), stop=False)
                    pe.matmul(ps[q][:, t0:TOK], wh, u_lo[:, k, t0:TOK], start=False, stop=False)
                    m = pe.matmul(ps[q][:, t0:TOK], wl, u_hi[:, k, t0:TOK], start=False, stop=(k == KD - 1))
                    if k == KD - 1:
                        m.then_inc(chunk_used, 1)

        def up(layer, f, n):
            base, a0, d0 = BASES[layer, f"up{f}"]
            t0 = t0_of(layer) if f else 0
            if n == 0:
                pe.wait_ge(cs_lo_done, 1)
            first, other = up_patterns(layer, f)
            block = ADA_OF.get((layer, f"up{f}"))
            pe.wait_ge(evac_act, a0)
            pe.wait_ge(evac_dve, d0)
            interleaved(base, n, t0)
            if block is not None:
                for j in range(4):
                    ada_chunk(base + 4 + j, (base + 4 + j) % SPLIT, block, j)

            with pe.Fori(1, CH_UP // 4) as i:
                for c, (kind, q) in enumerate(other):
                    r = base + c + len(other) * i
                    slot = (base + c) % SPLIT
                    if kind == "a":
                        if q == 0:
                            ada_columns(block - 1 + i)
                        ada_chunk(r, slot, block + i, q)
                        continue
                    pe.wait_ge(evac_act if q % 2 == 0 else evac_dve, (a0 if q % 2 == 0 else d0) - 1 + 2 * i + q // 2)
                    chunk(r, slot, q, of(u_hi, u_lo, range(KD), t0), t0)
            if block is not None:
                ada_columns(block + CH_UP // 4 - 1)

        def down(layer, f):
            base, a0, d0 = BASES[layer, f"down{f}"]
            t0 = t0_of(layer) if f else 0
            pe.wait_ge(g_ready, KF * (2 * layer + f + 1))
            pe.wait_ge(evac_act, a0)
            pe.wait_ge(evac_dve, d0)

            def body(i):
                for e in range(2):
                    pe.wait_ge(evac_dve, d0 - 1 + 2 * i + e)
                    for q, ks in enumerate(DOWN_K):
                        chunk(base + 8 * i + 4 * e + q, (base + 4 * e + q) % SPLIT, e,
                              of(g_hi, g_lo, ks, t0), t0, first=(q == 0), last=(q == 3))
            run(pe, KD // 2, body)

        def norm(n):
            t0 = norm_t0(n)
            k0 = KD * (n - 1)
            pe.wait_ge(sum_done, KD * n)
            pe.matmul(ps[6][:, t0:TOK], mean_w, scr[5][:, t0:TOK], start=True, stop=True).then_inc(ln_mean, 1)
            for k in range(KD):
                pe.wait_ge(ln_sq, k0 + k + 1)
                pe.matmul(ps[7][:, t0:TOK], mean_w, scr[k % 2][:, t0:TOK], start=(k == 0),
                          stop=(k == KD - 1)).then_inc(ln_sq_used, 1)

        def proj(layer, step):
            r, n, _, _, _ = PLAN[step]
            base, a0, d0 = BASES[layer, "proj"]
            t0 = t0_of(layer, step[0] in X_ONLY)
            if n >= 4:
                before = NTH_PROJ[n - 4]
                by = EVAC_ENGINE[before[0]]
                _, _, a, d, _ = PLAN[before]
                pe.wait_ge(evac_act if by == "act" else evac_dve, (a0 + a if by == "act" else d0 + d) + 1)
                chunk(base + r, (base + r) % SPLIT, n % 4, of(u_hi, u_lo, range(KD), t0), t0)
            elif n == 3:
                interleaved(base, 3 * layer + 1, t0)

        def turn_v(layer, v):
            kind, i = ("mv", v) if v < 8 else ("dv", v - 8)
            pe.wait_ge(evac_act, BASES[layer, "proj"][1] + PLAN[kind, i][2] + 1)
            g = 12 * layer + v
            wait(pe, v_placed, g - 1)
            if v == 0:
                pe.wait_ge(ada_ev, ADA_OF[layer, "proj"] + 1)
            if v == 8:
                pe.wait_ge(ht_ready, HEADS * (layer + 1))
            for t in range(TT):
                m = pe.transpose(ps[4 + v % 2][:, t * P:(t + 1) * P], scr[4 + v % 2][:, t * P:(t + 1) * P], ident)
            m.then_inc(v_turned, 1)

        def rope(layer, i):
            kind = ("dq", i) if i < 4 else ("dk", i - 4)
            pe.wait_ge(evac_act, BASES[layer, "proj"][1] + PLAN[kind][2] + 1)
            wait(pe, rope_done, 8 * layer + i - 1)
            pe.matmul(ps[6 + i % 2][:, 0:SEG], rot_w, dqk[:, i, SEG:TOK], start=True, stop=True
                      ).then_inc(rot_done, 1)

        def gates(layer):
            pe.wait_ge(wg_ready, layer + 1)
            for n, a in enumerate((u_hi, u_lo)):
                for k in range(KD):
                    m = pe.matmul(ps[6][:, :], wg[:, k, :], a[:, k, :].bitcast(F32),
                                  start=(n == 0 and k == 0), stop=(n == 1 and k == KD - 1))
            m.then_inc(mg_done, 1)

        def gates_turn(layer):
            pe.wait_ge(gate_dve, layer + 1)
            for t in range(TT):
                m = pe.transpose(ps[7][:, t * P:(t + 1) * P], gt[0][:, t * P:(t + 1) * P], ident)
            m.then_inc(gate_turn, 1)

        def ml_scores(layer, head, s):
            t0 = t0_of(layer)
            u = HEADS * layer + head
            if s == 0:
                pe.wait_ge(v_placed, 12 * layer + 8)
                pe.wait_ge(gate_act, 5 * layer + 5)
                wait(pe, ht_ready, u)
                for n in range(2):
                    row = 32 * n + head
                    m = pe.matmul(ps[4 + n][:, t0:TOK], ident[0:64, row:row + 1].to_broadcast([64, P]),
                                  neg_g[0:64, t0:TOK], start=True, stop=True)
                m.then_inc(ng_ready, 1)
                base, a0, d0 = BASES[layer, "proj"]
                pe.wait_ge(evac_act, a0 + PLAN["mq", head][2] + 1)
                pe.wait_ge(evac_dve, d0 + PLAN["mk", head][3] + 1)
                wait(pe, hsum_ready, nth_out(layer, head, 0))
            else:
                if s >= 2:
                    pe.wait_ge(pw_ready, 8 * u + 2 * (s - 1))
            ts = max(t0, SEG if s >= 2 else 0)
            pe.matmul(ps[6 + s % 2][:, ts:TOK], kt[:, head, s * P:(s + 1) * P], qt[:, head, ts:TOK],
                      start=True, stop=True).then_inc(s_ready, 1)

        def turn_h(layer, head, t):
            nt = nth_out(layer, head, t)
            pe.wait_ge(hsum_ready, nt + 1)
            for e in range(2):
                m = pe.transpose(ps[4 + e][:, t * P:(t + 1) * P], hs[:, t % 2, e * P:(e + 1) * P], ident)
            m.then_inc(h_turned, 1)

        def ml_numerator(layer, head, t):
            first = t0_of(layer) // P
            if t < first:
                return
            u = HEADS * layer + head
            pe.wait_ge(pw_ready, 8 * (u + 1))
            if t > first:
                pe.wait_ge(hsum_ready, nth_out(layer, head, t))
            for n, w in enumerate("fb"):
                keys = KEYS[w, t]
                for s in keys:
                    m = pe.matmul(ps[6 + n][:, 0:257], pw[:, n, s, t * P:(t + 1) * P], vaug[:, s, head, :],
                                  start=(s == keys[0]), stop=(s == keys[-1]))
            m.then_inc(num_ready, 1)
            if t > first:
                turn_h(layer, head, t - 1)

        def attend(layer):
            tiles = range(t0_of(layer) // P, TT)
            pe.wait_ge(v_placed, 12 * (layer + 1))
            pe.wait_ge(rope_done, 8 * (layer + 1))
            base, a0, d0 = BASES[layer, "gate"]
            pe.wait_ge(evac_act, a0)
            pe.wait_ge(evac_dve, d0)
            pe.wait_ge(ada_ev, ADA_OF[layer, "proj"] + 3)
            units, u0 = attention_units(layer)

            def scores(v):
                head, t, keys = units[v]
                wait(pe, p_ready, 2 * (u0 + v - 1) if v >= 2 else 0)
                for j in range(2):
                    rows_ = slice(j * DA_HALF, (j + 1) * DA_HALF)
                    pe.matmul(ps[SCORE_BANK[v % 2] + j][:, 0:len(keys) * P], dqk[rows_, head, t * P:(t + 1) * P],
                              dqk[rows_, 4 + head, 0:len(keys) * P], start=True, stop=True).then_inc(sc_ready, 1)

            def turn_weights(v):
                head, t, keys = units[v]
                pe.wait_ge(wgt_ready, u0 + v + 1)
                wait(pe, wt_ready, u0 + v - 1 if v >= 2 else 0)
                for k in keys:
                    m = pe.transpose(ps[6 - 4 * (v % 2)][:, k * P:(k + 1) * P], wgt[v % 2][:, k * P:(k + 1) * P], ident)
                m.then_inc(wgt_turned, 1)

            def outputs(v):
                head, t, keys = units[v]
                pe.wait_ge(wt_ready, u0 + v + 1)
                wait(pe, o_copied, u0 + v - 1 if v >= 2 else 0)
                for k in keys:
                    m = pe.matmul(ps[7 - 4 * (v % 2)][:, 0:P], wgt_t[v % 2][:, k * P:(k + 1) * P], dav[:, k, head, :],
                                  start=(k == keys[0]), stop=(k == keys[-1]))
                m.then_inc(o_ready, 1)
            scores(0)
            for v in range(len(units)):
                if v + 1 < len(units):
                    scores(v + 1)
                turn_weights(v)
                if v:
                    outputs(v - 1)
            outputs(len(units) - 1)
            pe.wait_ge(o_scaled, layer + 1)
            for head in range(HEADS):
                wait(pe, yda_f, 4 * layer + head - 1)
                for t in tiles:
                    m = pe.transpose(ps[4 + head % 2][:, t * P:(t + 1) * P], oda[:, t, head, :], ident)
                m.then_inc(o_turned, 1)

        def mixer(layer):
            t0 = t0_of(layer)
            pe.wait_ge(evac_dve, BASES[layer, "proj"][2])
            for step in ORDER:
                if step[0] in EVAC_ENGINE:
                    proj(layer, step)
                elif step[0] == "ada":
                    r = BASES[layer, "proj"][0] + PLAN[step][0]
                    ada_chunk(r, r % SPLIT, ADA_OF[layer, "proj"] + step[1], step[2])
                elif step[0] == "adat":
                    ada_columns(ADA_OF[layer, "proj"] + step[1])
                elif step[0] == "attend":
                    attend(layer)
                elif step[0] == "gates":
                    gates(layer)
                elif step[0] == "ml_gates":
                    gates_turn(layer)
                elif step[0] == "ml_t":
                    turn_h(layer, step[1], TT - 1)
                elif step[0] in ("ml_s", "ml_n"):
                    (ml_scores if step[0] == "ml_s" else ml_numerator)(layer, *step[1:])
                else:
                    {"turn_v": turn_v, "rope": rope}[step[0]](layer, step[1])
            base, a0, d0 = BASES[layer, "gate"]
            pe.wait_ge(evac_act, a0)
            pe.wait_ge(evac_dve, d0)
            pe.wait_ge(y_ready, 12 * (layer + 1))
            pattern = gate_pattern(layer)
            block = ADA_OF.get((layer, "gate"))

            def body(i):
                for c, (kind, q) in enumerate(pattern):
                    if kind == "a":
                        if q == 0:
                            pe.wait_ge(yda_f, 4 * (layer + 1))
                        ada_chunk(base + c + len(pattern) * i, (base + c) % SPLIT, block + i, q)
                        continue
                    if q == 5:
                        pe.wait_ge(yda_ready, 4 * (layer + 1))
                    pe.wait_ge(evac_act if q % 2 == 0 else evac_dve, (a0 if q % 2 == 0 else d0) - 1 + 6 * i + q // 2)
                    if q % 2 == 0:
                        parts = of(u_hi, u_lo, range(KD), t0)
                    else:
                        hi, lo, kn = ((ysc_hi, ysc_lo, 4), (yml_hi, yml_lo, 8), (yda_hi, yda_lo, 4))[(q // 2) % 3]
                        parts = of(hi, lo, range(kn), t0)
                    chunk(base + c + len(pattern) * i, (base + c) % SPLIT, q % 4, parts, t0)
                if block is not None:
                    ada_columns(block + i)
            run(pe, KD // 2, body)
            base, a0, d0 = BASES[layer, "wo"]
            pe.wait_ge(z_ready, KD * (layer + 1))
            pe.wait_ge(evac_act, a0)
            pe.wait_ge(evac_dve, d0)

            def body_o(i):
                for e in range(4):
                    pe.wait_ge(evac_dve, d0 - 3 + 4 * i + e)
                    chunk(base + 4 * i + e, (base + e) % SPLIT, e, of(z_hi, z_lo, range(KD), t0), t0)
            run(pe, KD // 4, body_o)

        for layer in range(DEPTH):
            up(layer, 0, 3 * layer)
            down(layer, 0)
            norm(3 * layer + 1)
            mixer(layer)
            norm(3 * layer + 2)
            up(layer, 1, 3 * layer + 2)
            down(layer, 1)
            norm(3 * layer + 3)
        for q in range(2):
            pe.wait_ge(h_ready, KD * 6 + 4 * (q + 1))
            for s in range(2):
                n = 2 * q + s
                for k in range(4):
                    m = pe.transpose(ps[n][:, k * P:(k + 1) * P], h[:, 4 * q + k, SEG + s * P:SEG + (s + 1) * P], ident)
                m.then_inc(out_turned, 1)

    @block.scalar
    def _(act):
        chain = [0]

        def link(ins):
            chain[0] += 1
            ins.then_inc(act_chain, 1)
            act.wait_ge(act_chain, chain[0])

        def split(r, slot, place):
            wait(act, chunk_used, r - SPLIT + 1)
            raw_slot, landed, _ = place
            act.wait_ge(raw_in[raw_slot], landed)
            act.activation(split_tiles(w_hi, slot), raw_tiles(raw_slot), ACT.Copy).then_inc(hi_done, 1)

        def ahead(base, c, i=0, step=0):
            r = base + c + SPLIT
            if isinstance(i, int) and r + step * i >= CHUNKS:
                return
            split(r + step * i, r % SPLIT, raw_place(base, c + SPLIT, i, step))

        def turn(a, tile, r0, n):
            act.dma_start(rows[r0:r0 + n, tile, :], a).then_inc(rows_in, 16)

        def as_rows(a):
            return a.rearrange("(r p) -> r p", p=P)
        turn(as_rows(c_ctx), 3, 60, 8)
        turn(c.rearrange("a (r p) -> (a r) p", p=P), 3, 68, 8)
        for layer in range(DEPTH):
            turn(as_rows(b_ada[layer]), layer, 0, 72)
            turn(as_rows(b_in[layer, 0:MG_COL]), 2, 72 * layer, 36)
            turn(as_rows(b_in[layer, MG_COL + 16:N_IN]), *((2, 36) if layer == 0 else (3, 0)), 36)
        turn(ln_g.rearrange("l i (r p) -> (l i r) p", p=P), 0, 72, 48)
        turn(ln_b.rearrange("l i (r p) -> (l i r) p", p=P), 1, 72, 48)
        turn(conv_w.rearrange("l t (r p) -> (l t r) p", p=P), 3, 36, 24)
        turn(da_norm_g, 3, 76, 2)
        for n, a in enumerate((lam_q1, lam_k1, lam_q2, lam_k2)):
            act.dma_start(lam_in[:, :, n, :], a.rearrange("l d -> (l d)").partition_broadcast(P)
                          .rearrange("p (l d) -> p l d", l=DEPTH)).then_inc(lam_landed, 16)
        act.wait_ge(zeroed, 2)
        for layer in range(DEPTH):
            for q in range(4):
                act.dma_start(gate_bias[32 * q:32 * q + 4, layer:layer + 1],
                              b_in[layer, MG_COL + 4 * q:MG_COL + 4 * q + 4].rearrange("(p a) -> p a", a=1)
                              ).then_inc(gate_in, 16)
        act.wait_ge(cols_ready, 4)
        act.activation(cs[:, :, 0], cols[:, 3, 60:68], ACT.Silu)
        link(act.activation(cs[:, :, 1], cols[:, 3, 68:76], ACT.Silu))
        act.activation(cs_parts[:, :, 0:2], cs[:, :, :], ACT.Copy).then_inc(cs_ready, 1)
        act.wait_ge(lam_dot, 1)
        act.activation(lam_e[:, :, :], lam_e[:, :, :], ACT.Exp).then_inc(lam_exp, 1)
        for d in range(0, KD, 2):
            act.wait_ge(x_turned, d + 1)
            act.activation(h[:, d, :], ps[d % 4][:, :], ACT.Copy).then_inc(evac_act, 1)
        for r in range(SPLIT):
            split(r, r, raw_place(r, 0))

        def modulate(n):
            t0 = norm_t0(n)
            act.wait_ge(cols_mod, n + 1)
            if n == 0:
                act.wait_ge(evac_act, 4)
                act.wait_ge(evac_dve, 4)
            last = None
            for k in range(KD + 1):
                if k < KD and n < 6:
                    if n:
                        act.wait_ge(ln_xn, KD * (n - 1) + k + 1)
                    for s, seg in halves(t0):
                        m = act.activation(u_hi[:, k, seg], h[:, k, seg], ACT.Identity,
                                           scale=mod_a[:, k, s:s + 1], bias=mod_b[:, k, s:s + 1])
                    m.then_inc(u_hi_done, 1)
                j = k - 1 if n < 6 else k
                if 0 <= j < KD:
                    if n < 6:
                        act.wait_ge(u_ready, KD * n + j + 1)
                    else:
                        act.wait_ge(ln_xn, KD * (n - 1) + j + 1)
                    act.activation(h[:, j, t0:TOK], h[:, j, t0:TOK], ACT.Identity, scale=res_g[:, j:j + 1],
                                   bias=res_b[:, j:j + 1]).then_inc(h_ready, 1)

        def norm(n):
            t0 = norm_t0(n)
            k0 = KD * (n - 1)
            act.activation(small[:, 15:16], small[:, 0:1], ACT.Sqrt)
            for k in range(KD):
                act.wait_ge(ln_cent, k0 + k + 1)
                wait(act, ln_sq_used, k0 + k - 1)
                act.activation(scr[k % 2][:, t0:TOK], h[:, k, t0:TOK], ACT.Square).then_inc(ln_sq, 1)
            act.wait_ge(ln_sq_used, k0 + KD)
            act.activation(scr[2][:, t0:TOK], ps[7][:, t0:TOK], ACT.Sqrt, bias=small[:, 0:1]).then_inc(ln_std, 1)
            modulate(n)

        def up(layer, f):
            base, a0, d0 = BASES[layer, f"up{f}"]
            g0 = KF * (2 * layer + f)
            t0 = t0_of(layer) if f else 0

            first, other = up_patterns(layer, f)

            def body_of(pattern):
                def body(i):
                    for c, (kind, q) in enumerate(pattern):
                        ahead(base, c, i, len(pattern))
                        if kind == "a":
                            continue
                        act.wait_ge(chunk_used, base + c + 1 + len(pattern) * i)
                        if q % 2 == 0:
                            act.wait_ge(evac_dve, d0 - 1 + 2 * i + q // 2)
                            act.activation(scr[q // 2][:, t0:TOK], ps[q][:, t0:TOK], ACT.Silu).then_inc(evac_act, 1)
                        else:
                            act.wait_ge(evac_dve, d0 + 1 + 2 * i + q // 2)
                            act.activation(g_hi[:, 2 * i + q // 2, t0:TOK], scr[2 + q // 2][:, t0:TOK], ACT.Copy
                                           ).then_inc(g_hi_done, 1)
                return body
            body_of(first)(0)
            with act.Fori(1, CH_UP // 4) as i:
                body_of(other)(i)

        def down(layer, f):
            base = BASES[layer, f"down{f}"][0]

            def body(i):
                for q in range(8):
                    ahead(base, q, i, 8)
            run(act, KD // 2, body, peel_last=(layer, f) == (DEPTH - 1, 1))

        def split_y(y, hi, k, t0):
            act.wait_ge(yf_ready, y + 1)
            act.activation(hi[:, k, t0:TOK], scr[2 + y % 2][:, t0:TOK], ACT.Copy).then_inc(y_hi_done, 1)

        def proj(layer, step):
            kind, i = step
            base, a0, d0 = BASES[layer, "proj"]
            r, n, a, d, y = PLAN[step]
            t0 = t0_of(layer, kind in X_ONLY)
            ahead(base, r)
            if kind in ("sx", "mk"):
                return
            y += 12 * layer
            if kind == "sb":
                split_y(y, ysc_hi, i, t0)
                return
            act.wait_ge(chunk_used, base + r + 1)
            ct, cc = bias_at(layer, SEC[kind] + i)
            bias = cols[:, ct, cc:cc + 1]
            if kind == "cg":
                dst, func = cgt[:, t0:TOK], ACT.Identity
                if i:
                    act.wait_ge(evac_dve, d0 + PLAN["sx", i - 1][3] + 1)
            elif kind == "mq":
                dst, func = qt[:, i, t0:TOK], ACT.Identity
            elif kind in ("mv", "dv"):
                v = i if kind == "mv" else 8 + i
                wait(act, v_turned, 12 * layer + v - 1)
                dst, func = scr[4 + v % 2][:, t0:TOK], ACT.Identity
            elif kind == "mo":
                dst, func = scr[i % 2][:, t0:TOK], ACT.Sigmoid
                if i >= 2:
                    act.wait_ge(yf_ready, y - 1)
            else:
                if kind == "dq" and i == 0:
                    act.wait_ge(ht_ready, HEADS * (layer + 1))
                dst, func = dqk[:, i if kind == "dq" else 4 + i, t0:TOK], ACT.Identity
            act.activation(dst, ps[n % 4][:, t0:TOK], func, bias=bias).then_inc(evac_act, 1)
            if kind == "mo":
                split_y(y, yml_hi, i, t0)

        def gates(layer):
            act.wait_ge(mg_done, layer + 1)
            act.wait_ge(gate_in, 16 * 4 * DEPTH)
            act.activation(gt[1][:, :], ps[6][:, :], ACT.Identity, bias=gate_bias[:, layer:layer + 1]
                           ).then_inc(gate_act, 1)
            act.wait_ge(gate_abs, layer + 1)
            link(act.activation(gt[3][64:128, :], gt[3][64:128, :], ACT.Exp, scale=-1.0))
            act.activation(gt[3][64:128, :], gt[3][64:128, :], ACT.Ln, bias=1.0).then_inc(gate_act, 1)

        def ml_gates(layer):
            act.wait_ge(gate_turn, layer + 1)
            turned = ps[7][:, :].rearrange("p (t n) -> p t n", t=TT)
            act.activation(am[:, :, :], turned, ACT.Copy).then_inc(gate_act, 1)
            act.activation(nam[:, :, :], turned[:, :, 0:64], ACT.Copy, scale=-1.0).then_inc(gate_act, 1)
            act.activation(em[:, :, :], turned[:, :, 64:128], ACT.Exp, scale=-1.0).then_inc(gate_act, 1)

        def ml_scores(layer, head, s):
            t0 = t0_of(layer)
            u = HEADS * layer + head
            if s == 0:
                act.wait_ge(ng_ready, u + 1)
                if head == 0:
                    act.wait_ge(gate_act, 5 * layer + 5)
            for n in range(2):
                v = 2 * s + n
                row = 32 * n + head
                found, diag = segments(s, n, t0)
                wait(act, pw_ready, 8 * u + v - 1 if v >= 2 else 8 * u)
                for b, e in found:
                    cuts = [(b, e)]
                    if diag is not None and b <= diag * P < e:
                        own = slice(diag * P, (diag + 1) * P)
                        link(act.activation(xt[:, n, own], ps[4 + n][:, own], ACT.Relu, scale=-1.0,
                                            bias=nam[:, s, row:row + 1]))
                        m = act.activation(xt[:, n, own], xt[:, n, own], ACT.Exp, scale=-1.0)
                        cuts = [(b, diag * P), ((diag + 1) * P, e)]
                    for cb, ce in cuts:
                        if cb < ce:
                            m = act.activation(xt[:, n, cb:ce], ps[4 + n][:, cb:ce], ACT.Exp,
                                               bias=am[:, s, row:row + 1])
                m.then_inc(e_ready, 1)

        def ml_turned(layer, head):
            t0 = t0_of(layer)
            act.wait_ge(h_turned, nth_out(layer, head, TT - 1) + 1)
            for e in range(2):
                m = act.activation(ht[:, 2 * head + e, t0:TOK], ps[4 + e][:, t0:TOK], ACT.Copy)
            m.then_inc(ht_ready, 1)

        def attend(layer):
            units, u0 = attention_units(layer)

            def probabilities(v):
                nk = len(units[v][2]) * P
                for j in range(2):
                    act.wait_ge(smax_ready, 2 * (u0 + v) + j + 1)
                    if j == 0 and v >= 2:
                        act.wait_ge(wgt_ready, u0 + v - 1)
                    act.activation(scr[2 * (v % 2) + j][:, 0:nk], ps[SCORE_BANK[v % 2] + j][:, 0:nk], ACT.Exp,
                                   scale=DA_HALF ** -0.5, bias=att[:, v % 2, j:j + 1],
                                   accum_out=att[:, v % 2, 2 + j:3 + j]).then_inc(p_ready, 1)

            def weights(v):
                nk = len(units[v][2]) * P
                act.wait_ge(wgt_turned, u0 + v + 1)
                if v >= 2:
                    act.wait_ge(o_ready, u0 + v - 1)
                act.activation(wgt_t[v % 2][:, 0:nk], ps[6 - 4 * (v % 2)][:, 0:nk], ACT.Copy).then_inc(wt_ready, 1)

            def squares(v):
                head, t, _ = units[v]
                act.wait_ge(o_copied, u0 + v + 1)
                wait(act, o_sq, u0 + v)
                act.activation(junk[:, :], oda[:, t, head, :], ACT.Square, accum_out=ssq[:, t, head:head + 1]
                               ).then_inc(o_sq, 1)
            probabilities(0)
            for v in range(len(units)):
                if v + 1 < len(units):
                    probabilities(v + 1)
                weights(v)
                if v:
                    squares(v - 1)
            squares(len(units) - 1)
            first = t0_of(layer) // P
            act.wait_ge(o_sq, u0 + len(units))
            act.activation(ssq[:, first:TT, :], ssq[:, first:TT, :], ACT.Sqrt, scale=1.0 / P, bias=small[:, 0:1]
                           ).then_inc(o_std, 1)
            for head in range(HEADS):
                act.wait_ge(yda_f, 4 * layer + head + 1)
                act.activation(yda_hi[:, head, first * P:TOK], scr[2 + head % 2][:, first * P:TOK], ACT.Copy
                               ).then_inc(yda_h, 1)

        def mixer(layer):
            t0 = t0_of(layer)
            for step in ORDER:
                if step[0] in EVAC_ENGINE:
                    proj(layer, step)
                elif step[0] == "ada":
                    ahead(BASES[layer, "proj"][0], PLAN[step][0])
                elif step[0] == "gates":
                    gates(layer)
                elif step[0] == "ml_gates":
                    ml_gates(layer)
                elif step[0] == "ml_s":
                    ml_scores(layer, *step[1:])
                elif step[0] == "ml_t":
                    ml_turned(layer, step[1])
                elif step[0] == "attend":
                    attend(layer)
            base, a0, d0 = BASES[layer, "gate"]
            pattern = gate_pattern(layer)

            def body(i):
                for c, (kind, q) in enumerate(pattern):
                    ahead(base, c, i, len(pattern))
                    if kind == "a":
                        continue
                    if q % 2 == 0:
                        act.wait_ge(chunk_used, base + c + 1 + len(pattern) * i)
                        act.wait_ge(evac_dve, d0 - 1 + 6 * i + q // 2)
                        tile = SEC[("gs", "gm", "gd")[(q // 2) % 3]] + q // 6
                        ct, cc = bias_at(layer, tile)
                        act.activation(scr[(q // 2) % 2][:, t0:TOK], ps[q % 4][:, t0:TOK], ACT.Sigmoid,
                                       bias=cols[:, ct, bass.ds(cc + 2 * i, 1)]).then_inc(evac_act, 1)
                    elif q % 6 == 5:
                        act.wait_ge(z_sum, 2 * i + (KD * layer + q // 6 + 1))
                        act.activation(z_hi[:, 2 * i + q // 6, t0:TOK], scr[2 + q // 6][:, t0:TOK], ACT.Copy
                                       ).then_inc(z_hi_done, 1)
            run(act, KD // 2, body)
            base = BASES[layer, "wo"][0]

            def body_o(i):
                for e in range(4):
                    ahead(base, e, i, 4)
            run(act, KD // 4, body_o)

        modulate(0)
        for layer in range(DEPTH):
            up(layer, 0)
            down(layer, 0)
            norm(3 * layer + 1)
            mixer(layer)
            norm(3 * layer + 2)
            up(layer, 1)
            down(layer, 1)
            norm(3 * layer + 3)
        for q in range(2):
            for s in range(2):
                act.wait_ge(out_turned, 2 * q + s + 1)
                act.activation(y_out[:, s, q * 512:(q + 1) * 512], ps[2 * q + s][:, :], ACT.Copy
                               ).then_inc(out_ready, 1)

    @block.vector
    def _(dve):
        chain = [0]

        def link(ins):
            chain[0] += 1
            ins.then_inc(dve_chain, 1)
            dve.wait_ge(dve_chain, chain[0])

        def split(r, slot, place):
            dve.wait_ge(hi_done, r + 1)
            wait(dve, chunk_used, r - SPLIT + 1)
            dve.tensor_tensor(split_tiles(w_lo, slot), raw_tiles(place[0]), split_tiles(w_hi, slot).bitcast(F32), ALU.subtract
                              ).then_inc(lo_done, 1)

        def ahead(base, c, i=0, step=0):
            r = base + c + SPLIT
            if isinstance(i, int) and r + step * i >= CHUNKS:
                return
            split(r + step * i, r % SPLIT, raw_place(base, c + SPLIT, i, step))

        dve.memset(gate_bias[:, :], 0.0).then_inc(zeroed, 1)
        dve.memset(one_zero[:, 0, :], 1.0)
        dve.memset(one_zero[:, 1, :], 0.0)
        link(dve.memset(small[:, 0:1], EPS))
        dve.memset(small[:, 1:2], 0.0).then_inc(zeroed, 1)
        for n, r in enumerate((120, 120, 108, 78)):
            dve.wait_ge(rows_turned, n + 1)
            dve.tensor_copy(cols[:, n, 0:r], ps[4 + n][:, 0:r]).then_inc(cols_ready, 1)
        dve.wait_ge(lam_landed, 64)
        for layer in range(DEPTH):
            link(dve.tensor_tensor(lam_p[:, layer], lam_in[:, layer, 0:4:2, :], lam_in[:, layer, 1:4:2, :], ALU.mult))
        dve.tensor_reduce(lam_e[:, :, :], lam_p[:, :, :, :], AXX, ALU.add).then_inc(lam_dot, 1)
        dve.wait_ge(lam_exp, 1)
        for layer in range(DEPTH):
            lam_init = 0.8 - 0.6 * math.exp(-0.3 * layer)
            link(dve.tensor_tensor(neg_lam[:, layer:layer + 1], lam_e[:, layer, 1:2], lam_e[:, layer, 0:1], ALU.subtract))
            link(dve.tensor_scalar(neg_lam[:, layer:layer + 1], neg_lam[:, layer:layer + 1], -lam_init, None, ALU.add))
        for d in range(1, KD, 2):
            dve.wait_ge(x_turned, d + 1)
            dve.tensor_copy(h[:, d, :], ps[d % 4][:, :]).then_inc(evac_dve, 1)

        def ada_copy(block, bank, n):
            wait(dve, ada_done, block)
            dve.tensor_copy(ada_row[0:n, :], ps[bank][0:n, :]).then_inc(ada_copied, 1)

        def ada_add(block, bank, layer):
            dve.wait_ge(ada_done, block + 1)
            first = 4 * block - layer * MODT
            m0 = 4 * block
            if isinstance(block, int):
                bias, dst = cols[:, layer, first:first + 4], mods[:, m0:m0 + 4, :]
            else:
                bias, dst = cols[:, layer, bass.ds(first, 4)], mods[:, bass.ds(m0, 4), :]
            dve.tensor_tensor(dst, ps[bank][:, 0:8].rearrange("p (t s) -> p t s", s=2),
                              bias.unsqueeze(2).to_broadcast([P, 4, 2]), ALU.add).then_inc(ada_ev, 1)

        for b in range(4):
            dve.wait_ge(ada_summed, b + 1)
            ada_copy(b, 4 + b, 2)
            ada_add(b, b, 0)
        dve.wait_ge(cs_ready, 1)
        dve.tensor_tensor(cs_parts[:, :, 2:4], cs[:, :, :], cs_parts[:, :, 0:2].bitcast(F32), ALU.subtract
                          ).then_inc(cs_lo_done, 1)
        for r in range(SPLIT):
            split(r, r, raw_place(r, 0))

        def columns(n):
            g, b = norm_cols(n)
            if n == 6:
                dve.tensor_copy(res_g[:, :], g)
                link(dve.tensor_copy(res_b[:, :], b))
            else:
                m0 = next_mods(n)
                shift, scale = mods[:, m0:m0 + KD, :], mods[:, m0 + KD:m0 + 2 * KD, :]
                for s in range(2):
                    link(dve.scalar_tensor_tensor(mod_a[:, :, s], scale[:, :, s], 1.0, g, ALU.add, ALU.mult))
                    link(dve.scalar_tensor_tensor(mod_b[:, :, s], scale[:, :, s], 1.0, b, ALU.add, ALU.mult))
                    link(dve.tensor_tensor(mod_b[:, :, s], mod_b[:, :, s], shift[:, :, s], ALU.add))
                dve.tensor_scalar(res_g[:, :], g, ALPHA, None, ALU.mult)
                link(dve.tensor_scalar(res_b[:, :], b, ALPHA, None, ALU.mult))
            dve.engine_nop().then_inc(cols_mod, 1)

        def modulate(n):
            t0 = norm_t0(n)

            def normed(k):
                dve.tensor_tensor(h[:, k, t0:TOK], h[:, k, t0:TOK], scr[3][:, t0:TOK], ALU.mult).then_inc(ln_xn, 1)
            if n:
                normed(0)
            for k in range(KD):
                if n and k + 1 < KD:
                    normed(k + 1)
                if n == 6:
                    continue
                if n:
                    dve.wait_ge(ln_xn, KD * (n - 1) + k + 1)
                for s, seg in halves(t0):
                    m = dve.tensor_scalar(scr[4 + k % 2][:, seg], h[:, k, seg], mod_a[:, k, s:s + 1],
                                          mod_b[:, k, s:s + 1], ALU.mult, ALU.add)
                link(m)
                dve.wait_ge(u_hi_done, KD * n + k + 1)
                dve.tensor_tensor(u_lo[:, k, t0:TOK], scr[4 + k % 2][:, t0:TOK], u_hi[:, k, t0:TOK].bitcast(F32),
                                  ALU.subtract).then_inc(u_ready, 1)

        def norm(n):
            t0 = norm_t0(n)
            k0 = KD * (n - 1)
            columns(n)
            dve.wait_ge(ln_mean, n)
            for k in range(KD):
                dve.tensor_tensor(h[:, k, t0:TOK], h[:, k, t0:TOK], ps[6][:, t0:TOK], ALU.subtract
                                  ).then_inc(ln_cent, 1)
            dve.wait_ge(ln_std, n)
            link(dve.reciprocal(scr[3][:, t0:TOK], scr[2][:, t0:TOK]))
            modulate(n)

        def gate_columns(layer, i, factor):
            m0 = gate_mods(layer, i)
            dve.wait_ge(h_ready, KD * (3 * layer + i + 1))
            dve.tensor_scalar(gate[:, :, :], mods[:, m0:m0 + KD, :], factor, None, ALU.mult)
            link(dve.memset(scr[5][:, :], 0.0))

        def add_branch(tile, bank, t0, evac, total):
            for s, seg in halves(t0):
                m = dve.scalar_tensor_tensor(h[:, tile, seg], ps[bank][:, seg], gate[:, tile, s:s + 1],
                                             h[:, tile, seg], ALU.mult, ALU.add)
            m.then_inc(evac_dve, 1)
            dve.wait_ge(evac_dve, evac)
            wait(dve, sum_done, total)
            dve.tensor_tensor(scr[5][:, t0:TOK], scr[5][:, t0:TOK], h[:, tile, t0:TOK], ALU.add).then_inc(sum_done, 1)

        def up(layer, f):
            base, a0, d0 = BASES[layer, f"up{f}"]
            g0 = KF * (2 * layer + f)
            t0 = t0_of(layer) if f else 0
            first, other = up_patterns(layer, f)
            block = ADA_OF.get((layer, f"up{f}"))
            last = CH_UP // 4 - 1

            def body_of(pattern):
                def body(i):
                    for c, (kind, q) in enumerate(pattern):
                        ahead(base, c, i, len(pattern))
                        if kind == "a":
                            if pattern is other and q == 0:
                                ada_add(block - 1 + i, 5, block // ADA_BLOCKS)
                            if q == 3:
                                dve.wait_ge(chunk_used, base + c + 1 + len(pattern) * i)
                                ada_copy(block + i, 4, 4)
                        elif q % 2:
                            e = q // 2
                            dve.wait_ge(chunk_used, base + c + 1 + len(pattern) * i)
                            dve.wait_ge(evac_act, a0 + e + 1 + 2 * i)
                            dve.tensor_tensor(scr[2 + e][:, t0:TOK], scr[e][:, t0:TOK], ps[q][:, t0:TOK], ALU.mult
                                              ).then_inc(evac_dve, 1)
                            dve.wait_ge(g_hi_done, g0 + e + 1 + 2 * i)
                            dve.tensor_tensor(g_lo[:, 2 * i + e, t0:TOK], scr[2 + e][:, t0:TOK],
                                              g_hi[:, 2 * i + e, t0:TOK].bitcast(F32), ALU.subtract
                                              ).then_inc(g_ready, 1)
                return body
            body_of(first)(0)
            with dve.Fori(1, last + 1) as i:
                body_of(other)(i)
            if block is not None:
                ada_add(block + last, 5, block // ADA_BLOCKS)

        def gate_weights(layer):
            link(dve.memset(wg[:, :, :], 0.0))
            dve.wait_ge(wg_landed, 16 * (layer + 1))
            dve.tensor_copy(wg[:, :, :].rearrange("p k (q n) -> p k q n", q=4)[:, :, :, 0:4],
                            wg_in[:, :, :].rearrange("p k (q n) -> p k q n", q=4)).then_inc(wg_ready, 1)

        def down(layer, f):
            base, _, d0 = BASES[layer, f"down{f}"]
            t0 = t0_of(layer) if f else 0
            s0 = KD * (3 * layer + 2 * f)
            gate_columns(layer, 2 * f, 0.5)
            if f == 0:
                gate_weights(layer)

            def body(i):
                for e in range(2):
                    for q in range(4):
                        ahead(base, 4 * e + q, i, 8)
                    dve.wait_ge(chunk_used, base + 4 * e + 4 + 8 * i)
                    add_branch(2 * i + e, e, t0, d0 + e + 1 + 2 * i, s0 + e + 2 * i)
            run(dve, KD // 2, body, peel_first=(layer, f) == (0, 0), peel_last=(layer, f) == (DEPTH - 1, 1))

        def split_y(y, hi, lo, k, t0):
            dve.wait_ge(y_hi_done, y + 1)
            dve.tensor_tensor(lo[:, k, t0:TOK], scr[2 + y % 2][:, t0:TOK], hi[:, k, t0:TOK].bitcast(F32),
                              ALU.subtract).then_inc(y_ready, 1)

        def proj(layer, step):
            kind, i = step
            base, a0, d0 = BASES[layer, "proj"]
            r, n, a, d, y = PLAN[step]
            t0 = t0_of(layer, kind in X_ONLY)
            bank = ps[n % 4]
            ahead(base, r)
            y += 12 * layer
            ct, cc = bias_at(layer, SEC[kind] + i)
            bias = cols[:, ct, cc:cc + 1]
            if kind == "mk":
                dve.wait_ge(chunk_used, base + r + 1)
                dve.tensor_scalar(kt[:, i, :], bank[:, :], bias, DQK ** -0.5, ALU.add, ALU.mult).then_inc(evac_dve, 1)
            elif kind == "sx":
                dve.wait_ge(chunk_used, base + r + 1)
                dve.wait_ge(evac_act, a0 + PLAN["cg", i][2] + 1)
                if i == 0:
                    link(dve.memset(zpad[:, :, :], 0.0))
                for s, seg in halves(t0):
                    m = dve.scalar_tensor_tensor(zpad[:, s, 1:SEG + 1], bank[:, seg], bias, cgt[:, seg],
                                                 ALU.add, ALU.mult)
                m.then_inc(evac_dve, 1)
                dve.wait_ge(evac_dve, d0 + d + 1)
                tap = [cols[:, 3, 36 + 12 * layer + 4 * j + i:37 + 12 * layer + 4 * j + i] for j in range(3)]
                s0 = t0 // SEG
                z, o = zpad[:, s0:2, :], cv[:, t0:TOK].rearrange("p (s t) -> p s t", t=SEG)
                link(dve.tensor_scalar(o, z[:, :, 0:SEG], tap[0], None, ALU.mult))
                link(dve.scalar_tensor_tensor(o, z[:, :, 1:SEG + 1], tap[1], o, ALU.mult, ALU.add))
                link(dve.scalar_tensor_tensor(o, z[:, :, 2:SEG + 2], tap[2], o, ALU.mult, ALU.add))
            elif kind == "sb":
                dve.wait_ge(chunk_used, base + r + 1)
                dve.scalar_tensor_tensor(scr[2 + y % 2][:, t0:TOK], bank[:, t0:TOK], bias, cv[:, t0:TOK],
                                         ALU.add, ALU.mult).then_inc(evac_dve, 1)
                dve.wait_ge(evac_dve, d0 + d + 1)
                dve.engine_nop().then_inc(yf_ready, 1)
                split_y(y, ysc_hi, ysc_lo, i, t0)
            elif kind == "mo":
                dve.wait_ge(evac_act, a0 + a + 1)
                dve.wait_ge(ht_ready, HEADS * (layer + 1))
                dve.tensor_tensor(scr[2 + y % 2][:, t0:TOK], scr[i % 2][:, t0:TOK], ht[:, i, t0:TOK], ALU.mult
                                  ).then_inc(yf_ready, 1)
                split_y(y, yml_hi, yml_lo, i, t0)

        def turn_v(layer, v):
            g = 12 * layer + v
            dve.wait_ge(v_turned, g + 1)
            src = ps[4 + v % 2][:, :].rearrange("p (t n) -> p t n", t=TT)
            if v < 8:
                dst = vaug[:, :, v // 2, (v % 2) * P:(v % 2 + 1) * P]
            else:
                dst = dav[:, :, v - 8, :]
            dve.tensor_copy(dst, src).then_inc(v_placed, 1)

        def rope(layer, i):
            xs = dqk[:, i, SEG:TOK]
            dve.wait_ge(rot_done, 8 * layer + i + 1)
            wait(dve, rope_done, 8 * layer + i)
            dve.tensor_tensor(scr[0][:, 0:SEG], ps[6 + i % 2][:, 0:SEG], rope_sin, ALU.mult)
            link(dve.tensor_tensor(xs, xs, rope_cos, ALU.mult))
            dve.tensor_tensor(xs, xs, scr[0][:, 0:SEG], ALU.add).then_inc(rope_done, 1)

        def flip(dst, src):
            dve.tensor_copy(dst[:, 0:SEG], rev(src, 0))
            return dve.tensor_copy(dst[:, SEG:TOK], rev(src, 1))

        def rev(src, s):
            return src[:, s * SEG:(s + 1) * SEG][:, ::-1]

        def gates(layer):
            dve.memset(vaug[:, :, :, 256:257], 1.0)
            raw_g, lf, ln1, ia, la = gt[1], gt[2], gt[3], gt[4], gt[5]
            dve.wait_ge(gate_act, 5 * layer + 1)
            link(dve.tensor_scalar(ln1[64:128, :], raw_g[64:128, :], -1.0, None, ALU.mult))
            dve.tensor_tensor(ln1[64:128, :], raw_g[64:128, :], ln1[64:128, :], ALU.max).then_inc(gate_abs, 1)
            link(dve.tensor_scalar(lf[64:128, :], raw_g[64:128, :], 0.0, None, ALU.min))
            dve.wait_ge(gate_act, 5 * layer + 2)
            link(dve.tensor_tensor(lf[64:128, :], lf[64:128, :], ln1[64:128, :], ALU.subtract))
            dve.tensor_copy(ia[0:32, :], raw_g[0:32, :])
            flip(ia[32:64, :], raw_g[32:64, :])
            dve.tensor_copy(la[0:32, :], lf[64:96, :])
            link(flip(la[32:64, :], lf[96:128, :]))
            ones, fsum, gmax = gt[6], gt[7], gt[2]
            link(dve.memset(ones[0:64, :], 1.0))
            link(dve.tensor_tensor_scan(fsum[0:64, :], ones[0:64, :], la[0:64, :], 0.0, ALU.mult, ALU.add))
            link(dve.tensor_tensor(ia[0:64, :], ia[0:64, :], fsum[0:64, :], ALU.subtract))
            link(dve.tensor_tensor_scan(gmax[0:64, :], ones[0:64, :], ia[0:64, :], -3.0e38, ALU.mult, ALU.max))
            link(dve.tensor_tensor(fsum[0:64, :], fsum[0:64, :], gmax[0:64, :], ALU.add))
            link(dve.tensor_scalar(gmax[0:64, :], gmax[0:64, :], -1.0, None, ALU.mult))
            top = gt[0]
            dve.tensor_copy(top[0:32, :], ia[0:32, :])
            flip(top[32:64, :], ia[32:64, :])
            dve.tensor_copy(top[64:96, :], fsum[0:32, :])
            flip(top[96:128, :], fsum[32:64, :])
            dve.tensor_copy(neg_g[0:32, :], gmax[0:32, :])
            flip(neg_g[32:64, :], gmax[32:64, :]).then_inc(gate_dve, 1)

        def ml_scores(layer, head, s):
            t0 = t0_of(layer)
            u = HEADS * layer + head
            for n in range(2):
                found, diag = segments(s, n, t0)
                dve.wait_ge(e_ready, 8 * u + 2 * s + n + 1)
                dve.wait_ge(s_ready, 4 * u + s + 1)
                for b, e in found:
                    m = dve.tensor_tensor(pw[:, n, s, b:e], xt[:, n, b:e], ps[6 + s % 2][:, b:e], ALU.mult)
                if diag is not None:
                    link(m)
                    own = pw[:, n, s, s * P:(s + 1) * P]
                    m = dve.tensor_tensor(own, own, (mask_f, mask_b)[n], ALU.mult)
                m.then_inc(pw_ready, 1)

        def ml_numerator(layer, head, t):
            first = t0_of(layer) // P
            if t < first:
                return
            if head == 0 and t == first:
                dve.wait_ge(gate_act, 5 * layer + 5)
            nt = nth_out(layer, head, t)
            dve.wait_ge(num_ready, nt + 1)
            for n in range(2):
                m = dve.tensor_scalar(small[:, 12 + n:13 + n], ps[6 + n][:, 256:257], -1.0, None, ALU.mult)
            link(m)
            for n in range(2):
                row = 32 * n + head
                m = dve.scalar_tensor_tensor(small[:, 6 + n:7 + n], small[:, 12 + n:13 + n],
                                             em[:, t, row:row + 1], ps[6 + n][:, 256:257], ALU.max, ALU.max)
            link(m)
            link(dve.reciprocal(small[:, 8:10], small[:, 6:8]))
            if nt >= 2:
                dve.wait_ge(h_turned, nt - 1)
            link(dve.tensor_scalar(hf[:, :], ps[6][:, 0:256], small[:, 8:9], None, ALU.mult))
            dve.scalar_tensor_tensor(hs[:, t % 2, :], ps[7][:, 0:256], small[:, 9:10], hf[:, :],
                                     ALU.mult, ALU.add).then_inc(hsum_ready, 1)

        def attend(layer):
            scale = DA_HALF ** -0.5
            units, u0 = attention_units(layer)
            tiles = range(t0_of(layer) // P, TT)

            def maxima(v):
                nk = len(units[v][2]) * P
                for j in range(2):
                    dve.wait_ge(sc_ready, 2 * (u0 + v) + j + 1)
                    m = dve.tensor_reduce(att[:, v % 2, 4 + j:5 + j], ps[SCORE_BANK[v % 2] + j][:, 0:nk], AXX, ALU.max)
                link(m)
                dve.tensor_scalar(att[:, v % 2, 0:2], att[:, v % 2, 4:6], -scale, None, ALU.mult
                                  ).then_inc(smax_ready, 2)

            def weights(v):
                nk = len(units[v][2]) * P
                p0, p1 = scr[2 * (v % 2)], scr[2 * (v % 2) + 1]
                a = att[:, v % 2, :]
                dve.wait_ge(p_ready, 2 * (u0 + v) + 2)
                link(dve.reciprocal(a[:, 6:8], a[:, 2:4]))
                link(dve.tensor_tensor(a[:, 8:9], a[:, 7:8], neg_lam[:, layer:layer + 1], ALU.mult))
                if v >= 2:
                    dve.wait_ge(wgt_turned, u0 + v - 1)
                link(dve.tensor_scalar(p1[:, 0:nk], p1[:, 0:nk], a[:, 8:9], None, ALU.mult))
                dve.scalar_tensor_tensor(wgt[v % 2][:, 0:nk], p0[:, 0:nk], a[:, 6:7], p1[:, 0:nk],
                                         ALU.mult, ALU.add).then_inc(wgt_ready, 1)

            def outputs(v):
                head, t, _ = units[v]
                dve.wait_ge(o_ready, u0 + v + 1)
                dve.tensor_copy(oda[:, t, head, :], ps[7 - 4 * (v % 2)][:, 0:P]).then_inc(o_copied, 1)
            maxima(0)
            for v in range(len(units)):
                if v + 1 < len(units):
                    maxima(v + 1)
                weights(v)
                if v:
                    outputs(v - 1)
            outputs(len(units) - 1)
            dve.wait_ge(o_std, layer + 1)
            link(dve.reciprocal(ssq[:, tiles[0]:TT, :], ssq[:, tiles[0]:TT, :]))
            for t in tiles:
                for head in range(HEADS):
                    m = dve.tensor_scalar(oda[:, t, head, :], oda[:, t, head, :], ssq[:, t, head:head + 1], None, ALU.mult)
            m.then_inc(o_scaled, 1)
            t0 = tiles[0] * P
            for head in range(HEADS):
                dve.wait_ge(o_turned, 4 * layer + head + 1)
                if head >= 2:
                    dve.wait_ge(yda_h, 4 * layer + head - 1)
                lam_init = 0.8 - 0.6 * math.exp(-0.3 * layer)
                f = scr[2 + head % 2][:, t0:TOK]
                dve.tensor_scalar(f, ps[4 + head % 2][:, t0:TOK], cols[:, 3, 76 + layer:77 + layer], 1.0 - lam_init,
                                  ALU.mult, ALU.mult).then_inc(yda_f, 1)
                dve.wait_ge(yda_h, 4 * layer + head + 1)
                dve.tensor_tensor(yda_lo[:, head, t0:TOK], f, yda_hi[:, head, t0:TOK].bitcast(F32), ALU.subtract
                                  ).then_inc(yda_ready, 1)

        def mixer(layer):
            t0 = t0_of(layer)
            for step in ORDER:
                if step[0] in EVAC_ENGINE:
                    proj(layer, step)
                elif step[0] == "ada":
                    r = BASES[layer, "proj"][0] + PLAN[step][0]
                    ahead(r, 0)
                    if step[2] == 3:
                        dve.wait_ge(chunk_used, r + 1)
                        ada_copy(ADA_OF[layer, "proj"] + step[1], 4, 4)
                elif step[0] == "adat":
                    ada_add(ADA_OF[layer, "proj"] + step[1], 5, layer)
                elif step[0] == "gates":
                    gates(layer)
                elif step[0] == "attend":
                    attend(layer)
                elif step[0] in ("ml_s", "ml_n"):
                    (ml_scores if step[0] == "ml_s" else ml_numerator)(layer, *step[1:])
                elif step[0] in ("turn_v", "rope"):
                    {"turn_v": turn_v, "rope": rope}[step[0]](layer, step[1])
            base, a0, d0 = BASES[layer, "gate"]
            pattern = gate_pattern(layer)
            block = ADA_OF.get((layer, "gate"))

            def body(i):
                for c, (kind, q) in enumerate(pattern):
                    ahead(base, c, i, len(pattern))
                    if kind == "a":
                        if q == 3:
                            dve.wait_ge(chunk_used, base + c + 1 + len(pattern) * i)
                            ada_copy(block + i, 4, 4)
                        continue
                    if q % 2 == 0:
                        continue
                    e = q // 6
                    dve.wait_ge(chunk_used, base + c + 1 + len(pattern) * i)
                    dve.wait_ge(evac_act, a0 + q // 2 + 1 + 6 * i)
                    z = scr[2 + e][:, t0:TOK]
                    dst = z if q % 6 == 1 else scr[4][:, t0:TOK]
                    dve.tensor_tensor(dst, scr[(q // 2) % 2][:, t0:TOK], ps[q % 4][:, t0:TOK], ALU.mult
                                      ).then_inc(evac_dve, 1)
                    dve.wait_ge(evac_dve, d0 + q // 2 + 1 + 6 * i)
                    if q % 6 == 3:
                        dve.tensor_tensor(z, z, dst, ALU.add).then_inc(z_part, 1)
                        dve.wait_ge(z_part, KD * layer + e + 1 + 2 * i)
                    if q % 6 == 5:
                        dve.tensor_tensor(z, z, dst, ALU.add).then_inc(z_sum, 1)
                        dve.wait_ge(z_hi_done, KD * layer + e + 1 + 2 * i)
                        dve.tensor_tensor(z_lo[:, 2 * i + e, t0:TOK], z, z_hi[:, 2 * i + e, t0:TOK].bitcast(F32),
                                          ALU.subtract).then_inc(z_ready, 1)
                if block is not None:
                    ada_add(block + i, 5, block // ADA_BLOCKS)
            run(dve, KD // 2, body)
            gate_columns(layer, 1, 1.0)
            base, _, d0 = BASES[layer, "wo"]
            s0 = KD * (3 * layer + 1)

            def body_o(i):
                for e in range(4):
                    ahead(base, e, i, 4)
                    dve.wait_ge(chunk_used, base + e + 1 + 4 * i)
                    add_branch(4 * i + e, e, t0, d0 + e + 1 + 4 * i, s0 + e + 4 * i)
            run(dve, KD // 4, body_o)

        dve.wait_ge(evac_act, 4)
        dve.wait_ge(evac_dve, 4)
        dve.wait_ge(ada_ev, 4)
        columns(0)
        modulate(0)
        for layer in range(DEPTH):
            up(layer, 0)
            down(layer, 0)
            norm(3 * layer + 1)
            mixer(layer)
            norm(3 * layer + 2)
            up(layer, 1)
            down(layer, 1)
            norm(3 * layer + 3)

    block.__exit__(None, None, None)


def constants():
    out = np.zeros((P, 1154), np.float32)
    row, col = np.arange(P)[:, None], np.arange(P)[None, :]
    out[:, 0:128] = row == col
    out[:, 128:256] = col >= row
    out[:, 256:384] = col <= row
    first = (col % 64) < 32
    out[:, 384:512] = np.where(first & (row == col + 32), -1.0, 0.0) + np.where(~first & (row == col - 32), 1.0, 0.0)
    out[:, 512:640] = 1.0 / D
    n_freq = DA_HALF // 4
    inv = np.float32(10000.0) ** (-np.arange(n_freq, dtype=np.float32) / np.float32(n_freq))
    t = np.arange(SEG)
    ang = np.concatenate([(t // GRID_W).astype(np.float32)[None, :] * inv[:, None],
                          (t % GRID_W).astype(np.float32)[None, :] * inv[:, None]], 0)
    out[:, 640:896] = np.tile(np.cos(ang), (4, 1))
    out[:, 896:1152] = np.tile(np.sin(ang), (4, 1))
    out[0:4, 1152:1154] = np.tile(np.eye(2), (2, 1))
    return out


_INS = ["x", "c", "ctx", "c_ctx", "w_ada", "b_ada", "ln_g", "ln_b", "ffn1_up", "ffn1_down", "ffn2_up",
        "ffn2_down", "w_in", "b_in", "conv_w", "w_sc", "w_ml", "w_da", "w_o", "lam_q1", "lam_k1", "lam_q2",
        "lam_k2", "da_norm_g"]


def kernel(**inputs):
    import concourse.bacc as _bacc
    from concourse.bass_utils import run_bass_kernel_spmd as _run

    nc = _bacc.Bacc("TRN2", target_bir_lowering=False, num_devices=1)
    arrays, args = {}, []
    for name in _INS + ["consts"]:
        a = constants() if name == "consts" else np.ascontiguousarray(inputs[name])
        arrays[f"in_{name}"] = a
        args.append(nc.dram_tensor(f"in_{name}", a.shape, mybir.dt.from_np(a.dtype), kind="ExternalInput").ap())
    args.append(nc.dram_tensor("out_0", (1, SEG, D), F32, kind="ExternalOutput").ap())
    build(nc, *args)
    r = _run(nc, [arrays], core_ids=[0])
    return r.results[0]["out_0"]
```

```python
import math

import numpy as np

import concourse.bass as bass
from concourse import mybir

F32 = mybir.dt.float32
F32R = mybir.dt.float32r
ACT = mybir.ActivationFunctionType
ALU = mybir.AluOpType
AXX = mybir.AxisListType.X

P = 128
D = 1024
KD = D // P
SEG = 256
TOK = 2 * SEG
TT = TOK // P
DEPTH = 2
FH = 2816
KF = FH // P
N_IN = 9232
MG_COL = 4608
GRID_W = 64
HEADS = 4
DQK = 128
DA_HALF = 64
ALPHA = (2 * DEPTH) ** 0.25
EPS = 1e-5
N_MOD = 9
MODT = N_MOD * KD
DOWN_K = [range(0, 6), range(6, 12), range(12, 17), range(17, 22)]
RAW = 2
RAW_LATE = 4
SPLIT = 4
CH_UP, CH_DOWN, CH_PROJ, CH_WO = 2 * KF, 4 * KD, 48, KD
BLOCK = 4 * P
ADA_BLOCKS = N_MOD * D // BLOCK

SEC = {"sb": 0, "cg": 4, "sx": 8, "mq": 12, "mk": 16, "mv": 20, "mo": 28,
       "dq": 36, "dk": 40, "dv": 44, "gs": 48, "gm": 56, "gd": 64}


UP_PLAIN = [("w", q) for q in range(4)]
UP_ADA = [("w", 0), ("a", 0), ("w", 1), ("a", 1), ("w", 2), ("a", 2), ("a", 3), ("w", 3)]
DOWN_PLAIN = [("w", q) for q in range(8)]
DOWN_ADA = (DOWN_PLAIN[0:2] + [("a", 0)] + DOWN_PLAIN[2:4] + [("a", 1)] + DOWN_PLAIN[4:6] + [("a", 2)]
            + DOWN_PLAIN[6:7] + [("a", 3)] + DOWN_PLAIN[7:8])
GATE_PLAIN = [("w", q) for q in range(12)]
GATE_ADA = (GATE_PLAIN[0:2] + [("a", 0)] + GATE_PLAIN[2:5] + [("a", 1)] + GATE_PLAIN[5:8] + [("a", 2)]
            + GATE_PLAIN[8:10] + [("a", 3)] + GATE_PLAIN[10:12])
ADA_OF = {(0, "up0"): 4, (0, "down0"): 14, (0, "proj"): 18, (0, "gate"): 21, (0, "up1"): 25, (0, "down1"): 35}
PROJ_ADA = ADA_OF[0, "gate"] - ADA_OF[0, "proj"]
assert ADA_OF[0, "down1"] + 1 == DEPTH * ADA_BLOCKS


def up_patterns(layer, f):
    return (UP_PLAIN, UP_ADA) if (layer, f"up{f}") in ADA_OF else (UP_PLAIN, UP_PLAIN)


def down_patterns(layer, f):
    if (layer, f"down{f}") not in ADA_OF:
        return DOWN_PLAIN, DOWN_PLAIN
    return DOWN_ADA, (DOWN_ADA if f == 0 else DOWN_PLAIN)


def gate_pattern(layer):
    return GATE_ADA if (layer, "gate") in ADA_OF else GATE_PLAIN


def round_base(base, first, other):
    return base + len(first) - len(other)


def in_col(tile):
    return tile * P + (16 if tile >= 36 else 0)


def bias_at(layer, tile):
    if layer == 0:
        return 2, tile
    return (2, 72 + tile) if tile < 36 else (3, tile - 36)


def proj_order(layer):
    order = [("mq", i) for i in range(4)] + [("gates", 0)]
    has_ada = (layer, "proj") in ADA_OF
    for n in range(12):
        order.append(("mk", n) if n < 4 else ("mv", n - 4))
        if n >= 5:
            order.append(("turn_v", n - 5))
        if has_ada:
            if n % 4 == 0 and n:
                order.append(("adat", n // 4 - 1))
            order.append(("ada", n // 4, n % 4))
        if n in (1, 3, 5):
            order.append(("gates", (n + 1) // 2))
    fill = [(kind, i) for i in range(4) for kind in ("cg", "sx", "sb")]
    fill += [("dq", 0), ("dk", 0)] + [("mo", i) for i in range(4)] + [("dq", 1), ("dk", 1), ("dq", 2), ("dk", 2)]
    fill += [("mo", 4), ("mo", 5), ("dv", 0), ("dv", 1)]
    order += [fill.pop(0), ("turn_v", 7)] + has_ada * [("adat", 2)] + [fill.pop(0), ("ml_gates", 0), fill.pop(0)]
    for h in range(HEADS):
        for group in ([("ml_s", h, 0), ("ml_s", h, 1)], [("ml_s", h, 2), ("ml_s", h, 3)], [("ml_n", h, 0)],
                      [("ml_n", h, 1), ("ml_n", h, 2)], [("ml_n", h, 3)], [("ml_t", h)]):
            order += group + fill[:1]
            del fill[:1]
    assert not fill
    order += [("mo", 6), ("rope", 0), ("rope", 4), ("turn_v", 8), ("ysplit", 0)]
    order += [("mo", 7), ("rope", 1), ("rope", 5), ("turn_v", 9), ("ysplit", 1)]
    order += [("dq", 3), ("rope", 2), ("rope", 6), ("ysplit", 2), ("ysplit", 3)]
    order += [("dk", 3), ("ysplit", 4), ("ysplit", 5)]
    order += [("dv", 2), ("rope", 3), ("rope", 7), ("ysplit", 6), ("ysplit", 7)]
    order += [("dv", 3), ("turn_v", 10), ("turn_v", 11)]
    order += [("attend", 0)]
    return order


def vector_order(order):
    order = list(order)
    for n in range(1, len(order) - 1):
        if order[n][0] == "ml_n" and order[n + 1][0] == "ml_n" and order[n - 1][0] in EVAC_ENGINE:
            order[n - 1], order[n] = order[n], order[n - 1]
    return order


ORDERS = [proj_order(layer) for layer in range(DEPTH)]
ROPES = [step[1] for step in ORDERS[0] if step[0] == "rope"]
EVAC_ENGINE = {"mq": "act", "mk": "dve", "mv": "act", "cg": "act", "sx": "dve", "sb": "dve",
               "mo": "act", "dv": "act", "dq": "act", "dk": "act"}
X_ONLY = {"cg", "sx", "sb", "mq", "mo", "dq"}


def proj_plan(order):
    plan, r, n, a, d = {}, 0, 0, 0, 0
    for step in order:
        if step[0] == "ada":
            plan[step] = (r,)
            r += 1
        elif step[0] in EVAC_ENGINE:
            plan[step] = (r, n, a, d)
            r += 1
            n += 1
            a += EVAC_ENGINE[step[0]] == "act"
            d += EVAC_ENGINE[step[0]] == "dve"
    assert n == CH_PROJ
    return plan, r, a, d


PLANS, PROJ_R, PROJ_A, PROJ_D = zip(*(proj_plan(order) for order in ORDERS))
NTH_PROJ = {v[1]: k for k, v in PLANS[0].items() if len(v) > 1}


def bases():
    out, r, a, d = {}, 0, 4, 4
    for layer in range(DEPTH):
        for name in ("up0", "down0", "proj", "gate", "wo", "up1", "down1"):
            out[layer, name] = (r, a, d)
            kind = name.rstrip("01")
            if kind in ("up", "down"):
                first, other = (up_patterns if kind == "up" else down_patterns)(layer, int(name[-1]))
                r += len(first) + (CH_UP // len(UP_PLAIN) if kind == "up" else CH_DOWN // len(DOWN_PLAIN)) * len(other)
                r -= len(other)
            else:
                r += {"proj": PROJ_R[layer], "gate": len(gate_pattern(layer)) * (KD // 2), "wo": CH_WO}[kind]
            a += {"up": KF, "down": 0, "proj": PROJ_A[layer], "gate": 3 * KD, "wo": 0}[kind]
            d += {"up": KF, "down": KD, "proj": PROJ_D[layer], "gate": 3 * KD, "wo": KD}[kind]
    return out, r


BASES, CHUNKS = bases()
LATE = BASES[DEPTH - 1, "gate"][0]
assert LATE % RAW == 0


def raw_place(base, c, i=0, step=0):
    r = base + c
    if r < LATE:
        return r % RAW, 16 * (r // RAW + 1) + 16 * step // RAW * i, r - RAW + 1 + step * i
    slot = (r - LATE) % RAW_LATE
    before = LATE // RAW if slot < RAW else 0
    return (slot, 16 * (before + (r - LATE) // RAW_LATE + 1) + 16 * step // RAW_LATE * i,
            r - RAW_LATE + 1 + step * i)


def segments(s, n, t0):
    if n == 0:
        found = [(max(s * P, t0), TOK)]
    elif s >= 2:
        found = [(SEG, (s + 1) * P)]
    else:
        found = [(0, (s + 1) * P), (SEG, TOK)] if t0 == 0 else [(SEG, TOK)]
        if t0 == 0 and s == 1:
            found = [(0, TOK)]
    return found, (s if s * P >= t0 else None)


KEYS = {("f", 0): [0], ("f", 1): [0, 1], ("f", 2): [0, 1, 2], ("f", 3): [0, 1, 2, 3],
        ("b", 0): [0, 1], ("b", 1): [1], ("b", 2): [0, 1, 2, 3], ("b", 3): [0, 1, 3]}


def build(nc, x, c, ctx, c_ctx, w_ada, b_ada, ln_g, ln_b, ffn1_up, ffn1_down, ffn2_up, ffn2_down,
          w_in, b_in, conv_w, w_sc, w_ml, w_da, w_o, lam_q1, lam_k1, lam_q2, lam_k2, da_norm_g,
          consts, out):
    spot = [16512]

    def at(name, shape, dtype, offset=None):
        size = int(np.prod(shape[1:])) * 4
        if offset is None:
            offset = spot[0]
            spot[0] += (size + 31) // 32 * 32
        return nc.alloc_sbuf_tensor_at(name, shape, dtype, offset=offset)

    h = at("h", [P, KD, TOK], F32)
    u_hi = at("u_hi", [P, KD, TOK], F32R)
    u_lo = at("u_lo", [P, KD, TOK], F32R)
    raw = at("raw", [P, RAW, D], F32)
    w_hi = at("w_hi", [P, SPLIT, D], F32R)
    w_lo = at("w_lo", [P, SPLIT, D], F32R)
    con = at("con", [P, 1154], F32)
    ada_sum = con[0:4, 1152:1154]
    ident, mask_f, mask_b = con[:, 0:128], con[:, 128:256], con[:, 256:384]
    rot_w, mean_w = con[:, 384:512], con[:, 512:640]
    rope_cos, rope_sin = con[:, 640:896], con[:, 896:1152]
    cols = at("cols", [P, 4, P], F32)
    mods = at("mods", [P, DEPTH * MODT, 2], F32)
    cs = at("cs", [P, KD, 2], F32)
    cs_parts = at("cs_parts", [P, KD, 4], F32R)
    ada_row = at("ada_row", [4, BLOCK], F32)
    one_zero = at("one_zero", [P, 2, KD], F32)
    mod_a = at("mod_a", [P, KD, 2], F32)
    mod_b = at("mod_b", [P, KD, 2], F32)
    res_g = at("res_g", [P, KD], F32)
    res_b = at("res_b", [P, KD], F32)
    gate = at("gate", [P, KD, 2], F32)
    neg_lam = at("neg_lam", [P, DEPTH], F32)
    lam_e = at("lam_e", [P, DEPTH, 2], F32)
    gate_bias = at("gate_bias", [P, DEPTH], F32)
    small = at("small", [P, 16], F32)
    wg_in = at("wg_in", [P, KD, 16], F32)
    att = at("att", [P, 2, 10], F32)
    region = spot[0]
    spot[0] += 96 * 1024
    scr = [at(f"scr{i}", [P, TOK], F32) for i in range(6)]
    assert spot[0] <= 229368, spot[0]
    KB = 1024
    g_hi = at("g_hi", [P, KF, TOK], F32R, region)
    g_lo = at("g_lo", [P, KF, TOK], F32R, region + KF * TOK * 4)
    x_in = at("x_in", [P, TT, D], F32, region)
    rows = at("rows", [P, 4, P], F32, region + 16 * KB)
    stage = at("stage", [P, 16, D], F32, region + 24 * KB)
    lam_in = at("lam_in", [P, DEPTH, 4, DA_HALF], F32, region + 20 * KB)
    lam_p = at("lam_p", [P, DEPTH, 2, DA_HALF], F32, region + 22 * KB)
    y_out = at("y_out", [P, 2, D], F32, region)
    ysc_hi = at("ysc_hi", [P, 4, TOK], F32R, region)
    ysc_lo = at("ysc_lo", [P, 4, TOK], F32R, region + 8 * KB)
    yml_hi = at("yml_hi", [P, 8, TOK], F32R, region + 16 * KB)
    yml_lo = at("yml_lo", [P, 8, TOK], F32R, region + 32 * KB)
    vaug = at("vaug", [P, TT, HEADS, 257], F32, region + 16 * KB)
    neg_g = at("neg_g", [P, TOK], F32, region + 33 * KB)
    am = at("am", [P, TT, P], F32, region + 35 * KB)
    em = at("em", [P, TT, 64], F32, region + 37 * KB)
    xt = at("xt", [P, 2, TOK], F32, region + 38 * KB)
    hs = at("hs", [P, 2, SEG], F32, region + 42 * KB)
    hf = at("hf", [P, SEG], F32, region + 44 * KB)
    pw = at("pw", [P, 2, TT, TOK], F32, region + 48 * KB)
    nam = at("nam", [P, TT, 64], F32, region + 45 * KB)
    cgt, cv = scr[0], scr[1]
    zpad = at("zpad", [P, 2, SEG + 2], F32, region + 96 * KB + 4 * 2 * KB)
    dav = at("dav", [P, TT, HEADS, P], F32, region + 48 * KB)
    yda_hi = at("yda_hi", [P, 4, TOK], F32R, region + 48 * KB)
    yda_lo = at("yda_lo", [P, 4, TOK], F32R, region + 56 * KB)
    gt = [at(f"gt{i}", [P, TOK], F32, region + (64 + 2 * i) * KB) for i in range(8)]
    ht = at("ht", [P, 8, TOK], F32, region + 64 * KB)
    oda = at("oda", [P, TT, HEADS, P], F32, region + 64 * KB)
    ssq = at("ssq", [P, TT, HEADS], F32, region + 72 * KB)
    q_first = at("q_first", [P, HEADS, TOK], F32, region + 56 * KB)
    wgt = [scr[4], at("wgt1", [P, TOK], F32, region + 73 * KB)]
    wgt_t = [scr[5], at("wgt_t1", [P, TOK], F32, region + 75 * KB)]
    junk = at("junk", [P, P], F32, region + 77 * KB)
    z_hi = at("z_hi", [P, KD, TOK], F32R, region + 64 * KB)
    z_lo = at("z_lo", [P, KD, TOK], F32R, region + 80 * KB)
    qt = at("qt", [P, HEADS, TOK], F32, region + 80 * KB)
    kt = at("kt", [P, HEADS, TOK], F32, region + 88 * KB)
    dqk = at("dqk", [P, 8, TOK], F32, region + 80 * KB)
    wg_hi = at("wg_hi", [P, KD, P], F32R, region + 88 * KB)
    wg_lo = at("wg_lo", [P, KD, P], F32R, region + 92 * KB)

    def value_bank(v):
        return (6 if v < 8 else 4) + v % 2

    def y_number(layer, kind, i):
        return 12 * layer + i + (4 if kind == "mo" else 0)

    def raw_tiles(slot, kt_n=KD):
        if slot < RAW:
            return raw[:, slot, :].rearrange("p (k n) -> p k n", n=P)[:, 0:kt_n, :]
        return h[:, 0:kt_n, (slot - RAW) * P:(slot - RAW + 1) * P]

    def split_tiles(w, slot):
        return w[:, slot, :].rearrange("p (k n) -> p k n", n=P)

    ps = [nc.alloc_psum_tensor(f"ps{i}", [P, 512], F32) for i in range(8)]

    def sem(name):
        return nc.alloc_semaphore(name)

    const_in, x_landed, rows_in, lam_landed, gate_in, wg_landed = (
        sem(n) for n in ("const_in", "x_landed", "rows_in", "lam_landed", "gate_in", "wg_landed"))
    raw_in = [sem(f"raw_in{i}") for i in range(RAW_LATE)]
    stage_in = [sem(f"stage_in{i}") for i in range(4)]
    zeroed = sem("zeroed")
    rows_turned, cols_ready, cs_ready, lam_dot, lam_exp = (
        sem(n) for n in ("rows_turned", "cols_ready", "cs_ready", "lam_dot", "lam_exp"))
    x_turned, hi_done, lo_done, chunk_used, evac_act, evac_dve = (
        sem(n) for n in ("x_turned", "hi_done", "lo_done", "chunk_used", "evac_act", "evac_dve"))
    ada_copied, ada_done, ada_ev, g_hi_done, g_ready, sum_done = (
        sem(n) for n in ("ada_copied", "ada_done", "ada_ev", "g_hi_done", "g_ready", "sum_done"))
    cs_lo_done = sem("cs_lo_done")
    ln_mean, ln_cent, ln_sq, ln_sq_used, ln_std, ln_xn = (
        sem(n) for n in ("ln_mean", "ln_cent", "ln_sq", "ln_sq_used", "ln_std", "ln_xn"))
    cols_mod, u_hi_done, u_ready, h_ready = (sem(n) for n in ("cols_mod", "u_hi_done", "u_ready", "h_ready"))
    yf_ready, y_hi_done, y_ready = (sem(n) for n in ("yf_ready", "y_hi_done", "y_ready"))
    v_turned, v_placed, rot_done, rope_done = (sem(n) for n in ("v_turned", "v_placed", "rot_done", "rope_done"))
    wg_ready, mg_done, gate_act, gate_dve, gate_turn = (
        sem(n) for n in ("wg_ready", "mg_done", "gate_act", "gate_dve", "gate_turn"))
    ng_ready, s_ready, e_ready, pw_ready = (sem(n) for n in ("ng_ready", "s_ready", "e_ready", "pw_ready"))
    num_ready, hsum_ready, h_turned, ht_ready = (sem(n) for n in ("num_ready", "hsum_ready", "h_turned", "ht_ready"))
    sc_ready, smax_ready, p_ready, wgt_ready, wgt_turned, wt_ready, o_ready, o_copied, o_sq = (
        sem(n) for n in ("sc_ready", "smax_ready", "p_ready", "wgt_ready", "wgt_turned", "wt_ready",
                         "o_ready", "o_copied", "o_sq"))
    o_std, o_scaled, o_turned, yda_f, yda_h, yda_ready = (
        sem(n) for n in ("o_std", "o_scaled", "o_turned", "yda_f", "yda_h", "yda_ready"))
    ada_summed = sem("ada_summed")
    z_part, z_sum, z_hi_done, z_ready = (sem(n) for n in ("z_part", "z_sum", "z_hi_done", "z_ready"))
    gate_abs = sem("gate_abs")
    out_turned, out_ready, out_done = (sem(n) for n in ("out_turned", "out_ready", "out_done"))
    dve_chain = sem("dve_chain")
    act_chain = sem("act_chain")

    def wait(eng, s, value):
        if isinstance(value, int) and value <= 0:
            return
        eng.wait_ge(s, value)

    def halves(t0):
        return [(0, slice(0, SEG)), (1, slice(SEG, TOK))] if t0 == 0 else [(1, slice(SEG, TOK))]

    def t0_of(layer, x_only=True):
        return SEG if layer == DEPTH - 1 and x_only else 0

    ups = (ffn1_up, ffn2_up)
    downs = (ffn1_down, ffn2_down)

    def norm_cols(n):
        if n == 0:
            return one_zero[:, 0, :], one_zero[:, 1, :]
        layer, i = (n - 1) // 3, (n - 1) % 3
        o = 72 + (layer * 3 + i) * KD
        return cols[:, 0, o:o + KD], cols[:, 1, o:o + KD]

    def next_mods(n):
        return (n // 3) * MODT + (n % 3) * 3 * KD

    def gate_mods(layer, i):
        return layer * MODT + (3 * i + 2) * KD

    def norm_t0(n):
        return SEG if n >= 5 else 0

    def norm_d(n):
        layer, i = (n - 1) // 3, (n - 1) % 3
        return BASES[layer, ("down0", "wo", "down1")[i]][2] + KD

    def run(eng, count, body, peel_first=False, peel_last=False):
        n = count - 1 if peel_last else count
        if peel_first:
            body(0)
        with eng.Fori(int(peel_first), n) as i:
            body(i)
        if peel_last:
            body(n)

    def run_from_1(eng, count, body, peel_last=False):
        with eng.Fori(1, count - 1 if peel_last else count) as i:
            body(i)
        if peel_last:
            body(count - 1)

    SCORE_BANK = (0, 4)

    def nth_out(layer, head, t):
        n = TT - t0_of(layer) // P
        return (HEADS * TT if layer else 0) + n * head + max(0, t - (TT - n))

    def attention_units(layer):
        tiles = range(t0_of(layer) // P, TT)
        return [(head, t, range(2 if t < 2 else 4)) for t in tiles for head in range(HEADS)], 16 * layer

    def as_rows(a):
        return a.rearrange("(r p) -> r p", p=P)

    VECTOR_ROWS = [(as_rows(c_ctx), 3, 60, 8), (c.rearrange("a (r p) -> (a r) p", p=P), 3, 68, 8)]
    for layer in range(DEPTH):
        VECTOR_ROWS += [(as_rows(b_ada[layer]), layer, 0, 72), (as_rows(b_in[layer, 0:MG_COL]), 2, 72 * layer, 36),
                        (as_rows(b_in[layer, MG_COL + 16:N_IN]), *((2, 36) if layer == 0 else (3, 0)), 36)]
    VECTOR_ROWS += [(ln_g.rearrange("l i (r p) -> (l i r) p", p=P), 0, 72, 48),
                    (ln_b.rearrange("l i (r p) -> (l i r) p", p=P), 1, 72, 48),
                    (conv_w.rearrange("l t (r p) -> (l t r) p", p=P), 3, 36, 24), (da_norm_g, 3, 76, 2)]

    block = nc.Block()
    block.__enter__()

    @block.sync
    def _(sp):
        sp.dma_start(con[:, :], consts).then_inc(const_in, 16)
        for a, tile, r0, n in VECTOR_ROWS[1::2]:
            sp.dma_start(rows[r0:r0 + n, tile, :], a).then_inc(rows_in, 16)
        ada_v = w_ada.rearrange("l (k p) n -> l p k n", p=P)
        for b in range(4):
            if b == 2:
                for p_, a in enumerate((ctx, x)):
                    sp.dma_start(x_in[:, 2 * p_:2 * p_ + 2, :], a[0].rearrange("(t p) d -> p t d", p=P)
                                 ).then_inc(x_landed, 16)
            for j in range(4):
                sp.dma_start(stage[:, 4 * b + j, :].rearrange("p (k n) -> p k n", k=2),
                             ada_v[0, :, 2 * j:2 * j + 2, b * BLOCK:(b + 1) * BLOCK]).then_inc(stage_in[b], 16)

        def load(place, src, kt_n):
            slot, _, split_before = place
            wait(sp, lo_done, split_before)
            sp.dma_start(raw_tiles(slot, kt_n), src).then_inc(raw_in[slot], 16)

        def ada_chunk(place, block, j, first_column):
            slot, _, split_before = place
            wait(sp, lo_done, split_before)
            sp.dma_start(raw[:, slot, :].rearrange("p (k n) -> p k n", k=2),
                         ada_v[block // ADA_BLOCKS, :, 2 * j:2 * j + 2, bass.ds(first_column, BLOCK)]
                         ).then_inc(raw_in[slot], 16)

        def columns(a, first, column):
            return a[:, :, first:][:, :, bass.ds(column, P)]

        def up(layer, f):
            base = BASES[layer, f"up{f}"][0]
            src = ups[f][layer].rearrange("(k p) n -> p k n", p=P)
            first, other = up_patterns(layer, f)
            block = ADA_OF.get((layer, f"up{f}"))

            def body_of(pattern, base):
                def body(i):
                    if pattern is UP_ADA:
                        ada_column = sp.snap((block - 1) % ADA_BLOCKS * BLOCK + BLOCK * i)
                    for c, (kind, q) in enumerate(pattern):
                        place = raw_place(base, c, i, len(pattern))
                        if kind == "a":
                            ada_chunk(place, block, q, ada_column)
                        else:
                            load(place, columns(src, q // 2 * P + q % 2 * FH, 2 * i * P), KD)
                return body
            body_of(first, base)(0)
            if f == 0:
                wait(sp, chunk_used, BASES[layer, "up0"][0])
                sp.dma_start(wg_in[:, :, :], w_in[layer, :, MG_COL:MG_COL + 16].rearrange("(k p) n -> p k n", p=P)
                             ).then_inc(wg_landed, 16)
            run_from_1(sp, CH_UP // 4, body_of(other, round_base(base, first, other)))

        def down(layer, f):
            base = BASES[layer, f"down{f}"][0]
            src = downs[f][layer].rearrange("(k p) n -> p k n", p=P)

            first, other = down_patterns(layer, f)
            block = ADA_OF.get((layer, f"down{f}"))

            def body_of(pattern, base):
                def body(i):
                    if pattern is DOWN_ADA:
                        ada_column = block % ADA_BLOCKS * BLOCK + BLOCK * i
                        ada_column = ada_column if isinstance(i, int) else sp.snap(ada_column)
                    for c, (kind, q) in enumerate(pattern):
                        place = raw_place(base, c, i, len(pattern))
                        if kind == "a":
                            ada_chunk(place, block, q, ada_column)
                            continue
                        ks = DOWN_K[q % 4]
                        load(place, columns(src[:, ks[0]:ks[-1] + 1, :], q // 4 * P, 2 * i * P), len(ks))
                return body
            body_of(first, base)(0)
            run_from_1(sp, KD // 2, body_of(other, round_base(base, first, other)))

        def mixer(layer):
            base = BASES[layer, "proj"][0]
            src = w_in[layer].rearrange("(k p) n -> p k n", p=P)
            for step in ORDERS[layer]:
                if step[0] == "ada":
                    block = ADA_OF[layer, "proj"] + step[1]
                    r = base + PLANS[layer][step][0]
                    ada_chunk(raw_place(r, 0), block, step[2], block % ADA_BLOCKS * BLOCK)
                elif step[0] in EVAC_ENGINE:
                    r = base + PLANS[layer][step][0]
                    col = in_col(SEC[step[0]] + step[1])
                    load(raw_place(r, 0), src[:, :, col:col + P], KD)
            base = BASES[layer, "gate"][0]
            pattern = gate_pattern(layer)
            block = ADA_OF.get((layer, "gate"))

            def body(i):
                after = sp.snap(i + 1)
                if block is not None:
                    ada_column = sp.snap(block % ADA_BLOCKS * BLOCK + BLOCK * i)
                for c, (kind, q) in enumerate(pattern):
                    place, e = raw_place(base, c, i, len(pattern)), q // 6
                    if kind == "a":
                        ada_chunk(place, block, q, ada_column)
                    elif q % 2 == 0:
                        first = e * P + in_col(SEC[("gs", "gm", "gd")[(q // 2) % 3]])
                        load(place, columns(src, first, 2 * i * P), KD)
                    else:
                        w, kn = ((w_sc, 4), (w_ml, 8), (w_da, 4))[(q // 2) % 3]
                        load(place, columns(w[layer].rearrange("(k p) n -> p k n", p=P), e * P, 2 * P * after - 2 * P), kn)
            if base == LATE:
                sp.wait_ge(lo_done, LATE)
                sp.wait_ge(h_ready, KD * 5)
            run(sp, KD // 2, body)
            base = BASES[layer, "wo"][0]
            srco = w_o[layer].rearrange("(k p) n -> p k n", p=P)

            def body_o(i):
                for e in range(4):
                    load(raw_place(base, e, i, 4), columns(srco, e * P, 4 * i * P), KD)
            run(sp, KD // 4, body_o)

        for layer in range(DEPTH):
            up(layer, 0)
            down(layer, 0)
            mixer(layer)
            up(layer, 1)
            down(layer, 1)
        for q in range(2):
            for s in range(2):
                sp.wait_ge(out_ready, 2 * q + s + 1)
                sp.dma_start(out[0, s * P:(s + 1) * P, q * 512:(q + 1) * 512], y_out[:, s, q * 512:(q + 1) * 512]
                             ).then_inc(out_done, 16)
        sp.wait_ge(out_done, 64)

    @block.tensor
    def _(pe):
        pe.wait_ge(const_in, 16)
        pe.wait_ge(rows_in, 16 * 12)
        for n, r in enumerate((120, 120, 108, 78)):
            pe.transpose(ps[4 + n][:, 0:r], rows[0:r, n, :], ident[0:r, 0:r]).then_inc(rows_turned, 1)

        def turn_x(tiles):
            pe.wait_ge(x_landed, 32)
            for d in tiles:
                if d >= 4:
                    pe.wait_ge(evac_act if d % 2 == 0 else evac_dve, (d - 4) // 2 + 1)
                for t in range(TT):
                    m = pe.transpose(ps[d % 4][:, t * P:(t + 1) * P], x_in[:, t, d * P:(d + 1) * P], ident)
                m.then_inc(x_turned, 1)

        def ada_turn(block, bank, rows_n, pick):
            pe.wait_ge(ada_copied, block + 1)
            for t in range(4):
                m = pe.matmul(ps[bank][:, 2 * t:2 * t + 2], ada_row[0:rows_n, t * P:(t + 1) * P], pick,
                              start=True, stop=True)
            m.then_inc(ada_done, 1)

        pe.wait_ge(cs_ready, 1)
        pe.wait_ge(cols_ready, 4)
        for b in range(4):
            pe.wait_ge(stage_in[b], 64)
            for k in range(KD):
                m = pe.matmul(ps[4 + b][0:2, :], cs[:, k, :], stage[:, 4 * b + k // 2, (k % 2) * BLOCK:(k % 2 + 1) * BLOCK],
                              start=(k == 0), stop=(k == KD - 1))
            m.then_inc(ada_summed, 1)
            if b:
                ada_turn(b - 1, 3 + b, 2, ident[0:2, 0:2])
            if b in (1, 2):
                turn_x(range(4 * b - 4, 4 * b))
        ada_turn(3, 7, 2, ident[0:2, 0:2])

        def ada_chunk(r, slot, block, j):
            pe.wait_ge(lo_done, r + 1)
            if j == 0:
                pe.wait_ge(ada_copied, block)
            for e in range(2):
                stationary = cs_parts[:, 2 * j + e, :]
                for part in (w_hi, w_lo):
                    m = pe.matmul(ps[4][0:4, :], stationary, part[:, slot, e * BLOCK:(e + 1) * BLOCK],
                                  start=(j == 0 and e == 0 and part is w_hi), stop=(j == 3 and e == 1 and part is w_lo))
            m.then_inc(chunk_used, 1)

        def ada_columns(block):
            pe.wait_ge(ada_ev, block)
            ada_turn(block, 5, 4, ada_sum)

        def chunk(r, slot, bank, parts, t0, first=True, last=True, ready=None):
            pe.wait_ge(lo_done, r + 1)
            for n, (a_hi, a_lo) in enumerate(parts):
                wh, wl = w_hi[:, slot, n * P:(n + 1) * P], w_lo[:, slot, n * P:(n + 1) * P]
                a, b = first and n == 0, last and n == len(parts) - 1
                if ready is not None:
                    pe.wait_ge(ready[0], ready[1] + n)
                pe.matmul(ps[bank][:, t0:TOK], wh, a_hi, start=a, stop=False)
                pe.matmul(ps[bank][:, t0:TOK], wh, a_lo, start=False, stop=False)
                m = pe.matmul(ps[bank][:, t0:TOK], wl, a_hi, start=False, stop=b)
            m.then_inc(chunk_used, 1)

        def of(hi, lo, ks, t0):
            return [(hi[:, k, t0:TOK], lo[:, k, t0:TOK]) for k in ks]

        def interleaved(base, n, t0):
            pe.wait_ge(lo_done, base + 4)
            for k in range(KD):
                pe.wait_ge(u_ready, KD * n + k + 1)
                for q in range(4):
                    wh, wl = (w[:, (base + q) % SPLIT, k * P:(k + 1) * P] for w in (w_hi, w_lo))
                    pe.matmul(ps[q][:, t0:TOK], wh, u_hi[:, k, t0:TOK], start=(k == 0), stop=False)
                    pe.matmul(ps[q][:, t0:TOK], wh, u_lo[:, k, t0:TOK], start=False, stop=False)
                    m = pe.matmul(ps[q][:, t0:TOK], wl, u_hi[:, k, t0:TOK], start=False, stop=(k == KD - 1))
                    if k == KD - 1:
                        m.then_inc(chunk_used, 1)

        def up(layer, f, n):
            base, a0, d0 = BASES[layer, f"up{f}"]
            t0 = t0_of(layer) if f else 0
            if n == 0:
                pe.wait_ge(cs_lo_done, 1)
            first, other = up_patterns(layer, f)
            block = ADA_OF.get((layer, f"up{f}"))
            pe.wait_ge(evac_act, a0)
            pe.wait_ge(evac_dve, d0)
            interleaved(base, n, t0)
            base = round_base(base, first, other)
            with pe.Fori(1, CH_UP // 4) as i:
                for c, (kind, q) in enumerate(other):
                    r = base + c + len(other) * i
                    slot = (base + c) % SPLIT
                    if kind == "a":
                        ada_chunk(r, slot, block - 1 + i, q)
                        continue
                    pe.wait_ge(evac_act if q % 2 == 0 else evac_dve, (a0 if q % 2 == 0 else d0) - 1 + 2 * i + q // 2)
                    chunk(r, slot, q, of(u_hi, u_lo, range(KD), t0), t0)
                if other is UP_ADA:
                    ada_columns(block - 1 + i)

        def down(layer, f):
            base, a0, d0 = BASES[layer, f"down{f}"]
            t0 = t0_of(layer) if f else 0
            pe.wait_ge(evac_act, a0 - 1)
            pe.wait_ge(evac_dve, d0 - 1)

            first, other = down_patterns(layer, f)
            block = ADA_OF.get((layer, f"down{f}"))

            def body_of(pattern, base, start=False):
                def body(i):
                    for c, (kind, q) in enumerate(pattern):
                        r, slot = base + c + len(pattern) * i, (base + c) % SPLIT
                        if kind == "a":
                            ada_chunk(r, slot, block + i, q)
                            continue
                        if start and q < 4:
                            pe.wait_ge(g_ready, KF * (2 * layer + f) + DOWN_K[q][-1] + 1)
                        if q % 4 == 0:
                            pe.wait_ge(evac_dve, d0 - 1 + 2 * i + q // 4)
                        chunk(r, slot, q // 4, of(g_hi, g_lo, DOWN_K[q % 4], t0), t0,
                              first=(q % 4 == 0), last=(q % 4 == 3))
                    if pattern is DOWN_ADA:
                        ada_columns(block + i)
                return body
            body_of(first, base, start=True)(0)
            run_from_1(pe, KD // 2, body_of(other, round_base(base, first, other)))

        def norm(n):
            t0 = norm_t0(n)
            k0 = KD * (n - 1)
            pe.wait_ge(sum_done, (KD - 1) * n)
            pe.matmul(ps[6][:, t0:TOK], mean_w, scr[5][:, t0:TOK], start=True, stop=False)
            pe.wait_ge(evac_dve, norm_d(n))
            pe.matmul(ps[6][:, t0:TOK], mean_w, h[:, KD - 1, t0:TOK], start=False, stop=True).then_inc(ln_mean, 1)
            for k in range(KD):
                pe.wait_ge(ln_sq, k0 + k + 1)
                pe.matmul(ps[7][:, t0:TOK], mean_w, scr[k % 2][:, t0:TOK], start=(k == 0),
                          stop=(k == KD - 1)).then_inc(ln_sq_used, 1)

        def proj(layer, step):
            r, n, _, _ = PLANS[layer][step]
            base, a0, d0 = BASES[layer, "proj"]
            t0 = t0_of(layer, step[0] in X_ONLY)
            if n >= 4:
                before = NTH_PROJ[n - 4]
                by = EVAC_ENGINE[before[0]]
                _, _, a, d = PLANS[layer][before]
                pe.wait_ge(evac_act if by == "act" else evac_dve, (a0 + a if by == "act" else d0 + d) + 1)
                chunk(base + r, (base + r) % SPLIT, n % 4, of(u_hi, u_lo, range(KD), t0), t0)
            elif n == 3:
                interleaved(base, 3 * layer + 1, t0)

        def turn_v(layer, v):
            kind, i = ("mv", v) if v < 8 else ("dv", v - 8)
            pe.wait_ge(evac_act, BASES[layer, "proj"][1] + PLANS[layer][kind, i][2] + 1)
            g = 12 * layer + v
            wait(pe, v_placed, g - 1)
            if v == 0:
                pe.wait_ge(gate_act, 5 * layer + 1)
            if v == 8:
                pe.wait_ge(ht_ready, HEADS * (layer + 1))
            for t in range(TT):
                m = pe.transpose(ps[value_bank(v)][:, t * P:(t + 1) * P], scr[4 + v % 2][:, t * P:(t + 1) * P], ident)
            m.then_inc(v_turned, 1)

        def rope(layer, i):
            kind = ("dq", i) if i < 4 else ("dk", i - 4)
            pe.wait_ge(evac_act, BASES[layer, "proj"][1] + PLANS[layer][kind][2] + 1)
            g = 8 * layer + ROPES.index(i)
            wait(pe, rope_done, g - 1)
            pe.matmul(ps[6 + g % 2][:, 0:SEG], rot_w, dqk[:, i, SEG:TOK], start=True, stop=True
                      ).then_inc(rot_done, 1)

        def gates(layer):
            pe.wait_ge(wg_ready, layer + 1)
            for k in range(KD):
                for n, (w, a) in enumerate(((wg_hi, u_hi), (wg_hi, u_lo), (wg_lo, u_hi))):
                    m = pe.matmul(ps[6][:, :], w[:, k, :], a[:, k, :], start=(n == 0 and k == 0),
                                  stop=(n == 2 and k == KD - 1))
            m.then_inc(mg_done, 1)

        def gates_turn(layer):
            pe.wait_ge(gate_dve, layer + 1)
            pe.wait_ge(v_placed, 12 * layer + 8)
            for t in range(TT):
                m = pe.transpose(ps[7][:, t * P:(t + 1) * P], gt[0][:, t * P:(t + 1) * P], ident)
            m.then_inc(gate_turn, 1)

        def ml_scores(layer, head, s):
            t0 = t0_of(layer)
            u = HEADS * layer + head
            if s == 0:
                pe.wait_ge(v_placed, 12 * layer + 8)
                pe.wait_ge(gate_act, 5 * layer + 5)
                wait(pe, ht_ready, u)
                if head == 0 and (layer, "proj") in ADA_OF:
                    pe.wait_ge(ada_ev, ADA_OF[layer, "proj"] + PROJ_ADA)
                for n in range(2):
                    row = 32 * n + head
                    m = pe.matmul(ps[4 + n][:, t0:TOK], ident[:, row:row + 1].to_broadcast([P, P]),
                                  neg_g[:, t0:TOK], start=True, stop=True)
                m.then_inc(ng_ready, 1)
                base, a0, d0 = BASES[layer, "proj"]
                pe.wait_ge(evac_act, a0 + PLANS[layer]["mq", head][2] + 1)
                pe.wait_ge(evac_dve, d0 + PLANS[layer]["mk", head][3] + 1)
                wait(pe, hsum_ready, nth_out(layer, head, 0))
            else:
                if s >= 2:
                    pe.wait_ge(pw_ready, 8 * u + 2 * (s - 1))
            ts = max(t0, SEG if s >= 2 else 0)
            pe.matmul(ps[6 + s % 2][:, ts:TOK], kt[:, head, s * P:(s + 1) * P], qt[:, head, ts:TOK],
                      start=True, stop=True).then_inc(s_ready, 1)

        def turn_h(layer, head, t):
            nt = nth_out(layer, head, t)
            pe.wait_ge(hsum_ready, nt + 1)
            for e in range(2):
                m = pe.transpose(ps[4 + e][:, t * P:(t + 1) * P], hs[:, t % 2, e * P:(e + 1) * P], ident)
            m.then_inc(h_turned, 1)

        def ml_numerator(layer, head, t):
            first = t0_of(layer) // P
            if t < first:
                return
            u = HEADS * layer + head
            pe.wait_ge(pw_ready, 8 * (u + 1))
            if t > first:
                pe.wait_ge(hsum_ready, nth_out(layer, head, t))
            for n, w in enumerate("fb"):
                keys = KEYS[w, t]
                for s in keys:
                    m = pe.matmul(ps[6 + n][:, 0:257], pw[:, n, s, t * P:(t + 1) * P], vaug[:, s, head, :],
                                  start=(s == keys[0]), stop=(s == keys[-1]))
            m.then_inc(num_ready, 1)
            if t > first:
                turn_h(layer, head, t - 1)

        def attend(layer):
            tiles = range(t0_of(layer) // P, TT)
            base, a0, d0 = BASES[layer, "gate"]
            pe.wait_ge(evac_act, a0)
            pe.wait_ge(evac_dve, d0)
            units, u0 = attention_units(layer)

            def scores(v):
                head, t, keys = units[v]
                wait(pe, p_ready, 2 * (u0 + v - 1) if v >= 2 else 0)
                if v < HEADS:
                    pe.wait_ge(rope_done, 8 * layer + 2 * (head + 1))
                if v == 1:
                    pe.wait_ge(v_placed, 12 * (layer + 1))
                for j in range(2):
                    queries = (q_first if j == 0 else dqk)[:, head, t * P:(t + 1) * P]
                    pe.matmul(ps[SCORE_BANK[v % 2] + j][:, 0:len(keys) * P], queries,
                              dqk[:, 4 + head, 0:len(keys) * P], start=True, stop=True).then_inc(sc_ready, 1)

            def turn_weights(v):
                head, t, keys = units[v]
                pe.wait_ge(wgt_ready, u0 + v + 1)
                wait(pe, wt_ready, u0 + v - 1 if v >= 2 else 0)
                for k in keys:
                    m = pe.transpose(ps[6 - 4 * (v % 2)][:, k * P:(k + 1) * P], wgt[v % 2][:, k * P:(k + 1) * P], ident)
                m.then_inc(wgt_turned, 1)

            def outputs(v):
                head, t, keys = units[v]
                pe.wait_ge(wt_ready, u0 + v + 1)
                wait(pe, o_copied, u0 + v - 1 if v >= 2 else 0)
                for k in keys:
                    m = pe.matmul(ps[7 - 4 * (v % 2)][:, 0:P], wgt_t[v % 2][:, k * P:(k + 1) * P], dav[:, k, head, :],
                                  start=(k == keys[0]), stop=(k == keys[-1]))
                m.then_inc(o_ready, 1)
            scores(0)
            for v in range(len(units)):
                if v + 1 < len(units):
                    scores(v + 1)
                turn_weights(v)
                if v:
                    outputs(v - 1)
            outputs(len(units) - 1)

        def attention_outputs(layer):
            for head in range(HEADS):
                pe.wait_ge(o_scaled, HEADS * layer + head + 1)
                wait(pe, yda_f, 4 * layer + head - 1)
                for t in range(t0_of(layer) // P, TT):
                    m = pe.transpose(ps[6 + head % 2][:, t * P:(t + 1) * P], oda[:, t, head, :], ident)
                m.then_inc(o_turned, 1)

        def mixer(layer):
            t0 = t0_of(layer)
            pe.wait_ge(evac_dve, BASES[layer, "proj"][2])
            for step in ORDERS[layer]:
                if step[0] in EVAC_ENGINE:
                    proj(layer, step)
                elif step[0] == "ada":
                    r = BASES[layer, "proj"][0] + PLANS[layer][step][0]
                    ada_chunk(r, r % SPLIT, ADA_OF[layer, "proj"] + step[1], step[2])
                elif step[0] == "adat":
                    ada_columns(ADA_OF[layer, "proj"] + step[1])
                elif step[0] == "attend":
                    attend(layer)
                elif step == ("gates", 0):
                    gates(layer)
                elif step[0] == "ml_gates":
                    gates_turn(layer)
                elif step[0] == "ml_t":
                    turn_h(layer, step[1], TT - 1)
                elif step[0] in ("ml_s", "ml_n"):
                    (ml_scores if step[0] == "ml_s" else ml_numerator)(layer, *step[1:])
                elif step[0] in ("turn_v", "rope"):
                    {"turn_v": turn_v, "rope": rope}[step[0]](layer, step[1])
            base, a0, d0 = BASES[layer, "gate"]
            pe.wait_ge(evac_act, a0)
            pe.wait_ge(evac_dve, d0)
            pe.wait_ge(y_ready, 12 * (layer + 1))
            units, u0 = attention_units(layer)
            units_done = u0 + len(units)
            pattern = gate_pattern(layer)
            block = ADA_OF.get((layer, "gate"))

            def body(i):
                for c, (kind, q) in enumerate(pattern):
                    if kind == "a":
                        ada_chunk(base + c + len(pattern) * i, (base + c) % SPLIT, block + i, q)
                        continue
                    if q == 5:
                        pe.wait_ge(yda_ready, 4 * (layer + 1))
                    pe.wait_ge(evac_act if q % 2 == 0 else evac_dve, (a0 if q % 2 == 0 else d0) - 1 + 6 * i + q // 2)
                    if q % 2 == 0:
                        parts = of(u_hi, u_lo, range(KD), t0)
                    else:
                        hi, lo, kn = ((ysc_hi, ysc_lo, 4), (yml_hi, yml_lo, 8), (yda_hi, yda_lo, 4))[(q // 2) % 3]
                        parts = of(hi, lo, range(kn), t0)
                    if isinstance(i, int) and q in (0, 2, 3):
                        pe.wait_ge(*{0: (p_ready, 2 * units_done), 2: (wt_ready, units_done), 3: (o_copied, units_done)}[q])
                    chunk(base + c + len(pattern) * i, (base + c) % SPLIT, q % 4, parts, t0)
                    if isinstance(i, int) and q == 0:
                        attention_outputs(layer)
                if block is not None:
                    ada_columns(block + i)
            run(pe, KD // 2, body, peel_first=True)
            base, a0, d0 = BASES[layer, "wo"]
            def body_o(i):
                for e in range(4):
                    if isinstance(i, int):
                        pe.wait_ge(*((evac_act, a0 - 1), (evac_dve, d0 - 1), (evac_act, a0), (evac_dve, d0))[e])
                    else:
                        pe.wait_ge(evac_dve, d0 - 3 + 4 * i + e)
                    chunk(base + 4 * i + e, (base + e) % SPLIT, e, of(z_hi, z_lo, range(KD), t0), t0,
                          ready=(z_ready, KD * layer + 1) if isinstance(i, int) and e == 0 else None)
            run(pe, KD // 4, body_o, peel_first=True)

        for layer in range(DEPTH):
            up(layer, 0, 3 * layer)
            down(layer, 0)
            norm(3 * layer + 1)
            mixer(layer)
            norm(3 * layer + 2)
            up(layer, 1, 3 * layer + 2)
            down(layer, 1)
            norm(3 * layer + 3)
        for q in range(2):
            pe.wait_ge(h_ready, KD * 6 + 4 * (q + 1))
            for s in range(2):
                n = 2 * q + s
                for k in range(4):
                    m = pe.transpose(ps[n][:, k * P:(k + 1) * P], h[:, 4 * q + k, SEG + s * P:SEG + (s + 1) * P], ident)
                m.then_inc(out_turned, 1)

    @block.scalar
    def _(act):
        chain = [0]

        def link(ins):
            chain[0] += 1
            ins.then_inc(act_chain, 1)
            act.wait_ge(act_chain, chain[0])

        def split(r, slot, place):
            wait(act, chunk_used, r - SPLIT + 1)
            raw_slot, landed, _ = place
            act.wait_ge(raw_in[raw_slot], landed)
            act.activation(split_tiles(w_hi, slot), raw_tiles(raw_slot), ACT.Copy).then_inc(hi_done, 1)

        def ahead(base, c, i=0, step=0):
            r = base + c + SPLIT
            if isinstance(i, int) and r + step * i >= CHUNKS:
                return
            split(r + step * i, r % SPLIT, raw_place(base, c + SPLIT, i, step))

        for a, tile, r0, n in VECTOR_ROWS[0::2]:
            act.dma_start(rows[r0:r0 + n, tile, :], a).then_inc(rows_in, 16)
        act.wait_ge(cols_ready, 4)
        act.activation(cs[:, :, 0], cols[:, 3, 60:68], ACT.Silu)
        link(act.activation(cs[:, :, 1], cols[:, 3, 68:76], ACT.Silu))
        act.activation(cs_parts[:, :, 0:2], cs[:, :, :], ACT.Copy).then_inc(cs_ready, 1)
        for n, a in enumerate((lam_q1, lam_k1, lam_q2, lam_k2)):
            act.dma_start(lam_in[:, :, n, :], a.rearrange("l d -> (l d)").partition_broadcast(P)
                          .rearrange("p (l d) -> p l d", l=DEPTH)).then_inc(lam_landed, 16)
        act.wait_ge(zeroed, 2)
        for layer in range(DEPTH):
            for q in range(4):
                act.dma_start(gate_bias[32 * q:32 * q + 4, layer:layer + 1],
                              b_in[layer, MG_COL + 4 * q:MG_COL + 4 * q + 4].rearrange("(p a) -> p a", a=1)
                              ).then_inc(gate_in, 16)
        for half in range(2):
            for d in range(4 * half, 4 * half + 4, 2):
                act.wait_ge(x_turned, d + 1)
                act.activation(h[:, d, :], ps[d % 4][:, :], ACT.Copy).then_inc(evac_act, 1)
            for r in range(2 * half, 2 * half + 2):
                split(r, r, raw_place(r, 0))
            if half == 0:
                act.wait_ge(lam_dot, 1)
                act.activation(lam_e[:, :, :], lam_e[:, :, :], ACT.Exp).then_inc(lam_exp, 1)

        def modulate(n):
            t0 = norm_t0(n)
            act.wait_ge(cols_mod, n + 1)
            if n == 0:
                act.wait_ge(evac_act, 4)
                act.wait_ge(evac_dve, 4)
            last = None
            for k in range(KD + 1):
                if k < KD and n < 6:
                    if n:
                        act.wait_ge(ln_xn, KD * (n - 1) + k + 1)
                    for s, seg in halves(t0):
                        m = act.activation(u_hi[:, k, seg], h[:, k, seg], ACT.Identity,
                                           scale=mod_a[:, k, s:s + 1], bias=mod_b[:, k, s:s + 1])
                    m.then_inc(u_hi_done, 1)
                j = k - 1 if n < 6 else k
                if 0 <= j < KD:
                    if n < 6:
                        act.wait_ge(u_ready, KD * n + j + 1)
                    else:
                        act.wait_ge(ln_xn, KD * (n - 1) + j + 1)
                    act.activation(h[:, j, t0:TOK], h[:, j, t0:TOK], ACT.Identity, scale=res_g[:, j:j + 1],
                                   bias=res_b[:, j:j + 1]).then_inc(h_ready, 1)

        def norm(n):
            t0 = norm_t0(n)
            k0 = KD * (n - 1)
            act.activation(small[:, 15:16], small[:, 0:1], ACT.Sqrt)
            for k in range(KD):
                act.wait_ge(ln_cent, k0 + k + 1)
                wait(act, ln_sq_used, k0 + k - 1)
                act.activation(scr[k % 2][:, t0:TOK], h[:, k, t0:TOK], ACT.Square).then_inc(ln_sq, 1)
            act.wait_ge(ln_sq_used, k0 + KD)
            act.activation(scr[2][:, t0:TOK], ps[7][:, t0:TOK], ACT.Sqrt, bias=small[:, 0:1]).then_inc(ln_std, 1)
            modulate(n)

        def up(layer, f):
            base, a0, d0 = BASES[layer, f"up{f}"]
            t0 = t0_of(layer) if f else 0

            first, other = up_patterns(layer, f)

            def body_of(pattern, base):
                def body(i):
                    for c, (kind, q) in enumerate(pattern):
                        ahead(base, c, i, len(pattern))
                        if kind == "a":
                            continue
                        act.wait_ge(chunk_used, base + c + 1 + len(pattern) * i)
                        if q % 2 == 0:
                            act.wait_ge(evac_dve, d0 - 1 + 2 * i + q // 2)
                            act.activation(scr[q // 2][:, t0:TOK], ps[q][:, t0:TOK], ACT.Silu).then_inc(evac_act, 1)
                        else:
                            act.wait_ge(evac_dve, d0 + 1 + 2 * i + q // 2)
                            act.activation(g_hi[:, 2 * i + q // 2, t0:TOK], scr[2 + q // 2][:, t0:TOK], ACT.Copy
                                           ).then_inc(g_hi_done, 1)
                return body
            body_of(first, base)(0)
            run_from_1(act, CH_UP // 4, body_of(other, round_base(base, first, other)))

        def down(layer, f):
            base = BASES[layer, f"down{f}"][0]
            first, other = down_patterns(layer, f)
            for c in range(len(first)):
                ahead(base, c)
            base = round_base(base, first, other)

            def body(i):
                for c in range(len(other)):
                    ahead(base, c, i, len(other))
            run_from_1(act, KD // 2, body, peel_last=(layer, f) == (DEPTH - 1, 1))

        def split_y(y, src, hi, k, t0):
            act.wait_ge(yf_ready, y + 1)
            act.activation(hi[:, k, t0:TOK], src[:, t0:TOK], ACT.Copy).then_inc(y_hi_done, 1)

        def proj(layer, step):
            kind, i = step
            base, a0, d0 = BASES[layer, "proj"]
            r, n, a, d = PLANS[layer][step]
            t0 = t0_of(layer, kind in X_ONLY)
            ahead(base, r)
            if kind in ("sx", "mk"):
                return
            y = y_number(layer, kind, i)
            if kind == "sb":
                split_y(y, scr[2 + y % 2], ysc_hi, i, t0)
                return
            act.wait_ge(chunk_used, base + r + 1)
            ct, cc = bias_at(layer, SEC[kind] + i)
            bias = cols[:, ct, cc:cc + 1]
            if kind == "cg":
                dst, func = cgt[:, t0:TOK], ACT.Identity
                if i:
                    act.wait_ge(evac_dve, d0 + PLANS[layer]["sx", i - 1][3] + 1)
            elif kind == "mq":
                dst, func = qt[:, i, t0:TOK], ACT.Identity
            elif kind in ("mv", "dv"):
                v = i if kind == "mv" else 8 + i
                wait(act, v_turned, 12 * layer + v - 1)
                if v in (8, 9):
                    act.wait_ge(yf_ready, y_number(layer, "sb", 3) + 1)
                dst, func = scr[4 + v % 2][:, t0:TOK], ACT.Identity
            elif kind == "mo":
                dst, func = scr[i % 2][:, t0:TOK], ACT.Sigmoid
                act.wait_ge(yf_ready, y - 1 if i >= 2 else y_number(layer, "sb", 3) + 1)
            else:
                act.wait_ge(s_ready, TT * (HEADS * layer + i + 1))
                dst, func = dqk[:, i if kind == "dq" else 4 + i, t0:TOK], ACT.Identity
            act.activation(dst, ps[n % 4][:, t0:TOK], func, bias=bias).then_inc(evac_act, 1)

        def gates(layer, part):
            if part == 0:
                act.wait_ge(mg_done, layer + 1)
                act.wait_ge(gate_in, 16 * 4 * DEPTH)
                act.activation(gt[1][:, :], ps[6][:, :], ACT.Identity, bias=gate_bias[:, layer:layer + 1]
                               ).then_inc(gate_act, 1)
            elif part == 1:
                act.wait_ge(gate_abs, layer + 1)
                link(act.activation(gt[3][64:128, :], gt[3][64:128, :], ACT.Exp, scale=-1.0))
                act.activation(gt[3][64:128, :], gt[3][64:128, :], ACT.Ln, bias=1.0).then_inc(gate_act, 1)

        def ml_gates(layer):
            act.wait_ge(gate_turn, layer + 1)
            turned = ps[7][:, :].rearrange("p (t n) -> p t n", t=TT)
            act.activation(am[:, :, :], turned, ACT.Copy).then_inc(gate_act, 1)
            act.activation(nam[:, :, :], turned[:, :, 0:64], ACT.Copy, scale=-1.0).then_inc(gate_act, 1)
            act.activation(em[:, :, :], turned[:, :, 64:128], ACT.Exp, scale=-1.0).then_inc(gate_act, 1)

        def ml_scores(layer, head, s):
            t0 = t0_of(layer)
            u = HEADS * layer + head
            if s == 0:
                act.wait_ge(ng_ready, u + 1)
                if head == 0:
                    act.wait_ge(gate_act, 5 * layer + 5)
            for n in range(2):
                v = 2 * s + n
                row = 32 * n + head
                found, diag = segments(s, n, t0)
                wait(act, pw_ready, 8 * u + v - 1 if v >= 2 else 8 * u)
                for b, e in found:
                    cuts = [(b, e)]
                    if diag is not None and b <= diag * P < e:
                        own = slice(diag * P, (diag + 1) * P)
                        link(act.activation(xt[:, n, own], ps[4 + n][:, own], ACT.Relu, scale=-1.0,
                                            bias=nam[:, s, row:row + 1]))
                        m = act.activation(xt[:, n, own], xt[:, n, own], ACT.Exp, scale=-1.0)
                        cuts = [(b, diag * P), ((diag + 1) * P, e)]
                    for cb, ce in cuts:
                        if cb < ce:
                            m = act.activation(xt[:, n, cb:ce], ps[4 + n][:, cb:ce], ACT.Exp,
                                               bias=am[:, s, row:row + 1])
                m.then_inc(e_ready, 1)

        def ml_turned(layer, head):
            t0 = t0_of(layer)
            act.wait_ge(h_turned, nth_out(layer, head, TT - 1) + 1)
            for e in range(2):
                m = act.activation(ht[:, 2 * head + e, t0:TOK], ps[4 + e][:, t0:TOK], ACT.Copy)
            m.then_inc(ht_ready, 1)

        def attend(layer):
            units, u0 = attention_units(layer)

            def probabilities(v):
                nk = len(units[v][2]) * P
                for j in range(2):
                    act.wait_ge(smax_ready, 2 * (u0 + v) + j + 1)
                    if j == 0 and v >= 2:
                        act.wait_ge(wgt_ready, u0 + v - 1)
                    act.activation(scr[2 * (v % 2) + j][:, 0:nk], ps[SCORE_BANK[v % 2] + j][:, 0:nk], ACT.Exp,
                                   scale=DA_HALF ** -0.5, bias=att[:, v % 2, j:j + 1],
                                   accum_out=att[:, v % 2, 2 + j:3 + j]).then_inc(p_ready, 1)

            def weights(v):
                nk = len(units[v][2]) * P
                act.wait_ge(wgt_turned, u0 + v + 1)
                if v >= 2:
                    act.wait_ge(o_ready, u0 + v - 1)
                act.activation(wgt_t[v % 2][:, 0:nk], ps[6 - 4 * (v % 2)][:, 0:nk], ACT.Copy).then_inc(wt_ready, 1)

            def squares(v):
                head, t, _ = units[v]
                act.wait_ge(o_copied, u0 + v + 1)
                wait(act, o_sq, u0 + v)
                act.activation(junk[:, :], oda[:, t, head, :], ACT.Square, accum_out=ssq[:, t, head:head + 1]
                               ).then_inc(o_sq, 1)
            probabilities(0)
            for v in range(len(units)):
                if v + 1 < len(units):
                    probabilities(v + 1)
                weights(v)
                if v:
                    squares(v - 1)
            squares(len(units) - 1)
            first = t0_of(layer) // P
            act.wait_ge(o_sq, u0 + len(units))
            act.activation(ssq[:, first:TT, :], ssq[:, first:TT, :], ACT.Sqrt, scale=1.0 / P, bias=small[:, 0:1]
                           ).then_inc(o_std, 1)
            for head in range(HEADS):
                act.wait_ge(yda_f, 4 * layer + head + 1)
                act.activation(yda_hi[:, head, first * P:TOK], scr[2 + head % 2][:, first * P:TOK], ACT.Copy
                               ).then_inc(yda_h, 1)

        def mixer(layer):
            t0 = t0_of(layer)
            for step in ORDERS[layer]:
                if step[0] in EVAC_ENGINE:
                    proj(layer, step)
                elif step[0] == "ada":
                    ahead(BASES[layer, "proj"][0], PLANS[layer][step][0])
                elif step[0] == "gates":
                    gates(layer, step[1])
                elif step[0] == "ml_gates":
                    ml_gates(layer)
                elif step[0] == "ml_s":
                    ml_scores(layer, *step[1:])
                elif step[0] == "ml_t":
                    ml_turned(layer, step[1])
                elif step[0] == "ysplit":
                    split_y(y_number(layer, "mo", step[1]), ht[:, step[1], :], yml_hi, step[1], t0)
                elif step[0] == "attend":
                    attend(layer)
            base, a0, d0 = BASES[layer, "gate"]
            pattern = gate_pattern(layer)

            def body(i):
                for c, (kind, q) in enumerate(pattern):
                    ahead(base, c, i, len(pattern))
                    if kind == "a":
                        continue
                    if q % 2 == 0:
                        act.wait_ge(chunk_used, base + c + 1 + len(pattern) * i)
                        act.wait_ge(evac_dve, d0 - 1 + 6 * i + q // 2)
                        tile = SEC[("gs", "gm", "gd")[(q // 2) % 3]] + q // 6
                        ct, cc = bias_at(layer, tile)
                        act.activation(scr[(q // 2) % 2][:, t0:TOK], ps[q % 4][:, t0:TOK], ACT.Sigmoid,
                                       bias=cols[:, ct, bass.ds(cc + 2 * i, 1)]).then_inc(evac_act, 1)
                    elif q % 6 == 5:
                        act.wait_ge(z_sum, 2 * i + (KD * layer + q // 6 + 1))
                        act.activation(z_hi[:, 2 * i + q // 6, t0:TOK], scr[2 + q // 6][:, t0:TOK], ACT.Copy
                                       ).then_inc(z_hi_done, 1)
            run(act, KD // 2, body)
            base = BASES[layer, "wo"][0]

            def body_o(i):
                for e in range(4):
                    ahead(base, e, i, 4)
            run(act, KD // 4, body_o)

        modulate(0)
        for layer in range(DEPTH):
            up(layer, 0)
            down(layer, 0)
            norm(3 * layer + 1)
            mixer(layer)
            norm(3 * layer + 2)
            up(layer, 1)
            down(layer, 1)
            norm(3 * layer + 3)
        for q in range(2):
            for s in range(2):
                act.wait_ge(out_turned, 2 * q + s + 1)
                act.activation(y_out[:, s, q * 512:(q + 1) * 512], ps[2 * q + s][:, :], ACT.Copy
                               ).then_inc(out_ready, 1)

    @block.vector
    def _(dve):
        chain = [0]

        def link(ins):
            chain[0] += 1
            ins.then_inc(dve_chain, 1)
            dve.wait_ge(dve_chain, chain[0])

        def split(r, slot, place):
            dve.wait_ge(hi_done, r + 1)
            wait(dve, chunk_used, r - SPLIT + 1)
            dve.tensor_tensor(split_tiles(w_lo, slot), raw_tiles(place[0]), split_tiles(w_hi, slot).bitcast(F32),
                              ALU.subtract
                              ).then_inc(lo_done, 1)

        def ahead(base, c, i=0, step=0):
            r = base + c + SPLIT
            if isinstance(i, int) and r + step * i >= CHUNKS:
                return
            split(r + step * i, r % SPLIT, raw_place(base, c + SPLIT, i, step))

        dve.memset(gate_bias[:, :], 0.0).then_inc(zeroed, 1)
        dve.memset(one_zero[:, 0, :], 1.0)
        dve.memset(one_zero[:, 1, :], 0.0)
        link(dve.memset(small[:, 0:1], EPS))
        dve.memset(small[:, 1:2], 0.0).then_inc(zeroed, 1)
        for n, r in enumerate((120, 120, 108, 78)):
            dve.wait_ge(rows_turned, n + 1)
            dve.tensor_copy(cols[:, n, 0:r], ps[4 + n][:, 0:r]).then_inc(cols_ready, 1)
        def ada_copy(block, bank, n):
            wait(dve, ada_done, block)
            dve.tensor_copy(ada_row[0:n, :], ps[bank][0:n, :]).then_inc(ada_copied, 1)

        def ada_add(block, bank, layer):
            dve.wait_ge(ada_done, block + 1)
            first = 4 * block - layer * MODT
            m0 = 4 * block
            if isinstance(block, int):
                bias, dst = cols[:, layer, first:first + 4], mods[:, m0:m0 + 4, :]
            else:
                bias, dst = cols[:, layer, bass.ds(first, 4)], mods[:, bass.ds(m0, 4), :]
            dve.tensor_tensor(dst, ps[bank][:, 0:8].rearrange("p (t s) -> p t s", s=2),
                              bias.unsqueeze(2).to_broadcast([P, 4, 2]), ALU.add).then_inc(ada_ev, 1)

        def place_x(tiles):
            for d in tiles:
                dve.wait_ge(x_turned, d + 1)
                dve.tensor_copy(h[:, d, :], ps[d % 4][:, :]).then_inc(evac_dve, 1)

        def first_block(b):
            dve.wait_ge(ada_summed, b + 1)
            ada_copy(b, 4 + b, 2)
            ada_add(b, 4 + b, 0)

        dve.wait_ge(cs_ready, 1)
        dve.tensor_tensor(cs_parts[:, :, 2:4], cs[:, :, :], cs_parts[:, :, 0:2].bitcast(F32), ALU.subtract
                          ).then_inc(cs_lo_done, 1)
        first_block(0)
        dve.wait_ge(lam_landed, 64)
        for layer in range(DEPTH):
            link(dve.tensor_tensor(lam_p[:, layer], lam_in[:, layer, 0:4:2, :], lam_in[:, layer, 1:4:2, :], ALU.mult))
        dve.tensor_reduce(lam_e[:, :, :], lam_p[:, :, :, :], AXX, ALU.add).then_inc(lam_dot, 1)
        for b in (1, 2):
            dve.wait_ge(ada_summed, b + 1)
            ada_copy(b, 4 + b, 2)
            place_x((4 * b - 3, 4 * b - 1))
            if b == 1:
                ada_add(b, 4 + b, 0)
            for r in (2 * b - 2, 2 * b - 1):
                split(r, r, raw_place(r, 0))
        ada_add(2, 6, 0)
        first_block(3)

        def lambdas():
            dve.wait_ge(lam_exp, 1)
            for layer in range(DEPTH):
                lam_init = 0.8 - 0.6 * math.exp(-0.3 * layer)
                link(dve.tensor_tensor(neg_lam[:, layer:layer + 1], lam_e[:, layer, 1:2], lam_e[:, layer, 0:1], ALU.subtract))
                link(dve.tensor_scalar(neg_lam[:, layer:layer + 1], neg_lam[:, layer:layer + 1], -lam_init, None, ALU.add))

        def columns(n):
            g, b = norm_cols(n)
            if n == 6:
                dve.tensor_copy(res_g[:, :], g)
                link(dve.tensor_copy(res_b[:, :], b))
            else:
                m0 = next_mods(n)
                shift, scale = mods[:, m0:m0 + KD, :], mods[:, m0 + KD:m0 + 2 * KD, :]
                for s in range(2):
                    link(dve.scalar_tensor_tensor(mod_a[:, :, s], scale[:, :, s], 1.0, g, ALU.add, ALU.mult))
                    link(dve.scalar_tensor_tensor(mod_b[:, :, s], scale[:, :, s], 1.0, b, ALU.add, ALU.mult))
                    link(dve.tensor_tensor(mod_b[:, :, s], mod_b[:, :, s], shift[:, :, s], ALU.add))
                dve.tensor_scalar(res_g[:, :], g, ALPHA, None, ALU.mult)
                link(dve.tensor_scalar(res_b[:, :], b, ALPHA, None, ALU.mult))
            dve.engine_nop().then_inc(cols_mod, 1)

        def modulate(n):
            t0 = norm_t0(n)

            def normed(k):
                dve.tensor_tensor(h[:, k, t0:TOK], h[:, k, t0:TOK], scr[3][:, t0:TOK], ALU.mult).then_inc(ln_xn, 1)
            if n:
                normed(0)
            for k in range(KD):
                if n and k + 1 < KD:
                    normed(k + 1)
                if n == 6:
                    continue
                if n:
                    dve.wait_ge(ln_xn, KD * (n - 1) + k + 1)
                for s, seg in halves(t0):
                    m = dve.tensor_scalar(scr[4 + k % 2][:, seg], h[:, k, seg], mod_a[:, k, s:s + 1],
                                          mod_b[:, k, s:s + 1], ALU.mult, ALU.add)
                link(m)
                dve.wait_ge(u_hi_done, KD * n + k + 1)
                dve.tensor_tensor(u_lo[:, k, t0:TOK], scr[4 + k % 2][:, t0:TOK], u_hi[:, k, t0:TOK].bitcast(F32),
                                  ALU.subtract).then_inc(u_ready, 1)

        def norm(n):
            t0 = norm_t0(n)
            k0 = KD * (n - 1)
            dve.wait_ge(ln_mean, n)
            for k in range(KD):
                dve.tensor_tensor(h[:, k, t0:TOK], h[:, k, t0:TOK], ps[6][:, t0:TOK], ALU.subtract
                                  ).then_inc(ln_cent, 1)
            dve.wait_ge(ln_std, n)
            link(dve.reciprocal(scr[3][:, t0:TOK], scr[2][:, t0:TOK]))
            modulate(n)

        def gate_columns(layer, i, factor):
            m0 = gate_mods(layer, i)
            dve.wait_ge(h_ready, KD * (3 * layer + i + 1))
            dve.tensor_scalar(gate[:, :, :], mods[:, m0:m0 + KD, :], factor, None, ALU.mult)
            link(dve.memset(scr[5][:, :], 0.0))
            columns(3 * layer + i + 1)

        def add_branch(tile, bank, t0, evac, total):
            for s, seg in halves(t0):
                m = dve.scalar_tensor_tensor(h[:, tile, seg], ps[bank][:, seg], gate[:, tile, s:s + 1],
                                             h[:, tile, seg], ALU.mult, ALU.add)
            m.then_inc(evac_dve, 1)
            if isinstance(tile, int) and tile == KD - 1:
                return
            dve.wait_ge(evac_dve, evac)
            wait(dve, sum_done, total)
            dve.tensor_tensor(scr[5][:, t0:TOK], scr[5][:, t0:TOK], h[:, tile, t0:TOK], ALU.add).then_inc(sum_done, 1)

        def gate_weights(layer):
            dve.memset(wg_hi[:, :, :].bitcast(F32), 0.0)
            link(dve.memset(wg_lo[:, :, :].bitcast(F32), 0.0))
            dve.wait_ge(wg_landed, 16 * (layer + 1))
            hi, lo = (w[:, :, :].rearrange("p k (q n) -> p k q n", q=4)[:, :, :, 0:4] for w in (wg_hi, wg_lo))
            whole = wg_in[:, :, :].rearrange("p k (q n) -> p k q n", q=4)
            link(dve.tensor_copy(hi, whole))
            dve.tensor_tensor(lo, whole, hi.bitcast(F32), ALU.subtract).then_inc(wg_ready, 1)

        def up(layer, f):
            base, a0, d0 = BASES[layer, f"up{f}"]
            g0 = KF * (2 * layer + f)
            t0 = t0_of(layer) if f else 0
            first, other = up_patterns(layer, f)
            block = ADA_OF.get((layer, f"up{f}"))

            def body_of(pattern, base):
                def body(i):
                    for c, (kind, q) in enumerate(pattern):
                        if (kind, q) == ("a", 3):
                            dve.wait_ge(chunk_used, base + c + 1 + len(pattern) * i)
                            ada_copy(block - 1 + i, 4, 4)
                        ahead(base, c, i, len(pattern))
                        if kind == "w" and q % 2:
                            e = q // 2
                            dve.wait_ge(chunk_used, base + c + 1 + len(pattern) * i)
                            dve.wait_ge(evac_act, a0 + e + 1 + 2 * i)
                            dve.tensor_tensor(scr[2 + e][:, t0:TOK], scr[e][:, t0:TOK], ps[q][:, t0:TOK], ALU.mult
                                              ).then_inc(evac_dve, 1)
                            dve.wait_ge(g_hi_done, g0 + e + 1 + 2 * i)
                            dve.tensor_tensor(g_lo[:, 2 * i + e, t0:TOK], scr[2 + e][:, t0:TOK],
                                              g_hi[:, 2 * i + e, t0:TOK].bitcast(F32), ALU.subtract
                                              ).then_inc(g_ready, 1)
                    if pattern is UP_ADA:
                        ada_add(block - 1 + i, 5, block // ADA_BLOCKS)
                return body
            body_of(first, base)(0)
            run_from_1(dve, CH_UP // 4, body_of(other, round_base(base, first, other)))

        def down(layer, f):
            base, _, d0 = BASES[layer, f"down{f}"]
            t0 = t0_of(layer) if f else 0
            s0 = (KD - 1) * (3 * layer + 2 * f)
            gate_columns(layer, 2 * f, 0.5)

            first, other = down_patterns(layer, f)
            block = ADA_OF.get((layer, f"down{f}"))


            def body_of(pattern, base, start=False):
                def body(i):
                    for c, (kind, q) in enumerate(pattern):
                        if (kind, q) == ("a", 3):
                            dve.wait_ge(chunk_used, base + c + 1 + len(pattern) * i)
                            ada_copy(block + i, 4, 4)
                        if kind == "w" and q % 4 == 3:
                            e = q // 4
                            dve.wait_ge(chunk_used, base + c + 1 + len(pattern) * i)
                            add_branch(2 * i + e, e, t0, d0 + e + 1 + 2 * i, s0 + e + 2 * i)
                        ahead(base, c, i, len(pattern))
                    if pattern is DOWN_ADA:
                        ada_add(block + i, 5, block // ADA_BLOCKS)
                return body
            body_of(first, base)(0)
            if f == 0:
                gate_weights(layer)
            run_from_1(dve, KD // 2, body_of(other, round_base(base, first, other)), peel_last=True)

        def split_y(y, src, hi, lo, k, t0):
            dve.wait_ge(y_hi_done, y + 1)
            dve.tensor_tensor(lo[:, k, t0:TOK], src[:, t0:TOK], hi[:, k, t0:TOK].bitcast(F32),
                              ALU.subtract).then_inc(y_ready, 1)

        def proj(layer, step):
            kind, i = step
            base, a0, d0 = BASES[layer, "proj"]
            r, n, a, d = PLANS[layer][step]
            t0 = t0_of(layer, kind in X_ONLY)
            bank = ps[n % 4]
            ahead(base, r)
            y = y_number(layer, kind, i)
            ct, cc = bias_at(layer, SEC[kind] + i)
            bias = cols[:, ct, cc:cc + 1]
            if kind == "mk":
                dve.wait_ge(chunk_used, base + r + 1)
                dve.tensor_scalar(kt[:, i, :], bank[:, :], bias, DQK ** -0.5, ALU.add, ALU.mult).then_inc(evac_dve, 1)
            elif kind == "sx":
                dve.wait_ge(chunk_used, base + r + 1)
                dve.wait_ge(evac_act, a0 + PLANS[layer]["cg", i][2] + 1)
                if i == 0:
                    link(dve.memset(zpad[:, :, :], 0.0))
                for s, seg in halves(t0):
                    m = dve.scalar_tensor_tensor(zpad[:, s, 1:SEG + 1], bank[:, seg], bias, cgt[:, seg],
                                                 ALU.add, ALU.mult)
                m.then_inc(evac_dve, 1)
                dve.wait_ge(evac_dve, d0 + d + 1)
                tap = [cols[:, 3, 36 + 12 * layer + 4 * j + i:37 + 12 * layer + 4 * j + i] for j in range(3)]
                s0 = t0 // SEG
                z, o = zpad[:, s0:2, :], cv[:, t0:TOK].rearrange("p (s t) -> p s t", t=SEG)
                link(dve.tensor_scalar(o, z[:, :, 0:SEG], tap[0], None, ALU.mult))
                link(dve.scalar_tensor_tensor(o, z[:, :, 1:SEG + 1], tap[1], o, ALU.mult, ALU.add))
                link(dve.scalar_tensor_tensor(o, z[:, :, 2:SEG + 2], tap[2], o, ALU.mult, ALU.add))
            elif kind == "sb":
                dve.wait_ge(chunk_used, base + r + 1)
                dve.scalar_tensor_tensor(scr[2 + y % 2][:, t0:TOK], bank[:, t0:TOK], bias, cv[:, t0:TOK],
                                         ALU.add, ALU.mult).then_inc(evac_dve, 1)
                dve.wait_ge(evac_dve, d0 + d + 1)
                dve.engine_nop().then_inc(yf_ready, 1)
                split_y(y, scr[2 + y % 2], ysc_hi, ysc_lo, i, t0)
            elif kind == "mo":
                dve.wait_ge(evac_act, a0 + a + 1)
                dve.wait_ge(ht_ready, HEADS * layer + i // 2 + 1)
                dve.tensor_tensor(ht[:, i, t0:TOK], scr[i % 2][:, t0:TOK], ht[:, i, t0:TOK], ALU.mult
                                  ).then_inc(yf_ready, 1)

        def turn_v(layer, v):
            g = 12 * layer + v
            dve.wait_ge(v_turned, g + 1)
            src = ps[value_bank(v)][:, :].rearrange("p (t n) -> p t n", t=TT)
            if v < 8:
                dst = vaug[:, :, v // 2, (v % 2) * P:(v % 2 + 1) * P]
            else:
                dst = dav[:, :, v - 8, :]
            dve.tensor_copy(dst, src).then_inc(v_placed, 1)

        def rope(layer, i):
            xs = dqk[:, i, SEG:TOK]
            g = 8 * layer + ROPES.index(i)
            dve.wait_ge(rot_done, g + 1)
            wait(dve, rope_done, g)
            if i == ROPES[0]:
                dve.wait_ge(y_ready, y_number(layer, "sb", 3) + 1)
                dve.memset(q_first[DA_HALF:P, :, :], 0.0)
            dve.tensor_tensor(scr[2][:, 0:SEG], ps[6 + g % 2][:, 0:SEG], rope_sin, ALU.mult)
            link(dve.tensor_tensor(xs, xs, rope_cos, ALU.mult))
            if i >= HEADS:
                dve.tensor_tensor(xs, xs, scr[2][:, 0:SEG], ALU.add).then_inc(rope_done, 1)
                return
            a, b = slice(0, DA_HALF), slice(DA_HALF, P)
            if t0_of(layer) == 0:
                dve.tensor_copy(q_first[a, i, 0:SEG], dqk[a, i, 0:SEG])
            link(dve.tensor_tensor(q_first[a, i, SEG:TOK], xs[a, :], scr[2][a, 0:SEG], ALU.add))
            dve.memset(dqk[a, i, t0_of(layer):TOK], 0.0)
            dve.tensor_tensor(xs[b, :], xs[b, :], scr[2][b, 0:SEG], ALU.add).then_inc(rope_done, 1)

        def flip(dst, src):
            dve.tensor_copy(dst[:, 0:SEG], rev(src, 0))
            return dve.tensor_copy(dst[:, SEG:TOK], rev(src, 1))

        def rev(src, s):
            return src[:, s * SEG:(s + 1) * SEG][:, ::-1]

        def gates(layer, part):
            raw_g, lf, ln1, ia, la = gt[1], gt[2], gt[3], gt[4], gt[5]
            ones, fsum, gmax, top = gt[6], gt[7], gt[2], gt[0]
            if part == 0:
                dve.memset(vaug[:, :, :, 256:257], 1.0)
                dve.memset(neg_g[64:128, :], 0.0)
                dve.wait_ge(gate_act, 5 * layer + 1)
                link(dve.tensor_scalar(ln1[64:128, :], raw_g[64:128, :], -1.0, None, ALU.mult))
                dve.tensor_tensor(ln1[64:128, :], raw_g[64:128, :], ln1[64:128, :], ALU.max).then_inc(gate_abs, 1)
                link(dve.tensor_scalar(lf[64:128, :], raw_g[64:128, :], 0.0, None, ALU.min))
            elif part == 1:
                dve.wait_ge(gate_act, 5 * layer + 2)
                link(dve.tensor_tensor(lf[64:128, :], lf[64:128, :], ln1[64:128, :], ALU.subtract))
                dve.tensor_copy(ia[0:32, :], raw_g[0:32, :])
                flip(ia[32:64, :], raw_g[32:64, :])
                dve.tensor_copy(la[0:32, :], lf[64:96, :])
                link(flip(la[32:64, :], lf[96:128, :]))
            elif part == 2:
                link(dve.memset(ones[0:64, :], 1.0))
                link(dve.tensor_tensor_scan(fsum[0:64, :], ones[0:64, :], la[0:64, :], 0.0, ALU.mult, ALU.add))
                link(dve.tensor_tensor(ia[0:64, :], ia[0:64, :], fsum[0:64, :], ALU.subtract))
                link(dve.tensor_tensor_scan(gmax[0:64, :], ones[0:64, :], ia[0:64, :], -3.0e38, ALU.mult, ALU.max))
            else:
                link(dve.tensor_tensor(fsum[0:64, :], fsum[0:64, :], gmax[0:64, :], ALU.add))
                link(dve.tensor_scalar(gmax[0:64, :], gmax[0:64, :], -1.0, None, ALU.mult))
                dve.tensor_copy(top[0:32, :], ia[0:32, :])
                flip(top[32:64, :], ia[32:64, :])
                dve.tensor_copy(top[64:96, :], fsum[0:32, :])
                flip(top[96:128, :], fsum[32:64, :])
                dve.tensor_copy(neg_g[0:32, :], gmax[0:32, :])
                flip(neg_g[32:64, :], gmax[32:64, :]).then_inc(gate_dve, 1)

        def ml_scores(layer, head, s):
            t0 = t0_of(layer)
            u = HEADS * layer + head
            for n in range(2):
                found, diag = segments(s, n, t0)
                dve.wait_ge(e_ready, 8 * u + 2 * s + n + 1)
                dve.wait_ge(s_ready, 4 * u + s + 1)
                for b, e in found:
                    m = dve.tensor_tensor(pw[:, n, s, b:e], xt[:, n, b:e], ps[6 + s % 2][:, b:e], ALU.mult)
                if diag is not None:
                    link(m)
                    own = pw[:, n, s, s * P:(s + 1) * P]
                    m = dve.tensor_tensor(own, own, (mask_f, mask_b)[n], ALU.mult)
                m.then_inc(pw_ready, 1)

        def ml_numerator(layer, head, t):
            first = t0_of(layer) // P
            if t < first:
                return
            if head == 0 and t == first:
                dve.wait_ge(gate_act, 5 * layer + 5)
            nt = nth_out(layer, head, t)
            dve.wait_ge(num_ready, nt + 1)
            for n in range(2):
                m = dve.tensor_scalar(small[:, 12 + n:13 + n], ps[6 + n][:, 256:257], -1.0, None, ALU.mult)
            link(m)
            for n in range(2):
                row = 32 * n + head
                m = dve.scalar_tensor_tensor(small[:, 6 + n:7 + n], small[:, 12 + n:13 + n],
                                             em[:, t, row:row + 1], ps[6 + n][:, 256:257], ALU.max, ALU.max)
            link(m)
            link(dve.reciprocal(small[:, 8:10], small[:, 6:8]))
            if nt >= 2:
                dve.wait_ge(h_turned, nt - 1)
            link(dve.tensor_scalar(hf[:, :], ps[6][:, 0:256], small[:, 8:9], None, ALU.mult))
            dve.scalar_tensor_tensor(hs[:, t % 2, :], ps[7][:, 0:256], small[:, 9:10], hf[:, :],
                                     ALU.mult, ALU.add).then_inc(hsum_ready, 1)

        def attend(layer):
            scale = DA_HALF ** -0.5
            units, u0 = attention_units(layer)
            tiles = range(t0_of(layer) // P, TT)

            def maxima(v):
                nk = len(units[v][2]) * P
                for j in range(2):
                    dve.wait_ge(sc_ready, 2 * (u0 + v) + j + 1)
                    link(dve.tensor_reduce(att[:, v % 2, 4 + j:5 + j], ps[SCORE_BANK[v % 2] + j][:, 0:nk], AXX, ALU.max))
                    dve.tensor_scalar(att[:, v % 2, j:j + 1], att[:, v % 2, 4 + j:5 + j], -scale, None, ALU.mult
                                      ).then_inc(smax_ready, 1)

            def weights(v):
                nk = len(units[v][2]) * P
                p0, p1 = scr[2 * (v % 2)], scr[2 * (v % 2) + 1]
                a = att[:, v % 2, :]
                dve.wait_ge(p_ready, 2 * (u0 + v) + 2)
                if v >= 2:
                    dve.wait_ge(o_copied, u0 + v - 1)
                link(dve.reciprocal(a[:, 6:8], a[:, 2:4]))
                link(dve.scalar_tensor_tensor(a[:, 8:9], a[:, 2:3], neg_lam[:, layer:layer + 1], a[:, 7:8],
                                              ALU.mult, ALU.mult))
                if v >= 2:
                    dve.wait_ge(wgt_turned, u0 + v - 1)
                dve.scalar_tensor_tensor(wgt[v % 2][:, 0:nk], p1[:, 0:nk], a[:, 8:9], p0[:, 0:nk],
                                         ALU.mult, ALU.add).then_inc(wgt_ready, 1)

            def outputs(v):
                head, t, _ = units[v]
                dve.wait_ge(o_ready, u0 + v + 1)
                dve.tensor_scalar(oda[:, t, head, :], ps[7 - 4 * (v % 2)][:, 0:P], att[:, v % 2, 6:7], None, ALU.mult
                                  ).then_inc(o_copied, 1)
            maxima(0)
            for v in range(len(units)):
                weights(v)
                if v + 1 < len(units):
                    maxima(v + 1)
                if v:
                    outputs(v - 1)
            outputs(len(units) - 1)
            dve.wait_ge(o_std, layer + 1)
            link(dve.reciprocal(ssq[:, tiles[0]:TT, :], ssq[:, tiles[0]:TT, :]))
            for head in range(HEADS):
                own = oda[:, tiles[0]:TT, head, :]
                dve.tensor_tensor(own, own, ssq[:, tiles[0]:TT, head:head + 1].to_broadcast([P, len(tiles), P]), ALU.mult
                                  ).then_inc(o_scaled, 1)
            t0 = tiles[0] * P
            for head in range(HEADS):
                dve.wait_ge(o_turned, 4 * layer + head + 1)
                if head >= 2:
                    dve.wait_ge(yda_h, 4 * layer + head - 1)
                lam_init = 0.8 - 0.6 * math.exp(-0.3 * layer)
                f = scr[2 + head % 2][:, t0:TOK]
                dve.tensor_scalar(f, ps[6 + head % 2][:, t0:TOK], cols[:, 3, 76 + layer:77 + layer], 1.0 - lam_init,
                                  ALU.mult, ALU.mult).then_inc(yda_f, 1)
                dve.wait_ge(yda_h, 4 * layer + head + 1)
                dve.tensor_tensor(yda_lo[:, head, t0:TOK], f, yda_hi[:, head, t0:TOK].bitcast(F32), ALU.subtract
                                  ).then_inc(yda_ready, 1)

        def mixer(layer):
            t0 = t0_of(layer)
            for step in vector_order(ORDERS[layer]):
                if step[0] in EVAC_ENGINE:
                    proj(layer, step)
                elif step[0] == "ada":
                    r = BASES[layer, "proj"][0] + PLANS[layer][step][0]
                    ahead(r, 0)
                    if step[2] == 3:
                        dve.wait_ge(chunk_used, r + 1)
                        ada_copy(ADA_OF[layer, "proj"] + step[1], 4, 4)
                elif step[0] == "ysplit":
                    split_y(y_number(layer, "mo", step[1]), ht[:, step[1], :], yml_hi, yml_lo, step[1], t0)
                elif step[0] == "adat":
                    ada_add(ADA_OF[layer, "proj"] + step[1], 5, ADA_OF[layer, "proj"] // ADA_BLOCKS)
                elif step[0] == "gates":
                    gates(layer, step[1])
                elif step[0] == "attend":
                    attend(layer)
                elif step[0] in ("ml_s", "ml_n"):
                    (ml_scores if step[0] == "ml_s" else ml_numerator)(layer, *step[1:])
                elif step[0] in ("turn_v", "rope"):
                    {"turn_v": turn_v, "rope": rope}[step[0]](layer, step[1])
            base, a0, d0 = BASES[layer, "gate"]
            pattern = gate_pattern(layer)
            block = ADA_OF.get((layer, "gate"))

            def body(i):
                for c, (kind, q) in enumerate(pattern):
                    if (kind, q) == ("a", 3):
                        dve.wait_ge(chunk_used, base + c + 1 + len(pattern) * i)
                        ada_copy(block + i, 4, 4)
                    ahead(base, c, i, len(pattern))
                    if kind == "a":
                        continue
                    if q % 2 == 0:
                        continue
                    e = q // 6
                    dve.wait_ge(chunk_used, base + c + 1 + len(pattern) * i)
                    dve.wait_ge(evac_act, a0 + q // 2 + 1 + 6 * i)
                    z = scr[2 + e][:, t0:TOK]
                    dst = z if q % 6 == 1 else scr[4][:, t0:TOK]
                    dve.tensor_tensor(dst, scr[(q // 2) % 2][:, t0:TOK], ps[q % 4][:, t0:TOK], ALU.mult
                                      ).then_inc(evac_dve, 1)
                    dve.wait_ge(evac_dve, d0 + q // 2 + 1 + 6 * i)
                    if q % 6 == 3:
                        dve.tensor_tensor(z, z, dst, ALU.add).then_inc(z_part, 1)
                        dve.wait_ge(z_part, KD * layer + e + 1 + 2 * i)
                    if q % 6 == 5:
                        dve.tensor_tensor(z, z, dst, ALU.add).then_inc(z_sum, 1)
                        dve.wait_ge(z_hi_done, KD * layer + e + 1 + 2 * i)
                        dve.tensor_tensor(z_lo[:, 2 * i + e, t0:TOK], z, z_hi[:, 2 * i + e, t0:TOK].bitcast(F32),
                                          ALU.subtract).then_inc(z_ready, 1)
                if block is not None:
                    ada_add(block + i, 5, block // ADA_BLOCKS)
            run(dve, KD // 2, body)
            gate_columns(layer, 1, 1.0)
            base, _, d0 = BASES[layer, "wo"]
            s0 = (KD - 1) * (3 * layer + 1)

            def body_o(i):
                for e in range(4):
                    dve.wait_ge(chunk_used, base + e + 1 + 4 * i)
                    add_branch(4 * i + e, e, t0, d0 + e + 1 + 4 * i, s0 + e + 4 * i)
                    ahead(base, e, i, 4)
            run(dve, KD // 4, body_o, peel_last=True)

        dve.wait_ge(evac_act, 4)
        dve.wait_ge(evac_dve, 4)
        dve.wait_ge(ada_ev, 4)
        columns(0)
        modulate(0)
        lambdas()
        for layer in range(DEPTH):
            up(layer, 0)
            down(layer, 0)
            norm(3 * layer + 1)
            mixer(layer)
            norm(3 * layer + 2)
            up(layer, 1)
            down(layer, 1)
            norm(3 * layer + 3)

    block.__exit__(None, None, None)


def constants():
    out = np.zeros((P, 1154), np.float32)
    row, col = np.arange(P)[:, None], np.arange(P)[None, :]
    out[:, 0:128] = row == col
    out[:, 128:256] = col >= row
    out[:, 256:384] = col <= row
    first = (col % 64) < 32
    out[:, 384:512] = np.where(first & (row == col + 32), -1.0, 0.0) + np.where(~first & (row == col - 32), 1.0, 0.0)
    out[:, 512:640] = 1.0 / D
    n_freq = DA_HALF // 4
    inv = np.float32(10000.0) ** (-np.arange(n_freq, dtype=np.float32) / np.float32(n_freq))
    t = np.arange(SEG)
    ang = np.concatenate([(t // GRID_W).astype(np.float32)[None, :] * inv[:, None],
                          (t % GRID_W).astype(np.float32)[None, :] * inv[:, None]], 0)
    out[:, 640:896] = np.tile(np.cos(ang), (4, 1))
    out[:, 896:1152] = np.tile(np.sin(ang), (4, 1))
    out[0:4, 1152:1154] = np.tile(np.eye(2), (2, 1))
    return out


_INS = ["x", "c", "ctx", "c_ctx", "w_ada", "b_ada", "ln_g", "ln_b", "ffn1_up", "ffn1_down", "ffn2_up",
        "ffn2_down", "w_in", "b_in", "conv_w", "w_sc", "w_ml", "w_da", "w_o", "lam_q1", "lam_k1", "lam_q2",
        "lam_k2", "da_norm_g"]


def kernel(**inputs):
    import concourse.bacc as _bacc
    from concourse.bass_utils import run_bass_kernel_spmd as _run

    nc = _bacc.Bacc("TRN2", target_bir_lowering=False, num_devices=1)
    arrays, args = {}, []
    for name in _INS + ["consts"]:
        a = constants() if name == "consts" else np.ascontiguousarray(inputs[name])
        arrays[f"in_{name}"] = a
        args.append(nc.dram_tensor(f"in_{name}", a.shape, mybir.dt.from_np(a.dtype), kind="ExternalInput").ap())
    args.append(nc.dram_tensor("out_0", (1, SEG, D), F32, kind="ExternalOutput").ap())
    build(nc, *args)
    r = _run(nc, [arrays], core_ids=[0])
    return r.results[0]["out_0"]
```
